# Optimizing a Trainium2 kernel written in Bass

```python
import jax, jax.numpy as jnp
from jax import lax
import numpy as np

D_MODEL = 1024
BATCH = 1
SEQ = 512
DEPTH = 2
DEC_BATCH = 1
DEC_SEQ = 64
PAST_LEN = 256

CHUNK = 64
HEAD_DIM = 64
SWA_HEADS = 8
SWA_KV_HEADS = 2
SWA_GROUP = SWA_HEADS // SWA_KV_HEADS
WINDOW = 128
WINDOW_CHUNKS = WINDOW // CHUNK
SWA_Q = SWA_HEADS * HEAD_DIM
SWA_KV = SWA_KV_HEADS * HEAD_DIM
GMLP_GROUPS = 4
GMLP_BLOCK = 128
GMLP_WIDTH = GMLP_GROUPS * HEAD_DIM
RET_HEADS = 4
RET_WIDTH = RET_HEADS * HEAD_DIM
ROPE_BASE = 10000.0
IN_SPLITS = (SWA_Q, SWA_KV, SWA_KV, GMLP_WIDTH, GMLP_WIDTH, RET_WIDTH, RET_WIDTH, RET_WIDTH, RET_WIDTH)
IN_WIDTH = sum(IN_SPLITS)
MIX_WIDTH = SWA_Q + GMLP_WIDTH + RET_WIDTH
D_FF = ((8 * D_MODEL + 3 * 256 - 1) // (3 * 256)) * 256
EPS = 1e-6
NEG = -1e30

kernel_name = 'hybrid_swa_gmlp_retention_stream_step'

def rms_norm(x, g):
    xf = x.astype(jnp.float32)
    y = xf * lax.rsqrt(jnp.mean(xf * xf, axis=-1, keepdims=True) + EPS)
    return (y * g.astype(jnp.float32)).astype(x.dtype)

def layer_norm(x, g, b):
    xf = x.astype(jnp.float32)
    mu = jnp.mean(xf, axis=-1, keepdims=True)
    var = jnp.mean(jnp.square(xf - mu), axis=-1, keepdims=True)
    y = (xf - mu) * lax.rsqrt(var + EPS)
    return (y * g.astype(jnp.float32) + b.astype(jnp.float32)).astype(x.dtype)

def project(h, w_in):
    y = h @ w_in
    cuts = [int(c) for c in np.cumsum(IN_SPLITS)[:-1]]
    return jnp.split(y, cuts, axis=-1)

def sink_attention(q, k, v, sinks, mask):
    s = jnp.einsum('...lhgd,...mhd->...hglm', q, k).astype(jnp.float32) * (HEAD_DIM ** -0.5)
    if mask is not None:
        s = jnp.where(mask, s, NEG)
    sink = jnp.broadcast_to(sinks.astype(jnp.float32)[..., None, None], s.shape[:-1] + (1,))
    p = jax.nn.softmax(jnp.concatenate([s, sink], axis=-1), axis=-1)[..., :-1]
    return jnp.einsum('...hglm,...mhd->...lhgd', p.astype(v.dtype), v)

def swa_prompt(q, k, v, sinks):
    B, S = q.shape[:2]
    n = S // CHUNK
    qc = q.reshape(B, n, CHUNK, SWA_KV_HEADS, SWA_GROUP, HEAD_DIM)
    pad = ((0, 0), (WINDOW_CHUNKS * CHUNK, 0), (0, 0), (0, 0))
    kp = jnp.pad(k, pad).reshape(B, n + WINDOW_CHUNKS, CHUNK, SWA_KV_HEADS, HEAD_DIM)
    vp = jnp.pad(v, pad).reshape(B, n + WINDOW_CHUNKS, CHUNK, SWA_KV_HEADS, HEAD_DIM)
    kw = jnp.concatenate([kp[:, j:j + n] for j in range(WINDOW_CHUNKS + 1)], axis=2)
    vw = jnp.concatenate([vp[:, j:j + n] for j in range(WINDOW_CHUNKS + 1)], axis=2)
    key_pos = (jnp.arange(n)[:, None] * CHUNK + jnp.arange((WINDOW_CHUNKS + 1) * CHUNK)[None, :]
               - WINDOW_CHUNKS * CHUNK)
    mask = (key_pos >= 0)[:, None, None, None, :]
    o = sink_attention(qc, kw, vw, sinks, mask)
    return o.reshape(B, S, SWA_Q)

def swa_sample(q, k, v, cache_k, cache_v, sinks):
    B, T = q.shape[:2]
    qh = q.reshape(B, T, SWA_KV_HEADS, SWA_GROUP, HEAD_DIM)
    kk = jnp.concatenate([cache_k.astype(k.dtype), k], axis=1)
    vv = jnp.concatenate([cache_v.astype(v.dtype), v], axis=1)
    o = sink_attention(qh, kk, vv, sinks, None)
    return o.reshape(B, T, SWA_Q)

def gmlp_mix(u, v, w_s, b_s, ln_g, ln_b):
    B, S, _ = u.shape
    L = min(S, GMLP_BLOCK)
    n = S // L
    u = jax.nn.gelu(u)
    v = layer_norm(jax.nn.gelu(v), ln_g, ln_b)
    i = jnp.arange(L)
    mask = (i[:, None] // CHUNK) >= (i[None, :] // CHUNK)
    w = jnp.where(mask, w_s[:, :L, :L], 0.0)
    vb = v.reshape(B, n, L, GMLP_GROUPS, HEAD_DIM)
    mixed = jnp.einsum('gij,bnjgc->bnigc', w, vb) + b_s[:, :L].T[:, :, None]
    return u * mixed.reshape(B, S, GMLP_WIDTH).astype(u.dtype), v

def rotary(x, pos):
    half = HEAD_DIM // 2
    inv = ROPE_BASE ** (-jnp.arange(half, dtype=jnp.float32) / half)
    ang = pos.astype(jnp.float32)[:, None] * inv[None, :]
    cos = jnp.cos(ang)[None, :, None, :]
    sin = jnp.sin(ang)[None, :, None, :]
    x1 = x[..., :half].astype(jnp.float32)
    x2 = x[..., half:].astype(jnp.float32)
    return jnp.concatenate([x1 * cos - x2 * sin, x2 * cos + x1 * sin], axis=-1).astype(x.dtype)

def retention(q, k, v, state0, block):
    B, S, H, d = q.shape
    n = S // block
    logg = jnp.log(1.0 - 2.0 ** (-5.0 - jnp.arange(H, dtype=jnp.float32)))
    idx = jnp.arange(block, dtype=jnp.float32)
    rel = idx[:, None] - idx[None, :]
    decay_mat = jnp.where(rel >= 0, jnp.exp(logg[:, None, None] * jnp.maximum(rel, 0.0)), 0.0)
    xi = jnp.exp(logg[:, None] * (idx + 1.0))
    zeta = jnp.exp(logg[:, None] * (block - 1.0 - idx))
    chunk_decay = jnp.exp(logg * block)[None, :, None, None]
    qc = q.reshape(B, n, block, H, d).astype(jnp.float32)
    kc = k.reshape(B, n, block, H, d).astype(jnp.float32)
    vc = v.reshape(B, n, block, H, d).astype(jnp.float32)
    inner = jnp.einsum('bclhd,bcmhd->bchlm', qc, kc) * decay_mat
    inner = jnp.einsum('bchlm,bcmhe->bclhe', inner, vc)
    kv = jnp.einsum('bcmhd,bcmhe,hm->bchde', kc, vc, zeta)

    def step(state, kv_c):
        return chunk_decay * state + kv_c, state

    final, prev = lax.scan(step, state0.astype(jnp.float32), jnp.moveaxis(kv, 1, 0))
    prev = jnp.moveaxis(prev, 0, 1)
    cross = jnp.einsum('bclhd,bchde,hl->bclhe', qc, prev, xi)
    return (inner + cross).reshape(B, S, H, d), final.astype(state0.dtype)

def head_group_norm(o, g):
    B, S, H, d = o.shape
    mu = jnp.mean(o, axis=-1, keepdims=True)
    var = jnp.mean(jnp.square(o - mu), axis=-1, keepdims=True)
    y = ((o - mu) * lax.rsqrt(var + EPS)).reshape(B, S, H * d)
    return y * g.astype(jnp.float32)

def trunk_layer(x, pos, p, cache_k, cache_v, ret_state):
    B, S, _ = x.shape
    h = rms_norm(x, p['pre_mix'])
    q_a, k_a, v_a, u_b, v_b, q_c, k_c, v_c, g_c = project(h, p['w_in'])
    k_a = k_a.reshape(B, S, SWA_KV_HEADS, HEAD_DIM)
    v_a = v_a.reshape(B, S, SWA_KV_HEADS, HEAD_DIM)
    sinks = p['sinks'].reshape(SWA_KV_HEADS, SWA_GROUP)
    if cache_k is None:
        a = swa_prompt(q_a, k_a, v_a, sinks)
        swa_new = (k_a[:, S - WINDOW:], v_a[:, S - WINDOW:])
        state0 = jnp.zeros((B, RET_HEADS, HEAD_DIM, HEAD_DIM), x.dtype)
        block = CHUNK
    else:
        a = swa_sample(q_a, k_a, v_a, cache_k, cache_v, sinks)
        swa_new = (k_a, v_a)
        state0 = ret_state
        block = S
    b, v_rows = gmlp_mix(u_b, v_b, p['gmlp_w'], p['gmlp_b'], p['gmlp_ln_g'], p['gmlp_ln_b'])
    qr = rotary(q_c.reshape(B, S, RET_HEADS, HEAD_DIM), pos)
    kr = rotary(k_c.reshape(B, S, RET_HEADS, HEAD_DIM), pos) * (HEAD_DIM ** -0.5)
    r, ret_final = retention(qr, kr, v_c.reshape(B, S, RET_HEADS, HEAD_DIM), state0, block)
    c = (head_group_norm(r, p['ret_g']) * jax.nn.silu(g_c.astype(jnp.float32))).astype(x.dtype)
    merged = jnp.concatenate([rms_norm(a, p['norm_a']), rms_norm(b, p['norm_b']), c], axis=-1) @ p['w_out']
    x = x + rms_norm(merged, p['post_mix'])
    h = rms_norm(x, p['pre_ffn'])
    f = (jax.nn.silu(h @ p['w_gate']) * (h @ p['w_up'])) @ p['w_down']
    x = x + rms_norm(f, p['post_ffn'])
    return x, swa_new, ret_final, v_rows

def setup_inputs(seed: int = 0) -> dict:
    key = jax.random.key(seed)
    ks = jax.random.split(key, 24)

    def nrm(k, shape, scale):
        return scale * jax.random.normal(k, shape, jnp.float32)

    swa_cache = min(WINDOW, PAST_LEN)
    return {
        'x_prompt': nrm(ks[0], (BATCH, SEQ, D_MODEL), 1.0),
        'x_sample': nrm(ks[1], (DEC_BATCH, DEC_SEQ, D_MODEL), 1.0),
        'cache_swa_k': nrm(ks[2], (DEC_BATCH, DEPTH, swa_cache, SWA_KV_HEADS, HEAD_DIM), 1.0),
        'cache_swa_v': nrm(ks[3], (DEC_BATCH, DEPTH, swa_cache, SWA_KV_HEADS, HEAD_DIM), 1.0),
        'state_ret': nrm(ks[4], (DEC_BATCH, DEPTH, RET_HEADS, HEAD_DIM, HEAD_DIM), 1.0),
        'w_in': nrm(ks[5], (DEPTH, D_MODEL, IN_WIDTH), D_MODEL ** -0.5),
        'w_out': nrm(ks[6], (DEPTH, MIX_WIDTH, D_MODEL), MIX_WIDTH ** -0.5),
        'swa_sinks': nrm(ks[7], (DEPTH, SWA_HEADS), 0.5),
        'gmlp_w': nrm(ks[8], (DEPTH, GMLP_GROUPS, GMLP_BLOCK, GMLP_BLOCK), GMLP_BLOCK ** -0.5),
        'gmlp_b': 1.0 + nrm(ks[9], (DEPTH, GMLP_GROUPS, GMLP_BLOCK), 0.1),
        'gmlp_ln_g': 1.0 + nrm(ks[10], (DEPTH, GMLP_WIDTH), 0.1),
        'gmlp_ln_b': nrm(ks[11], (DEPTH, GMLP_WIDTH), 0.02),
        'norm_a_g': 1.0 + nrm(ks[12], (DEPTH, SWA_Q), 0.1),
        'norm_b_g': 1.0 + nrm(ks[13], (DEPTH, GMLP_WIDTH), 0.1),
        'ret_norm_g': 1.0 + nrm(ks[14], (DEPTH, RET_WIDTH), 0.1),
        'ln_pre_mix': 1.0 + nrm(ks[15], (DEPTH, D_MODEL), 0.1),
        'ln_post_mix': 1.0 + nrm(ks[16], (DEPTH, D_MODEL), 0.1),
        'ln_pre_ffn': 1.0 + nrm(ks[17], (DEPTH, D_MODEL), 0.1),
        'ln_post_ffn': 1.0 + nrm(ks[18], (DEPTH, D_MODEL), 0.1),
        'w_gate': nrm(ks[19], (DEPTH, D_MODEL, D_FF), D_MODEL ** -0.5),
        'w_up': nrm(ks[20], (DEPTH, D_MODEL, D_FF), D_MODEL ** -0.5),
        'w_down': nrm(ks[21], (DEPTH, D_FF, D_MODEL), D_FF ** -0.5),
    }

def reference(x_prompt, x_sample, cache_swa_k, cache_swa_v, state_ret, w_in, w_out, swa_sinks,
              gmlp_w, gmlp_b, gmlp_ln_g, gmlp_ln_b, norm_a_g, norm_b_g, ret_norm_g,
              ln_pre_mix, ln_post_mix, ln_pre_ffn, ln_post_ffn, w_gate, w_up, w_down):
    pos_p = jnp.arange(x_prompt.shape[1], dtype=jnp.int32)
    pos_s = PAST_LEN + jnp.arange(x_sample.shape[1], dtype=jnp.int32)
    xp, xs = x_prompt, x_sample
    kp_l, vp_l, ks_l, vs_l, rp_l, rs_l, gv_l = [], [], [], [], [], [], []
    for l in range(DEPTH):
        p = {
            'w_in': w_in[l], 'w_out': w_out[l], 'sinks': swa_sinks[l],
            'gmlp_w': gmlp_w[l], 'gmlp_b': gmlp_b[l], 'gmlp_ln_g': gmlp_ln_g[l], 'gmlp_ln_b': gmlp_ln_b[l],
            'norm_a': norm_a_g[l], 'norm_b': norm_b_g[l], 'ret_g': ret_norm_g[l],
            'pre_mix': ln_pre_mix[l], 'post_mix': ln_post_mix[l],
            'pre_ffn': ln_pre_ffn[l], 'post_ffn': ln_post_ffn[l],
            'w_gate': w_gate[l], 'w_up': w_up[l], 'w_down': w_down[l],
        }
        xp, (kp, vp), rp, _ = trunk_layer(xp, pos_p, p, None, None, None)
        xs, (ks, vs), rs, gv = trunk_layer(xs, pos_s, p, cache_swa_k[:, l], cache_swa_v[:, l], state_ret[:, l])
        kp_l.append(kp); vp_l.append(vp); ks_l.append(ks); vs_l.append(vs)
        rp_l.append(rp); rs_l.append(rs); gv_l.append(gv)
    return (xp, xs, jnp.stack(kp_l, axis=1), jnp.stack(vp_l, axis=1), jnp.stack(ks_l, axis=1),
            jnp.stack(vs_l, axis=1), jnp.stack(rp_l, axis=1), jnp.stack(rs_l, axis=1), jnp.stack(gv_l, axis=1))


_drawn_inputs = setup_inputs


def setup_inputs(seed=0):
    import zlib

    import numpy as np

    out = dict(_drawn_inputs(seed))
    spreads = {}
    factors = {'swa_sinks': 8.0, 'gmlp_ln_b': 2.699}
    for name, (base, spread) in spreads.items():
        noise = np.random.default_rng([zlib.crc32(name.encode()), seed]).standard_normal(out[name].shape)
        drawn = base * np.exp(spread * noise) if base else spread * noise
        out[name] = __import__('jax').numpy.asarray(drawn.astype(out[name].dtype))
    for name, factor in factors.items():
        out[name] = (out[name] * factor).astype(out[name].dtype)
    return out
```

```python
from contextlib import ExitStack

import numpy as np
import concourse.bass as bass
from concourse import mybir
from concourse.alu_op_type import AluOpType as ALU

F32 = mybir.dt.float32
F32R = mybir.dt.float32r
BF16 = mybir.dt.bfloat16
ACT = mybir.ActivationFunctionType
AX = mybir.AxisListType
ds = bass.ds

P = 128
DEPTH = 2
D = 1024
SEQ = 512
DEC = 64
PAST = 256
T = SEQ + DEC
HD = 64
KT = D // P
D_FF = ((8 * D + 3 * 256 - 1) // (3 * 256)) * 256
FT = D_FF // P
EPS = 1e-6
SCALE = HD ** -0.5
SWA_HEADS, KV_HEADS = 8, 2
RET_HEADS = 4
CHUNK = 64

GROUPS = ((0, 256), (256, T))
GW = max(b - a for a, b in GROUPS)
TB = [(0, 128), (128, 128), (256, 128), (384, 128), (512, 64)]
NB = len(TB)
GROUP_BLOCKS = ((0, 1), (2, 3, 4))

IN_QA, IN_QB, IN_KA, IN_KB, IN_V0, IN_V1, IN_G0, IN_G1, IN_VB0, IN_VB1, IN_UB0, IN_UB1, IN_K, IN_V, IN_Q0 = range(15)
IN_T = 18
OUT_T = KT
S_IN, S_OUT, S_GU, S_DN = 0, IN_T, IN_T + OUT_T, IN_T + OUT_T + 2 * FT
SLOTS = S_DN + KT * FT // 8
RING, RAW = 4, 2
assert SLOTS % RING == 0 and SLOTS % RAW == 0 and (KT * FT) % 8 == 0

TILES = IN_T + OUT_T + 2 * FT + KT
A_IN, A_OUT, A_GATE, A_DN = 0, IN_T, IN_T + OUT_T, IN_T + OUT_T + FT
A_TILES = A_DN + KT

SQ = dict(pre_mix=0, post_mix=16, pre_ffn=32, post_ffn=48)
SQS = 64
ST = dict(pre_mix=0, merged=2, post_mix=6, pre_ffn=8, post_ffn=10)
STS = 12
HR = dict(pre_mix=0, merged=16, pre_ffn=32)
HRS = 48

SP = dict(pre_mix=0, post_mix=8, pre_ffn=16, post_ffn=24, na=32, nb=36, rg=38, sink=40)
SP_N = 48
TAB = {}
_n = 0
for _name, _w in (("cos", T), ("sin", T), ("cosk", T), ("sink", T), ("xi", P), ("decay", 4 * P),
                  ("zeta", 2 * P), ("zetas", 2 * P), ("blk", P), ("cdec", 2), ("head", RET_HEADS)):
    TAB[_name] = _n
    _n += _w
TAB_N = _n
LP = {}
_n = 0
for _name, _w in (("lng", 256), ("lnb", 256), ("gb", 256), ("gw", 512)):
    LP[_name] = _n
    _n += _w
LP_N = _n

KC = SEQ + 128 + DEC
WINDOW = [(0, 128), (0, 256), (128, 256), (256, 256), (512, 192)]
VTILES = [(0,), (0, 1), (1, 2), (2, 3), (4, 5)]
NOUT = 13
DN_FREE = sum((8 * i + 7) % FT != FT - 1 for i in range(SLOTS - S_DN))
DVE_LINKS = 128
POOL_LINKS = 14
UNITS = NB * 4


def program(nc, xT, wts, small, tabs, lpar, kcache, vcache, ret0, ident_d, mask_d,
            o_x, o_k, o_v, o_rp, o_rs, o_gv):
    with ExitStack() as ctx:
        sem = lambda name: ctx.enter_context(nc.semaphore(name))

        base = (nc.sbuf_base + 63) // 64 * 64
        at = [base]

        def place(name, shape, dt=F32, offset=None):
            size = int(np.prod(shape[1:])) * (2 if dt == BF16 else 4)
            size = (size + 31) // 32 * 32
            o = at[0] if offset is None else offset
            t = nc.alloc_sbuf_tensor_at(name, shape, dt, offset=o)
            if offset is None:
                at[0] += size
            assert o + size <= nc.sbuf_usable_end, (name, o + size, nc.sbuf_usable_end)
            return t

        x = place("x", [P, KT, T])
        h_at = at[0]
        h_hi = place("h_hi", [P, KT, T], F32R)
        h_lo = place("h_lo", [P, KT, T], F32R)
        raw = place("raw", [P, RAW, 1024])
        w_hi = place("w_hi", [P, RING, 1024], F32R)
        w_lo = place("w_lo", [P, RING, 1024], F32R)
        sp = place("sp", [P, SP_N])
        ident = place("ident", [P, P])
        ones = place("ones", [P, P])
        mask = place("mask", [P, P + 256], BF16)
        epsc = place("epsc", [P, 1])
        acc = place("acc", [P, T])
        rstd = place("rstd", [P, T])
        sq = place("sq", [P, 2, GW])
        tp = place("tp", [P, 2, GW])
        st_p = place("st_p", [P, 2, 256])
        bst = place("bst", [P, NB, 6])
        bmv = place("bmv", [P, NB, 2])
        brs = place("brs", [P, NB])
        nsink = place("nsink", [P, 8])
        mx = place("mx", [P, 2, 2])
        nm = place("nm", [P, 2, 2])
        sm = place("sm", [P, 2, 2])
        es = place("es", [P, 2, 2])
        den = place("den", [P, 2, 2])
        rd = place("rd", [P, 2, 2])
        region = at[0]
        hid_hi = place("hid_hi", [P, FT, T], F32R)
        hid_lo = place("hid_lo", [P, FT, T], F32R)
        region_end = at[0]
        at[0] = region
        ret = place("ret", [P, 6, T])
        rtmp = place("rtmp", [P, 2, T])
        qxi = place("qxi", [P, 2, T])
        vtok = place("vtok", [P, NB, 256])
        kz = place("kz", [P, 2, 256])
        inner = place("inner", [P, 2, 4, P])
        zone2 = at[0]
        at[0] = region
        prob = place("prob", [P, 4, 2, 256])
        probT = place("probT", [P, 4, 2, 2, P])
        sqa = place("sqa", [P, 4, P])
        assert at[0] <= zone2
        y_mix = place("y_mix", [P, KT, T], offset=region)
        y_ffn = place("y_ffn", [P, KT, T], offset=h_at)
        at[0] = zone2
        sg = place("sg", [P, 2, T])
        gv = place("gv", [P, 2, T])
        ub = place("ub", [P, 2, T])
        rT = place("rT", [P, 2, T])
        rsq = place("rsq", [P, 2, T])
        gvt_at = at[0]
        gvt = place("gvt", [P, NB, 256])
        ptmp = place("ptmp", [P, 2, T], offset=gvt_at)
        kk = place("kk", [P, KC])
        vv = place("vv", [P, T])
        vk = place("vk", [P, 6, P])
        qm = place("qm", [P, 2, 2, RET_HEADS, P], offset=at[0])
        qq = place("qq", [P, 4, T])
        st_s = place("st_s", [P, 2, 256])
        tab_at = at[0]
        tab = place("tab", [P, TAB_N])
        lp = place("lp", [P, LP_N])
        aT = place("aT", [P, 4, T], offset=tab_at)
        assert max(at[0], region_end) <= nc.sbuf_usable_end

        psum = ctx.enter_context(nc.psum_tensor("psum", [P, 8, 512], F32))
        banks = [psum[:, i, :] for i in range(8)]

        def out_bank(parity, g):
            a, b = GROUPS[g]
            return banks[2 * parity + g][:, 0:b - a]

        x_landed = sem("x_landed")
        const_landed = sem("const_landed")
        ones_set = sem("ones_set")
        small_landed = sem("small_landed")
        tab_landed = sem("tab_landed")
        cache_landed = sem("cache_landed")
        raw_landed = [sem(f"raw_landed{i}") for i in range(RAW)]
        hi_made = sem("hi_made")
        lo_made = sem("lo_made")
        dn_free = sem("dn_free")
        tile_done = sem("tile_done")
        act_took = sem("act_took")
        dve_took = sem("dve_took")
        sq_ready = sem("sq_ready")
        sq_added = sem("sq_added")
        stat_done = sem("stat_done")
        std_ready = sem("std_ready")
        x_ready = sem("x_ready")
        prod_ready = sem("prod_ready")
        hhi_ready = sem("hhi_ready")
        h_ready = sem("h_ready")
        hid_hi_ready = sem("hid_hi_ready")
        hid_ready = sem("hid_ready")
        rotq_ready = sem("rotq_ready")
        rotk_ready = sem("rotk_ready")
        qm_ready = sem("qm_ready")
        rk_done = sem("rk_done")
        rv_done = sem("rv_done")
        vtok_ready = sem("vtok_ready")
        kz_ready = sem("kz_ready")
        rs_done = sem("rs_done")
        inner_ready = sem("inner_ready")
        ro_done = sem("ro_done")
        ro_taken = sem("ro_taken")
        state_ready = sem("state_ready")
        gn_mean = sem("gn_mean")
        gn_cent = sem("gn_cent")
        gn_sq = sem("gn_sq")
        gn_var = sem("gn_var")
        gn_std = sem("gn_std")
        c_ready = sem("c_ready")
        gt_done = sem("gt_done")
        gt_taken = sem("gt_taken")
        bn_ready = sem("bn_ready")
        ln_std = sem("ln_std")
        gvt_ready = sem("gvt_ready")
        mixed_done = sem("mixed_done")
        b_ready = sem("b_ready")
        b_ssq = sem("b_ssq")
        nsink_ready = sem("nsink_ready")
        vk_done = sem("vk_done")
        vk_ready = sem("vk_ready")
        s_done = sem("s_done")
        nm_ready = sem("nm_ready")
        p_ready = sem("p_ready")
        pn_ready = sem("pn_ready")
        pt_done = sem("pt_done")
        pt_ready = sem("pt_ready")
        o_done = sem("o_done")
        a_taken = sem("a_taken")
        a_ssq = sem("a_ssq")

        dve_chain = sem("dve_chain")
        pool_chain = sem("pool_chain")
        out_landed = sem("out_landed")
        y_landed = sem("y_landed")
        pe_passed, dve_passed, pool_passed = sem("pe_passed"), sem("dve_passed"), sem("pool_passed")

        block = ctx.enter_context(nc.Block())

        def cols(g):
            return slice(*GROUPS[g])

        def width(g):
            return GROUPS[g][1] - GROUPS[g][0]

        def slot_used(l, s):
            if s < S_DN:
                return tile_done, l * (2 * TILES) + (1 + 2 * (s + 1))
            last = 8 * (s - S_DN) + 7
            if last % FT == FT - 1:
                return tile_done, l * (2 * TILES) + (1 + 2 * (TILES - KT) + 2 * (last // FT + 1))
            before = sum((8 * i + 7) % FT != FT - 1 for i in range(s - S_DN + 1))
            return dn_free, l * DN_FREE + before

        def seg(g):
            if g == 0:
                return [(slice(0, 256), slice(0, 256))]
            return [(slice(0, 256), slice(256, 512)), (slice(256, GW), slice(KC - DEC, KC))]

        def score_bank(u, hh):
            return banks[2 * (u % 2) + hh]

        def grid(b, bank, w):
            return bank.rearrange("p (i n) -> p i n", n=P)[:, 0:w, 0:TB[b][1]]

        @block.sync
        def _(spe):
            spe.dma_start(x[:, :, :], xT).then_inc(x_landed, 16)
            for r in range(RAW):
                spe.dma_start(raw[:, r, :], wts[r]).then_inc(raw_landed[r], 16)
            with spe.Fori(1, DEPTH * SLOTS // RAW) as i:
                for r in range(RAW):
                    spe.wait_ge(lo_made, i * RAW + (r - RAW + 1))
                    spe.dma_start(raw[:, r, :], wts[ds(i * RAW + r, 1)].rearrange("o p n -> (o p) n"))\
                       .then_inc(raw_landed[r], 16)
            spe.wait_ge(x_ready, 1 + DEPTH * 32)
            spe.dma_start(o_x, x[:, :, :]).then_inc(y_landed, 16)
            spe.wait_ge(y_landed, 16)
            spe.wait_ge(out_landed, DEPTH * 16 * NOUT)

        @block.tensor
        def _(pe):
            pe.sem_inc(act_took, 4)
            pe.sem_inc(dve_took, 2)
            pe.sem_inc(tile_done, 1)
            pe.sem_inc(stat_done, 1)
            pe.wait_ge(const_landed, 32)
            pe.wait_ge(ones_set, 1)
            with pe.Fori(0, DEPTH) as l:

                def L(n, per):
                    return l * per + n

                def alone(s, v):
                    pe.wait_ge(s, v)
                    pe.sem_inc(pe_passed, 1)

                def three(out, ring, j, rhs_k, g, first, last, hi=h_hi, lo=h_lo):
                    wh, wl = w_hi[:, ring, j * P:(j + 1) * P], w_lo[:, ring, j * P:(j + 1) * P]
                    pe.matmul(out, wh, hi[:, rhs_k, cols(g)], start=first, stop=False)
                    pe.matmul(out, wh, lo[:, rhs_k, cols(g)], start=False, stop=False)
                    return pe.matmul(out, wl, hi[:, rhs_k, cols(g)], start=False, stop=last)

                def tile_of_8(slot, ring, parity, took, operand=None):
                    pe.wait_ge(lo_made, slot + 1)
                    for g in (0, 1):
                        pe.wait_ge(took[0], took[1] + g + 1)
                        for k in range(KT):
                            if operand is not None:
                                pe.wait_ge(h_ready, operand + (8 * g + k + 2))
                            mm = three(out_bank(parity, g), ring, k, k, g, k == 0, k == KT - 1)
                        mm.then_inc(tile_done, 1)

                def stat(g, src, bank, n, waits):
                    for s, v in waits:
                        pe.wait_ge(s, v)
                    pe.matmul(banks[bank][:, 0:width(g)], ones[:, :], src[:, cols(g)],
                              start=True, stop=True).then_inc(stat_done, 1)

                for g in (0, 1):
                    stat(g, acc, 4 + g, ST["pre_mix"] + g,
                         [(sq_added, 1 + L(SQ["pre_mix"] + 8 * (g + 1), SQS)), (std_ready, 1 + L(g, STS))])

                def ret_in(b):
                    t0, n = TB[b]
                    if b == 0:
                        pe.wait_ge(act_took, L(4 + 2 * (A_IN + IN_V1 + 1), 2 * A_TILES))
                        alone(rotk_ready, L(1, 1))
                    else:
                        pe.wait_ge(vtok_ready, L(b, NB))
                        alone(kz_ready, L(b, NB))
                    for bank, row, done in ((5, 2, rk_done), (4, 4, rv_done)):
                        for i in (0, 1):
                            mm = pe.transpose(banks[bank][0:n, i * P:(i + 1) * P], ret[:, row + i, t0:t0 + n],
                                              ident[:, :])
                        mm.then_inc(done, 1)
                    if b:
                        pe.wait_ge(inner_ready, L(b, NB))
                    alone(qm_ready, L(b + 1, NB))
                    for half in (0, 1):
                        mm = pe.matmul(banks[6][0:n, 0:RET_HEADS * P].rearrange("p (h n) -> p h n", n=P)[:, :, 0:n],
                                       ret[:, 2 + half, t0:t0 + n], qm[:, b % 2, half, :, 0:n],
                                       start=half == 0, stop=half == 1)
                    mm.then_inc(rs_done, 1)

                def ret_out(b):
                    t0, n = TB[b]
                    pe.wait_ge(vtok_ready, L(b + 1, NB))
                    pe.wait_ge(kz_ready, L(b + 1, NB))
                    if b > 0:
                        pe.wait_ge(ro_taken, L(b, NB))
                        pe.wait_ge(state_ready, L(b, NB))
                    if b == NB - 1:
                        pe.wait_ge(cache_landed, L(1, 1) * 96)
                    alone(inner_ready, L(b + 1, NB))
                    state = None if b == 0 else st_s if b == NB - 1 else st_p
                    for hh in range(RET_HEADS):
                        c = P * (hh // 2)
                        out = banks[7][64 * (hh % 2):64 * (hh % 2) + 64, c:c + n]
                        e = slice(hh * HD, (hh + 1) * HD)
                        pe.matmul(out, vtok[0:n, b, e], inner[0:n, b % 2, hh, 0:n], start=True, stop=state is None)
                        if state is not None:
                            for half in (0, 1):
                                pe.matmul(out, state[:, half, e], qxi[:, half, t0:t0 + n], start=False, stop=half == 1)
                    for hh in range(RET_HEADS):
                        for half in (0, 1):
                            c = 2 * P + half * HD
                            mm = pe.matmul(banks[7][32 * hh:32 * hh + 32, c:c + HD],
                                           kz[0:n, b % 2, half * P + 32 * hh:half * P + 32 * hh + 32],
                                           vtok[0:n, b, hh * HD:(hh + 1) * HD], start=True, stop=True,
                                           tile_position=(0, 32 * hh))
                    mm.then_inc(ro_done, 1)

                def gn(i, var):
                    c, g = i // 2, i % 2
                    a, b_ = GROUPS[g]
                    bank = banks[4 + i][:, 0:b_ - a]
                    if not var:
                        pe.wait_ge(state_ready, L(NB, NB))
                    else:
                        pe.wait_ge(gn_sq, L(i + 1, 4))
                    pe.matmul(bank, tab[:, TAB["blk"]:TAB["blk"] + P], (rsq if var else rT)[:, c, a:b_],
                              start=True, stop=True).then_inc(gn_var if var else gn_mean, 1)

                def gm_in(b):
                    t0, n = TB[b]
                    if b < 4:
                        alone(gn_std, L(b + 1, 4))
                    else:
                        alone(gt_taken, L(b - 3, NB))
                    for i in (0, 1):
                        mm = pe.transpose(banks[4 + b % 4][0:n, i * P:(i + 1) * P], gv[:, i, t0:t0 + n], ident[:, :])
                    mm.then_inc(gt_done, 1)

                def gm_mix(b):
                    t0, n = TB[b]
                    if b == 4:
                        pe.wait_ge(b_ready, L(1, NB))
                    alone(gvt_ready, L(b + 1, NB))
                    for g4 in range(4):
                        mm = pe.matmul(banks[4 + b % 4][64 * (g4 % 2):64 * (g4 % 2) + 64,
                                                        (g4 // 2) * P:(g4 // 2) * P + n],
                                       gvt[0:n, b, g4 * HD:(g4 + 1) * HD],
                                       lp[0:n, LP["gw"] + g4 * P:LP["gw"] + g4 * P + n], start=True, stop=True)
                    mm.then_inc(mixed_done, 1)

                def v_tokens():
                    alone(b_ready, L(NB, NB))
                    for b in range(4):
                        mm = pe.transpose(banks[4][:, b * P:(b + 1) * P], vv[:, b * P:(b + 1) * P], ident[:, :])
                    mm.then_inc(vk_done, 1)
                    pe.transpose(banks[5][0:DEC, 0:P], vv[:, SEQ:T], ident[:, :]).then_inc(vk_done, 1)

                fill = {i: [] for i in range(IN_T)}
                for b in range(NB):
                    fill[6 + b].append(lambda b=b: ret_in(b))
                    fill[7 + b].insert(0, lambda b=b: ret_out(b))
                    fill[14].append(lambda b=b: gm_in(b))
                    fill[16].append(lambda b=b: gm_mix(b))
                fill[12].append(lambda: [gn(i, False) for i in range(4)])
                fill[13].append(lambda: [gn(i, True) for i in range(4)])
                fill[17].append(v_tokens)

                for i in range(IN_T):
                    tile_of_8(L(S_IN + i, SLOTS), (S_IN + i) % RING, i % 2,
                              (act_took, L(2 * i, 2 * A_TILES)), L(HR["pre_mix"], HRS) if i == 0 else None)
                    for f in fill[i]:
                        f()

                def scores(u):
                    b, j = divmod(u, 4)
                    t0, n = TB[b]
                    k0, kn = WINDOW[b]
                    if u == 0:
                        alone(act_took, L(4 + 2 * (A_IN + IN_T), 2 * A_TILES))
                    elif u >= 2:
                        alone(p_ready, L(u - 1, UNITS))
                    if b == NB - 1 and j == 0:
                        alone(cache_landed, L(1, 1) * 96)
                    for hh in (0, 1):
                        out = score_bank(u, hh)[0:n, 0:kn]
                        r = slice(64 * hh, 64 * hh + 64)
                        masked = b < NB - 1
                        if masked:
                            pe.matmul(out, mask[r, 0:P], mask[r, P + 256 - kn:P + 256], start=True, stop=False)
                        mm = pe.matmul(out, qq[r, j, t0:t0 + n], kk[r, k0:k0 + kn], start=not masked, stop=True)
                    mm.then_inc(s_done, 1)

                def turn(u):
                    b, j = divmod(u, 4)
                    t0, n = TB[b]
                    kn = WINDOW[b][1]
                    if u >= 2:
                        pe.wait_ge(pt_ready, L(u - 1, UNITS))
                    elif u == 0:
                        pe.wait_ge(vk_ready, L(2, 2))
                    alone(pn_ready, L(u + 1, UNITS))
                    for hh in (0, 1):
                        for kt in range((kn + P - 1) // P):
                            w = min(P, kn - kt * P)
                            mm = pe.transpose(banks[4 + u % 2][0:w, (hh * 2 + kt) * P:(hh * 2 + kt) * P + n],
                                              prob[0:n, u % 4, hh, kt * P:kt * P + w], ident[0:n, 0:n])
                    mm.then_inc(pt_done, 1)

                def values(u):
                    b, j = divmod(u, 4)
                    t0, n = TB[b]
                    kn = WINDOW[b][1]
                    if j == 0:
                        if b >= 2:
                            pe.wait_ge(a_taken, L(b - 1, NB))
                        if b == 0:
                            pe.wait_ge(ro_taken, L(NB, NB))
                            pe.wait_ge(state_ready, L(NB, NB))
                            pe.wait_ge(b_ready, L(NB, NB))
                    alone(pt_ready, L(u + 1, UNITS))
                    for hh in (0, 1):
                        for kt in range((kn + P - 1) // P):
                            w = min(P, kn - kt * P)
                            mm = pe.matmul(banks[6 + b % 2][64 * hh:64 * hh + 64, j * P:j * P + n],
                                           vk[0:w, VTILES[b][kt], 64 * hh:64 * hh + 64],
                                           probT[0:w, u % 4, hh, kt, 0:n], start=kt == 0,
                                           stop=kt == (kn + P - 1) // P - 1, tile_position=(0, 64 * hh))
                    mm.then_inc(o_done, 1)

                for u in range(UNITS + 5):
                    if u < UNITS:
                        scores(u)
                    if 3 <= u < UNITS + 3:
                        turn(u - 3)
                    if u >= 5:
                        values(u - 5)

                for g in (0, 1):
                    stat(g, acc, 4 + g, ST["merged"] + 2 * g,
                         [(a_ssq, L(GROUP_BLOCKS[g][-1] + 1, NB)), (pt_ready, L(UNITS, UNITS))])
                    stat(g, rstd, 6 + g, ST["merged"] + 2 * g + 1, [(b_ssq, L(1, 1)), (a_taken, L(NB, NB))])

                for m in range(OUT_T):
                    s = S_OUT + m
                    if m == 0:
                        pe.wait_ge(p_ready, L(UNITS, UNITS))
                        pe.wait_ge(nm_ready, L(UNITS, UNITS))
                    tile_of_8(L(s, SLOTS), s % RING, m % 2, (act_took, L(2 * (A_OUT + m), 2 * A_TILES)),
                              L(HR["merged"], HRS) if m == 0 else None)

                for what in ("post_mix", "pre_ffn"):
                    for g in (0, 1):
                        stat(g, acc, 4 + g, ST[what] + g,
                             [(sq_added, 1 + L(SQ[what] + (15 + g if what == "post_mix" else 8 * (g + 1)), SQS)),
                              (std_ready, 1 + L(ST[what], STS))])

                alone(h_ready, 1 + L(HR["pre_ffn"] + 16, HRS))
                with pe.Fori(0, FT // 2) as it:
                    for i in (0, 1):
                        s = S_GU + 2 * i
                        tile_of_8(L(s, SLOTS) + it * 4, s % RING, 0,
                                  (act_took, L(4 + 2 * (A_GATE + i - 1), 2 * A_TILES) + it * 4))
                        tile_of_8(L(s + 1, SLOTS) + it * 4, (s + 1) % RING, 1,
                                  (dve_took, L(2 * i, 2 * FT) + it * 4))

                pe.wait_ge(hid_ready, L(2 * FT, 2 * FT))
                pe.wait_ge(act_took, L(4 + 2 * A_DN, 2 * A_TILES))
                pe.wait_ge(dve_took, L(2 + 2 * FT, 2 * FT))
                for m in range(KT):
                    for k in range(FT):
                        f = m * FT + k
                        s = S_DN + f // 8
                        if f % 8 == 0:
                            pe.wait_ge(lo_made, L(s + 1, SLOTS))
                        for g in (0, 1):
                            if k == 0 and m >= 2:
                                pe.wait_ge(act_took, L(4 + 2 * (A_DN + m - 2) + g + 1, 2 * A_TILES))
                            mm = three(out_bank(m % 2, g), s % RING, f % 8, k, g, k == 0, k == FT - 1, hid_hi, hid_lo)
                            if k == FT - 1:
                                mm.then_inc(tile_done, 1)
                        if f % 8 == 7 and k < FT - 1:
                            mm.then_inc(dn_free, 1)
                for g in (0, 1):
                    stat(g, acc, 4 + g, ST["post_ffn"] + g,
                         [(sq_added, 1 + L(SQ["post_ffn"] + 15 + g, SQS)), (std_ready, 1 + L(ST["post_ffn"], STS))])

        @block.scalar
        def _(act):
            def fn(out, in_, f, **kw):
                return act.activation(out, in_, f, **kw)

            act.sem_inc(std_ready, 1)
            act.wait_ge(x_landed, 16)
            act.wait_ge(ones_set, 1)
            with act.Fori(0, DEPTH) as l:

                def L(n, per):
                    return l * per + n

                def split(s, off=0, raw_count=None):
                    r = s % RAW
                    act.wait_ge(raw_landed[r], (L(s // RAW + 1, SLOTS // RAW) + off // RAW) * 16
                                if raw_count is None else raw_count)
                    fn(w_hi[:, s % RING, :], raw[:, r, :], ACT.Copy).then_inc(hi_made, 1)

                def squares(what, g, k, src):
                    i = 8 * g + k
                    act.wait_ge(sq_added, 1 + L(SQ[what] + max(i - 1, 0), SQS))
                    fn(sq[:, i % 2, 0:width(g)], src, ACT.Square).then_inc(sq_ready, 1)

                def root(n, g, out, bank, count):
                    act.wait_ge(stat_done, 1 + L(n + 1, STS))
                    fn(out[:, cols(g)], banks[bank][:, 0:width(g)], ACT.Sqrt, bias=epsc[:, 0:1],
                       scale=1.0 / count).then_inc(std_ready, 1)

                def hi_of_operand(what, g, k):
                    i = 8 * g + k
                    act.wait_ge(prod_ready, L(HR[what] + i + 1, HRS))
                    fn(h_hi[:, k, cols(g)], tp[:, i % 2, 0:width(g)], ACT.Copy).then_inc(hhi_ready, 1)

                act.wait_ge(tile_done, 1 + L(0, 2 * TILES))
                for s in range(RING):
                    split(s)
                act.wait_ge(x_ready, 1 + L(0, 32))
                for g in (0, 1):
                    for k in range(KT):
                        squares("pre_mix", g, k, x[:, k, cols(g)])
                for g in (0, 1):
                    root(ST["pre_mix"] + g, g, rstd, 4 + g, D)
                for g in (0, 1):
                    for k in range(KT):
                        hi_of_operand("pre_mix", g, k)

                def vtok_copy(b):
                    n = TB[b][1]
                    act.wait_ge(rv_done, L(b + 1, NB))
                    fn(vtok[0:n, b, :], banks[4][0:n, 0:256], ACT.Copy).then_inc(vtok_ready, 1)

                def gt_copy(b):
                    n = TB[b][1]
                    act.wait_ge(gt_done, L(b + 1, NB))
                    fn(gvt[0:n, b, :], banks[4 + b % 4][0:n, 0:256], ACT.Copy)\
                        .then_inc(gt_taken, 1)

                def gn_square(i):
                    c, g = i // 2, i % 2
                    act.wait_ge(gn_cent, L(i + 1, 4))
                    fn(rsq[:, c, cols(g)], rT[:, c, cols(g)], ACT.Square).then_inc(gn_sq, 1)

                def gn_root(i):
                    c, g = i // 2, i % 2
                    act.wait_ge(gn_var, L(i + 1, 4))
                    fn(rsq[:, c, cols(g)], banks[4 + i][:, 0:width(g)], ACT.Sqrt, bias=epsc[:, 0:1])\
                        .then_inc(gn_std, 1)

                def ln_root():
                    act.wait_ge(bn_ready, L(NB, NB))
                    n = TB[-1][1]
                    fn(brs[:, 0:NB - 1], bmv[:, 0:NB - 1, 1], ACT.Sqrt, bias=epsc[:, 0:1])
                    fn(brs[0:n, NB - 1:NB], bmv[0:n, NB - 1:NB, 1], ACT.Sqrt, bias=epsc[0:n, 0:1])\
                        .then_inc(ln_std, 1)

                def vk_copy():
                    act.wait_ge(vk_done, L(1, 2))
                    fn(vk[:, 0:4, :], banks[4][:, :].rearrange("p (i n) -> p i n", n=P), ACT.Copy)\
                        .then_inc(vk_ready, 1)
                    act.wait_ge(vk_done, L(2, 2))
                    fn(vk[0:DEC, 5, :], banks[5][0:DEC, 0:P], ACT.Copy).then_inc(vk_ready, 1)

                more = {i: [] for i in range(IN_T)}
                for b in range(NB):
                    more[6 + b].append(lambda b=b: vtok_copy(b))
                    more[14].append(lambda b=b: gt_copy(b))
                for i in range(4):
                    more[12].append(lambda i=i: gn_square(i))
                    more[13].append(lambda i=i: gn_root(i))
                more[14].append(ln_root)
                more[17].append(vk_copy)

                for i in range(IN_T):
                    for g in (0, 1):
                        act.wait_ge(tile_done, 1 + L(2 * (S_IN + i) + g + 1, 2 * TILES))
                        bank = out_bank(i % 2, g)
                        if i == IN_K:
                            for n, (a, b) in enumerate(seg(g)):
                                last = fn(kk[:, b], bank[:, a], ACT.Copy)
                        elif i <= IN_V1:
                            last = fn(ret[:, i, cols(g)], bank, ACT.Copy)
                        elif i <= IN_G1:
                            last = fn(sg[:, i - IN_G0, cols(g)], bank, ACT.Silu)
                        elif i <= IN_VB1:
                            last = fn(gv[:, i - IN_VB0, cols(g)], bank, ACT.Gelu_apprx_tanh)
                        elif i <= IN_UB1:
                            last = fn(ub[:, i - IN_UB0, cols(g)], bank, ACT.Gelu_apprx_tanh)
                        elif i == IN_V:
                            last = fn(vv[:, cols(g)], bank, ACT.Copy)
                        else:
                            last = fn(qq[:, i - IN_Q0, cols(g)], bank, ACT.Copy)
                        last.then_inc(act_took, 1)
                    split(S_IN + i + RING)
                    for f in more[i]:
                        f()

                def exps(u):
                    b, j = divmod(u, 4)
                    n, kn = TB[b][1], WINDOW[b][1]
                    act.wait_ge(nm_ready, L(u + 1, UNITS))
                    for hh in (0, 1):
                        fn(prob[0:n, u % 4, hh, 0:kn], score_bank(u, hh)[0:n, 0:kn], ACT.Exp,
                           bias=nm[0:n, u % 2, hh:hh + 1], scale=SCALE, accum_out=den[0:n, u % 2, hh:hh + 1])
                    fn(es[0:n, u % 2, :], sm[0:n, u % 2, :], ACT.Exp).then_inc(p_ready, 1)

                def turned(u):
                    b = u // 4
                    n, kn = TB[b][1], WINDOW[b][1]
                    act.wait_ge(pt_done, L(u + 1, UNITS))
                    bank = banks[4 + u % 2][:, :].rearrange("p (h k n) -> p h k n", h=2, k=2)
                    for kt in range((kn + P - 1) // P):
                        w = min(P, kn - kt * P)
                        last = fn(probT[0:w, u % 4, :, kt, 0:n], bank[0:w, :, kt, 0:n], ACT.Copy)
                    last.then_inc(pt_ready, 1)

                def outs(b):
                    t0, n = TB[b]
                    act.wait_ge(o_done, L(4 * b + 4, UNITS))
                    fn(aT[:, :, t0:t0 + n], grid(b, banks[6 + b % 2][:, :], 4), ACT.Copy)
                    if b:
                        act.wait_ge(a_ssq, L(b, NB))
                    fn(sqa[:, :, 0:n], grid(b, banks[6 + b % 2][:, :], 4), ACT.Square).then_inc(a_taken, 1)

                for u in range(UNITS + 5):
                    if u < UNITS:
                        exps(u)
                    if 3 <= u < UNITS + 3:
                        turned(u - 3)
                    if u >= 5 and (u - 5) % 4 == 3:
                        outs((u - 5) // 4)

                for g in (0, 1):
                    root(ST["merged"] + 2 * g, g, acc, 4 + g, SWA_HEADS * HD)
                    root(ST["merged"] + 2 * g + 1, g, rstd, 6 + g, 256)
                for g in (0, 1):
                    for k in range(KT):
                        hi_of_operand("merged", g, k)

                for m in range(OUT_T):
                    for g in (0, 1):
                        act.wait_ge(tile_done, 1 + L(2 * (S_OUT + m) + g + 1, 2 * TILES))
                        i = 2 * m + g
                        act.wait_ge(sq_added, 1 + L(SQ["post_mix"] + max(i - 1, 0), SQS))
                        fn(sq[:, g, 0:width(g)], out_bank(m % 2, g), ACT.Square).then_inc(sq_ready, 1)
                        fn(y_mix[:, m, cols(g)], out_bank(m % 2, g), ACT.Copy).then_inc(act_took, 1)
                    split(S_OUT + m + RING)
                for g in (0, 1):
                    root(ST["post_mix"] + g, g, rstd, 4 + g, D)
                for g in (0, 1):
                    for k in range(KT):
                        act.wait_ge(x_ready, 1 + L(8 * g + k + 1, 32))
                        squares("pre_ffn", g, k, x[:, k, cols(g)])
                for g in (0, 1):
                    root(ST["pre_ffn"] + g, g, rstd, 4 + g, D)
                for g in (0, 1):
                    for k in range(KT):
                        hi_of_operand("pre_ffn", g, k)

                act.wait_ge(out_landed, L(NOUT, NOUT) * 16)
                with act.Fori(0, FT // 2) as it:
                    for i in (0, 1):
                        s = S_GU + 2 * i
                        for g in (0, 1):
                            act.wait_ge(tile_done, 1 + L(2 * s + g + 1, 2 * TILES) + it * 8)
                            fn(sq[:, g, 0:width(g)], out_bank(0, g), ACT.Silu).then_inc(act_took, 1)
                        split(s + RING, off=it * 4)
                        act.wait_ge(tile_done, 1 + L(2 * (s + 2), 2 * TILES) + it * 8)
                        split(s + 1 + RING, off=it * 4)
                        for g in (0, 1):
                            act.wait_ge(dve_took, L(2 + 2 * i + g + 1, 2 * FT) + it * 4)
                            fn(hid_hi[:, ds(it * 2 + i, 1), cols(g)], tp[:, g:g + 1, 0:width(g)], ACT.Copy)\
                                .then_inc(hid_hi_ready, 1)

                for s in range(S_DN, SLOTS):
                    a, b = 8 * (s - S_DN), 8 * (s - S_DN) + 8
                    if s + RING < SLOTS:
                        act.wait_ge(*slot_used(l, s))
                        split(s + RING)
                    for m in range(KT):
                        if not a <= m * FT + FT - 1 < b:
                            continue
                        for g in (0, 1):
                            act.wait_ge(tile_done, 1 + L(2 * (TILES - KT + m) + g + 1, 2 * TILES))
                            i = 2 * m + g
                            act.wait_ge(sq_added, 1 + L(SQ["post_ffn"] + max(i - 1, 0), SQS))
                            fn(sq[:, g, 0:width(g)], out_bank(m % 2, g), ACT.Square).then_inc(sq_ready, 1)
                            fn(y_ffn[:, m, cols(g)], out_bank(m % 2, g), ACT.Copy).then_inc(act_took, 1)
                for g in (0, 1):
                    root(ST["post_ffn"] + g, g, rstd, 4 + g, D)

        @block.vector
        def _(dve):
            dve.sem_inc(x_ready, 1)
            dve.sem_inc(h_ready, 1)
            dve.memset(ones[:, :], 1.0).then_inc(dve_chain, 1)
            dve.memset(st_p[:, :, :], 0.0)
            dve.memset(epsc[:, :], EPS).then_inc(ones_set, 1)
            with dve.Fori(0, DEPTH) as l:
                links = [0]

                def L(n, per):
                    return l * per + n

                def link(last):
                    links[0] += 1
                    last.then_inc(dve_chain, 1)
                    dve.wait_ge(dve_chain, l * DVE_LINKS + (links[0] + 1))

                def split(s, off=0):
                    dve.wait_ge(hi_made, L(s + 1, SLOTS) + off)
                    dve.tensor_tensor(w_lo[:, s % RING, :], raw[:, s % RAW, :],
                                      w_hi[:, s % RING, :].bitcast(F32), ALU.subtract).then_inc(lo_made, 1)

                def recip(n, g, t):
                    dve.wait_ge(std_ready, 1 + L(n + 1, STS))
                    link(dve.reciprocal(t[:, cols(g)], t[:, cols(g)]))

                def operand(what, g, products):
                    def lo(k):
                        i = 8 * g + k
                        dve.wait_ge(hhi_ready, L(HR[what] + i + 1, HRS))
                        dve.tensor_tensor(h_lo[:, k, cols(g)], tp[:, i % 2, 0:width(g)],
                                          h_hi[:, k, cols(g)].bitcast(F32), ALU.subtract).then_inc(h_ready, 1)

                    for k in range(KT):
                        i = 8 * g + k
                        if i >= 2:
                            dve.wait_ge(h_ready, 1 + L(HR[what] + i - 1, HRS))
                        else:
                            dve.wait_ge(h_ready, 1 + L(HR[what], HRS))
                            dve.wait_ge(x_ready, 1 + L(16 if what == "pre_ffn" else 0, 32))
                        src, gain, scale = products(k)
                        dve.scalar_tensor_tensor(out=tp[:, k % 2, 0:width(g)], in0=src, scalar=gain, in1=scale,
                                                 op0=ALU.mult, op1=ALU.mult).then_inc(prod_ready, 1)
                        if k:
                            lo(k - 1)
                    lo(KT - 1)

                def gain(what, k):
                    c = SP[what] + k
                    return sp[:, c:c + 1]

                def residual(g, y, what):
                    base = 0 if what == "post_mix" else 16
                    if g == 0:
                        if what == "post_mix":
                            dve.wait_ge(h_ready, 1 + L(HR["pre_ffn"], HRS))
                        else:
                            dve.wait_ge(hid_ready, L(2 * FT, 2 * FT))
                    for k in range(0, KT, 2):
                        dve.wait_ge(x_ready, 1 + L(base + 8 * g + k, 32))
                        for i in (0, 1):
                            last = dve.scalar_tensor_tensor(
                                out=tp[:, i, 0:width(g)], in0=y[:, k + i, cols(g)], scalar=gain(what, k + i),
                                in1=rstd[:, cols(g)], op0=ALU.mult, op1=ALU.mult)
                        link(last)
                        for i in (0, 1):
                            dve.tensor_tensor(x[:, k + i, cols(g)], x[:, k + i, cols(g)], tp[:, i, 0:width(g)],
                                              ALU.add).then_inc(x_ready, 1)

                for s in range(RING):
                    split(s)
                dve.wait_ge(small_landed, L(1, 1) * 16)
                for g in (0, 1):
                    recip(ST["pre_mix"] + g, g, rstd)
                    operand("pre_mix", g, lambda k: (x[:, k, cols(g)], gain("pre_mix", k), rstd[:, cols(g)]))
                dve.tensor_scalar(nsink[:, :], sp[:, SP["sink"]:SP["sink"] + 8], -1.0, None, ALU.mult)\
                   .then_inc(nsink_ready, 1)

                def table(name, w, n=P):
                    return tab[0:n, TAB[name]:TAB[name] + w]

                def rotate_q():
                    dve.wait_ge(tab_landed, L(1, 1) * 32)
                    gw = lp[CHUNK:P, LP["gw"]:LP["gw"] + 4 * P].rearrange("p (g i) -> p g i", i=P)
                    dve.memset(gw[:, :, 0:CHUNK], 0.0)
                    dve.wait_ge(act_took, L(4 + 2 * (A_IN + IN_QB + 1), 2 * A_TILES))
                    A, B = ret[:, 0, :], ret[:, 1, :]
                    dve.tensor_tensor(rtmp[:, 0, :], A, table("sin", T), ALU.mult)
                    link(dve.tensor_tensor(rtmp[:, 1, :], B, table("sin", T), ALU.mult))
                    dve.tensor_tensor(A, A, table("cos", T), ALU.mult)
                    link(dve.tensor_tensor(B, B, table("cos", T), ALU.mult))
                    dve.tensor_tensor(A, A, rtmp[:, 1, :], ALU.subtract)
                    link(dve.tensor_tensor(B, B, rtmp[:, 0, :], ALU.add))
                    xi = table("xi", P)
                    for half in (0, 1):
                        dve.tensor_tensor(qxi[:, half, 0:SEQ].rearrange("p (b n) -> p b n", n=P),
                                          ret[:, half, 0:SEQ].rearrange("p (b n) -> p b n", n=P),
                                          xi.unsqueeze(1).to_broadcast([P, 4, P]), ALU.mult)
                        last = dve.tensor_tensor(qxi[:, half, SEQ:T], ret[:, half, SEQ:T], xi[:, 0:DEC], ALU.mult)
                    last.then_inc(rotq_ready, 1)

                def decay(b):
                    n = TB[b][1]
                    if b >= 2:
                        dve.wait_ge(ro_done, L(b - 1, NB))
                    dve.wait_ge(rk_done, L(b + 1, NB))
                    dve.tensor_tensor(kz[0:n, b % 2, :], banks[5][0:n, 0:256],
                                      table("zeta" if b < NB - 1 else "zetas", 256, n), ALU.mult).then_inc(kz_ready, 1)
                    dve.wait_ge(rs_done, L(b + 1, NB))
                    dve.tensor_tensor(inner[0:n, b % 2, :, 0:n], grid(b, banks[6][0:n, :], 4),
                                      grid(b, table("decay", 512, n), 4), ALU.mult).then_inc(inner_ready, 1)

                def state(b):
                    t0, n = TB[b]
                    dve.wait_ge(ro_done, L(b + 1, NB))
                    dve.tensor_copy(rT[:, :, t0:t0 + n], grid(b, banks[7][:, 0:2 * P], 2)).then_inc(ro_taken, 1)
                    if b:
                        dve.wait_ge(state_ready, L(b, NB))
                    st = st_s if b == NB - 1 else st_p
                    c = TAB["cdec"] + (b == NB - 1)
                    for hh in range(RET_HEADS):
                        r = slice(32 * hh, 32 * hh + 32)
                        new = banks[7][r, 2 * P:3 * P].rearrange("p (h d) -> p h d", h=2)
                        old = st[r, :, hh * HD:(hh + 1) * HD]
                        if b == 0:
                            last = dve.tensor_copy(old, new)
                        else:
                            last = dve.scalar_tensor_tensor(out=old, in0=old, scalar=tab[r, c:c + 1], in1=new,
                                                            op0=ALU.mult, op1=ALU.add)
                    last.then_inc(state_ready, 1)

                def bn(b):
                    n = TB[b][1]
                    dve.wait_ge(gt_taken, L(b + 1, NB))
                    link(dve.bn_stats(bst[0:n, b, :], gvt[0:n, b, :]))
                    dve.sem_inc(dve_passed, 1)
                    dve.bn_aggr(bmv[0:n, b, :], bst[0:n, b, :]).then_inc(bn_ready, 1)

                def centre(i):
                    c, g = i // 2, i % 2
                    dve.wait_ge(gn_mean, L(i + 1, 4))
                    dve.tensor_tensor(rT[:, c, cols(g)], rT[:, c, cols(g)], banks[4 + i][:, 0:width(g)],
                                      ALU.subtract).then_inc(gn_cent, 1)

                def scale_r(i):
                    c, g = i // 2, i % 2
                    dve.wait_ge(gn_std, L(i + 1, 4))
                    link(dve.reciprocal(rsq[:, c, cols(g)], rsq[:, c, cols(g)]))
                    dve.tensor_tensor(rT[:, c, cols(g)], rT[:, c, cols(g)], rsq[:, c, cols(g)], ALU.mult)\
                       .then_inc(c_ready, 1)

                def v_rows():
                    dve.wait_ge(ln_std, L(1, 1))
                    dve.wait_ge(gt_taken, L(NB, NB))
                    n = TB[-1][1]
                    dve.reciprocal(brs[:, 0:NB - 1], brs[:, 0:NB - 1])
                    link(dve.reciprocal(brs[0:n, NB - 1:NB], brs[0:n, NB - 1:NB]))
                    for b in range(NB):
                        n = TB[b][1]
                        last = dve.tensor_scalar(gvt[0:n, b, :], gvt[0:n, b, :], bmv[0:n, b, 0:1],
                                                 brs[0:n, b:b + 1], ALU.subtract, ALU.mult)
                    link(last)
                    for b in range(NB):
                        n = TB[b][1]
                        last = dve.tensor_tensor(gvt[0:n, b, :], gvt[0:n, b, :], lp[0:n, LP["lng"]:LP["lng"] + 256],
                                                 ALU.mult)
                    link(last)
                    for b in range(NB):
                        n = TB[b][1]
                        dve.tensor_tensor(gvt[0:n, b, :], gvt[0:n, b, :], lp[0:n, LP["lnb"]:LP["lnb"] + 256],
                                          ALU.add).then_inc(gvt_ready, 1)

                def gate_b(b):
                    t0, n = TB[b]
                    dve.wait_ge(mixed_done, L(b + 1, NB))
                    bank = banks[4 + b % 4][:, 0:2 * P]
                    if b == 0:
                        dve.wait_ge(c_ready, L(4, 4))
                    link(dve.tensor_tensor(rsq[:, :, t0:t0 + n], grid(b, bank, 2),
                                           grid(b, lp[:, LP["gb"]:LP["gb"] + 256], 2), ALU.add))
                    dve.tensor_tensor(ub[:, :, t0:t0 + n], ub[:, :, t0:t0 + n], rsq[:, :, t0:t0 + n],
                                      ALU.mult).then_inc(b_ready, 1)

                more = {i: [] for i in range(IN_T)}
                more[3].append(rotate_q)
                for b in range(NB):
                    more[7 + b].append(lambda b=b: state(b))
                    more[6 + b].append(lambda b=b: decay(b))
                    more[14].append(lambda b=b: bn(b))
                    more[16].append(lambda b=b: gate_b(b))
                for i in range(4):
                    more[12].append(lambda i=i: centre(i))
                    more[13].append(lambda i=i: scale_r(i))
                more[14].append(v_rows)
                for i in range(IN_T):
                    split(S_IN + i + RING)
                    for f in more[i]:
                        f()

                dve.wait_ge(nsink_ready, L(1, 1))

                def maxima(u):
                    b, j = divmod(u, 4)
                    n, kn = TB[b][1], WINDOW[b][1]
                    dve.wait_ge(s_done, L(u + 1, UNITS))
                    i = 2 * (u % 2)
                    bank = psum[0:n, i:i + 2, 0:kn]
                    ns = nsink[0:n, 2 * j:2 * j + 2]
                    if u >= 2:
                        dve.wait_ge(nm_ready, L(u - 1, UNITS))
                    link(dve.tensor_reduce(mx[0:n, u % 2, :], bank, AX.X, ALU.max))
                    link(dve.scalar_tensor_tensor(out=nm[0:n, u % 2, :], in0=mx[0:n, u % 2, :], scalar=-SCALE,
                                                  in1=ns, op0=ALU.mult, op1=ALU.min))
                    dve.tensor_tensor(sm[0:n, u % 2, :], nm[0:n, u % 2, :], ns, ALU.subtract).then_inc(nm_ready, 1)

                def normalise(u):
                    b = u // 4
                    n, kn = TB[b][1], WINDOW[b][1]
                    dve.wait_ge(p_ready, L(u + 1, UNITS))
                    if u >= 2:
                        dve.wait_ge(pn_ready, L(u - 1, UNITS))
                    link(dve.tensor_tensor(rd[0:n, u % 2, :], den[0:n, u % 2, :], es[0:n, u % 2, :], ALU.add))
                    link(dve.reciprocal(rd[0:n, u % 2, :], rd[0:n, u % 2, :]))
                    for hh in (0, 1):
                        last = dve.tensor_scalar(prob[0:n, u % 4, hh, 0:kn], prob[0:n, u % 4, hh, 0:kn],
                                                 rd[0:n, u % 2, hh:hh + 1], None, ALU.mult)
                    last.then_inc(pn_ready, 1)

                for u in range(UNITS + 1):
                    if u < UNITS:
                        maxima(u)
                    if u:
                        normalise(u - 1)

                for g in (0, 1):
                    recip(ST["merged"] + 2 * g, g, acc)
                    recip(ST["merged"] + 2 * g + 1, g, rstd)

                    def merged(k, g=g):
                        if k < 4:
                            return aT[:, k, cols(g)], gain("na", k), acc[:, cols(g)]
                        if k < 6:
                            return ub[:, k - 4, cols(g)], gain("nb", k - 4), rstd[:, cols(g)]
                        return rT[:, k - 6, cols(g)], gain("rg", k - 6), sg[:, k - 6, cols(g)]

                    operand("merged", g, merged)

                for m in range(OUT_T):
                    split(S_OUT + m + RING)
                for g in (0, 1):
                    recip(ST["post_mix"] + g, g, rstd)
                    residual(g, y_mix, "post_mix")
                for g in (0, 1):
                    recip(ST["pre_ffn"] + g, g, rstd)
                    operand("pre_ffn", g, lambda k: (x[:, k, cols(g)], gain("pre_ffn", k), rstd[:, cols(g)]))

                with dve.Fori(0, FT // 2) as it:
                    for i in (0, 1):
                        s = S_GU + 2 * i
                        split(s + RING, off=it * 4)
                        for g in (0, 1):
                            dve.wait_ge(tile_done, 1 + L(2 * (s + 1) + g + 1, 2 * TILES) + it * 8)
                            dve.wait_ge(act_took, L(4 + 2 * (A_GATE + i) + g + 1, 2 * A_TILES) + it * 4)
                            dve.tensor_tensor(tp[:, g, 0:width(g)], sq[:, g, 0:width(g)], out_bank(1, g),
                                              ALU.mult).then_inc(dve_took, 1)
                        split(s + 1 + RING, off=it * 4)
                        for g in (0, 1):
                            dve.wait_ge(hid_hi_ready, L(2 * i + g + 1, 2 * FT) + it * 4)
                            dve.tensor_tensor(hid_lo[:, ds(it * 2 + i, 1), cols(g)], tp[:, g:g + 1, 0:width(g)],
                                              hid_hi[:, ds(it * 2 + i, 1), cols(g)].bitcast(F32), ALU.subtract)\
                               .then_inc(hid_ready, 1)
                        dve.wait_ge(hid_ready, L(2 * i + 2, 2 * FT) + it * 4)

                for s in range(S_DN, SLOTS - RING):
                    split(s + RING)
                for g in (0, 1):
                    recip(ST["post_ffn"] + g, g, rstd)
                    residual(g, y_ffn, "post_ffn")
                assert links[0] == DVE_LINKS, links[0]

        @block.gpsimd
        def _(pool):
            pool.sem_inc(sq_added, 1)
            pool.dma_start(ident[:, :], ident_d).then_inc(const_landed, 16)
            pool.dma_start(mask[:, :], mask_d).then_inc(const_landed, 16)
            with pool.Fori(0, DEPTH) as l:
                links = [0]

                def L(n, per):
                    return l * per + n

                def link(last):
                    links[0] += 1
                    last.then_inc(pool_chain, 1)
                    pool.wait_ge(pool_chain, l * POOL_LINKS + links[0])

                def alone(s, v):
                    pool.wait_ge(s, v)
                    pool.sem_inc(pool_passed, 1)

                def states(dram):
                    return dram[ds(l, 1)].rearrange("o p h d -> (o p) h d")

                def layer(dram):
                    return dram[ds(l, 1)].rearrange("o p n -> (o p) n")

                pool.wait_ge(ones_set, 1)
                alone(x_ready, 1 + L(0, 32))
                pool.dma_start(sp[:, :], layer(small)).then_inc(small_landed, 16)
                alone(tile_done, 1 + L(0, 2 * TILES))
                link(pool.memset(st_s[:, :, :], 0.0))
                pool.sem_inc(pool_passed, 1)
                pool.dma_start(tab[:, :], tabs).then_inc(tab_landed, 16)
                pool.dma_start(lp[:, :], layer(lpar)).then_inc(tab_landed, 16)
                pool.dma_start(kk[:, SEQ:SEQ + P], layer(kcache)).then_inc(cache_landed, 16)
                pool.dma_start(vk[:, 4, :], layer(vcache)).then_inc(cache_landed, 16)
                for hh in range(RET_HEADS):
                    r = slice(32 * hh, 32 * hh + 32)
                    pool.dma_start(st_s[r, :, hh * HD:(hh + 1) * HD], states(ret0)[r]).then_inc(cache_landed, 16)

                def add_squares(what, g, k, n):
                    pool.wait_ge(sq_ready, L(SQ[what] + n + 1, SQS))
                    buf = sq[:, n % 2, 0:width(g)]
                    if k == 0:
                        alone(stat_done, 1 + L(dict(pre_mix=0, post_mix=6, pre_ffn=8, post_ffn=10)[what], STS))
                        pool.tensor_copy(acc[:, cols(g)], buf).then_inc(sq_added, 1)
                    else:
                        pool.wait_ge(sq_added, 1 + L(SQ[what] + n, SQS))
                        pool.tensor_tensor(acc[:, cols(g)], acc[:, cols(g)], buf, ALU.add).then_inc(sq_added, 1)

                for g in (0, 1):
                    for k in range(KT):
                        add_squares("pre_mix", g, k, 8 * g + k)

                pool.wait_ge(tab_landed, L(1, 1) * 32)
                pool.wait_ge(act_took, L(4 + 2 * (A_IN + IN_KB + 1), 2 * A_TILES))
                A, B = ret[:, 2, :], ret[:, 3, :]
                cosk, sink = (tab[:, TAB[x_]:TAB[x_] + T] for x_ in ("cosk", "sink"))
                pool.tensor_tensor(ptmp[:, 0, :], A, sink, ALU.mult)
                link(pool.tensor_tensor(ptmp[:, 1, :], B, sink, ALU.mult))
                pool.tensor_tensor(A, A, cosk, ALU.mult)
                link(pool.tensor_tensor(B, B, cosk, ALU.mult))
                pool.tensor_tensor(A, A, ptmp[:, 1, :], ALU.subtract)
                pool.tensor_tensor(B, B, ptmp[:, 0, :], ALU.add).then_inc(rotk_ready, 1)

                head = tab[:, TAB["head"]:TAB["head"] + RET_HEADS].unsqueeze(2)
                pool.wait_ge(rotq_ready, L(1, 1))
                for b in range(NB):
                    t0, n = TB[b]
                    if b >= 2:
                        pool.wait_ge(rs_done, L(b - 1, NB))
                    for half in (0, 1):
                        last = pool.tensor_tensor(qm[:, b % 2, half, :, 0:n],
                                                  ret[:, half, t0:t0 + n].unsqueeze(1).to_broadcast([P, RET_HEADS, n]),
                                                  head.to_broadcast([P, RET_HEADS, n]), ALU.mult)
                    last.then_inc(qm_ready, 1)

                alone(state_ready, L(NB, NB))
                for hh in range(RET_HEADS):
                    r = slice(32 * hh, 32 * hh + 32)
                    for dram, st in ((o_rp, st_p), (o_rs, st_s)):
                        pool.dma_start(states(dram)[r], st[r, :, hh * HD:(hh + 1) * HD]).then_inc(out_landed, 16)
                alone(gvt_ready, L(NB, NB))
                pool.dma_start(layer(o_gv), gvt[0:DEC, NB - 1, :]).then_inc(out_landed, 16)
                alone(act_took, L(4 + 2 * (A_IN + IN_V + 1), 2 * A_TILES))
                W = P + DEC
                for dram, t, end in ((o_k, kk, KC), (o_v, vv, T)):
                    pool.dma_start(layer(dram)[:, 0:P], t[:, SEQ - P:SEQ]).then_inc(out_landed, 16)
                    pool.dma_start(layer(dram)[:, P:W], t[:, end - DEC:end]).then_inc(out_landed, 16)

                pool.wait_ge(b_ready, L(NB, NB))
                link(pool.tensor_tensor(gv[:, :, :], ub[:, :, :], ub[:, :, :], ALU.mult))
                pool.tensor_tensor(rstd[:, :], gv[:, 0, :], gv[:, 1, :], ALU.add).then_inc(b_ssq, 1)
                for b in range(NB):
                    t0, n = TB[b]
                    pool.wait_ge(a_taken, L(b + 1, NB))
                    link(pool.tensor_tensor(acc[:, t0:t0 + n], sqa[:, 0, 0:n], sqa[:, 1, 0:n], ALU.add))
                    link(pool.tensor_tensor(acc[:, t0:t0 + n], acc[:, t0:t0 + n], sqa[:, 2, 0:n], ALU.add))
                    pool.tensor_tensor(acc[:, t0:t0 + n], acc[:, t0:t0 + n], sqa[:, 3, 0:n], ALU.add)\
                        .then_inc(a_ssq, 1)

                for m in range(OUT_T):
                    for g in (0, 1):
                        add_squares("post_mix", g, m, 2 * m + g)
                for g in (0, 1):
                    for k in range(KT):
                        add_squares("pre_ffn", g, k, 8 * g + k)
                for m in range(KT):
                    for g in (0, 1):
                        add_squares("post_ffn", g, m, 2 * m + g)
                assert links[0] == POOL_LINKS, links[0]


IN_SPLITS = (512, 128, 128, 256, 256, 256, 256, 256, 256)


def in_columns():
    qa, ka, va, ub, vb, qc, kc, vc, gc = (int(v) for v in np.cumsum((0,) + IN_SPLITS[:-1]))
    half = lambda o, h: np.concatenate([o + HD * r + 32 * h + np.arange(32) for r in range(RET_HEADS)])
    run = lambda o, n: np.arange(o, o + n)
    pairs = [np.concatenate([qa + HD * j + np.arange(HD), qa + HD * (j + 4) + np.arange(HD)]) for j in range(4)]
    return np.concatenate([half(qc, 0), half(qc, 1), half(kc, 0), half(kc, 1), run(vc, 256), run(gc, 256),
                           run(vb, 256), run(ub, 256), run(ka, 128), run(va, 128)] + pairs)


def pair_rows():
    return np.concatenate([np.concatenate([HD * j + np.arange(HD), HD * (j + 4) + np.arange(HD)]) for j in range(4)])


def slots_of(w):
    k, n = w.shape
    return w.reshape(k // P, P, n // P, P).transpose(2, 1, 0, 3)


def constants():
    f = np.float32
    half = HD // 2
    inv = (f(10000.0) ** (-np.arange(half, dtype=f) / f(half))).astype(f)
    pos = np.concatenate([np.arange(SEQ), PAST + np.arange(DEC)]).astype(f)
    ang = (pos[:, None] * inv[None, :]).astype(f).astype(np.float64)
    cos, sin = (np.tile(t(ang).astype(f).T, (RET_HEADS, 1)) for t in (np.cos, np.sin))
    logg = np.log(1.0 - 2.0 ** (-5.0 - np.arange(RET_HEADS)))
    i = np.arange(P)
    of_row = np.repeat(np.arange(RET_HEADS), 32)
    xi = np.exp(logg[of_row][:, None] * (i + 1.0)[None, :])
    rel = i[None, :] - i[:, None]
    decay = np.where(rel[:, None, :] >= 0, np.exp(logg[None, :, None] * np.maximum(rel, 0)[:, None, :]), 0.0)
    zeta = lambda block: np.tile(np.exp(logg[of_row][None, :] * (block - 1.0 - i)[:, None]), (1, 2))
    blk = np.kron(np.eye(2), np.ones((HD, HD))) / HD
    cdec = np.exp(logg[of_row][:, None] * np.array([P, DEC], float)[None, :])
    parts = [cos, sin, cos * f(SCALE), sin * f(SCALE), xi, decay.reshape(P, -1), zeta(P),
             np.where(i[:, None] < DEC, zeta(DEC), 0.0), blk, cdec,
             of_row[:, None] == np.arange(RET_HEADS)[None, :]]
    return np.ascontiguousarray(np.concatenate([p.astype(f) for p in parts], axis=1))


def kernel(**inputs):
    import concourse.bacc as bacc
    from concourse.bass_utils import run_bass_kernel_spmd
    import ml_dtypes

    a = {k: np.asarray(v) for k, v in inputs.items()}
    f = np.float32
    to_tiles = lambda t: np.ascontiguousarray(t.reshape(t.shape[0], -1, P).transpose(2, 1, 0))
    xT = to_tiles(np.concatenate([a["x_prompt"][0], a["x_sample"][0]], axis=0))
    cols_in, rows_a = in_columns(), pair_rows()
    rows_out = np.concatenate([rows_a, np.arange(512, 1024)])
    wts = []
    for l in range(DEPTH):
        wts.append(slots_of(a["w_in"][l][:, cols_in]))
        wts.append(slots_of(a["w_out"][l][rows_out]))
        gu = np.stack([slots_of(a["w_gate"][l]), slots_of(a["w_up"][l])], axis=1)
        wts.append(gu.reshape((2 * FT,) + gu.shape[2:]))
        dn = slots_of(a["w_down"][l]).transpose(0, 2, 1, 3).reshape(-1, 8, P, P)
        wts.append(dn.transpose(0, 2, 1, 3))
    wts = np.ascontiguousarray(np.concatenate(wts, axis=0).reshape(DEPTH * SLOTS, P, 1024))

    col = lambda v: v.reshape(-1, P).T
    small = np.stack([np.concatenate([
        col(a["ln_pre_mix"][l]), col(a["ln_post_mix"][l]), col(a["ln_pre_ffn"][l]), col(a["ln_post_ffn"][l]),
        col(a["norm_a_g"][l][rows_a]), col(a["norm_b_g"][l]), col(a["ret_norm_g"][l]),
        np.broadcast_to(a["swa_sinks"][l].reshape(2, 4).T.reshape(1, 8), (P, 8))], axis=1) for l in range(DEPTH)])
    rows = lambda v: np.broadcast_to(v[None, :], (P, v.size))
    lpar = []
    for l in range(DEPTH):
        gb = np.repeat(a["gmlp_b"][l].reshape(2, 2, 1, P), HD, axis=2).transpose(1, 2, 0, 3).reshape(P, 2 * P)
        gw = np.ascontiguousarray(a["gmlp_w"][l].transpose(2, 0, 1))
        lpar.append(np.concatenate([rows(a["gmlp_ln_g"][l]), rows(a["gmlp_ln_b"][l]), gb, gw.reshape(P, 4 * P)], axis=1))
    lpar = np.stack(lpar)
    ck, cv = a["cache_swa_k"][0], a["cache_swa_v"][0]
    kcache = np.ascontiguousarray(ck.reshape(DEPTH, P, P).transpose(0, 2, 1))
    vcache = np.ascontiguousarray(cv.reshape(DEPTH, P, P))
    ret0 = np.ascontiguousarray(a["state_ret"][0].reshape(DEPTH, RET_HEADS, 2, 32, HD).transpose(0, 1, 3, 2, 4)
                                .reshape(DEPTH, P, 2, HD))
    q = np.arange(P) < CHUNK
    keys = np.arange(256)
    two = np.concatenate([np.stack([q, ~q]).astype(f), np.stack([keys >= 192, keys < 64]) * f(-1e30)], axis=1)
    mask = np.zeros((2, HD, P + 256), ml_dtypes.bfloat16)
    mask[:, 0:2] = two
    mask = mask.reshape(P, -1)

    arrays = dict(xT=xT, wts=wts, small=small, tabs=constants(), lpar=lpar, kcache=kcache, vcache=vcache, ret0=ret0,
                  ident=np.eye(P, dtype=f), mask=mask)
    outs = dict(x=(P, KT, T), k=(DEPTH, P, P + DEC), v=(DEPTH, P, P + DEC), rp=(DEPTH, P, 2, HD),
                rs=(DEPTH, P, 2, HD), gv=(DEPTH, DEC, 256))
    nc = bacc.Bacc("TRN2", target_bir_lowering=False, num_devices=1)
    arrays = {f"in_{n}": np.ascontiguousarray(v) for n, v in arrays.items()}
    args = [nc.dram_tensor(n, v.shape, mybir.dt.from_np(v.dtype), kind="ExternalInput").ap() for n, v in arrays.items()]
    args += [nc.dram_tensor(f"out_{n}", s, F32, kind="ExternalOutput").ap() for n, s in outs.items()]
    program(nc, *args)
    r = run_bass_kernel_spmd(nc, [arrays], core_ids=[0]).results[0]

    y = r["out_x"].transpose(2, 1, 0).reshape(T, D)
    kv = []
    for n in ("k", "v"):
        t = r[f"out_{n}"].transpose(0, 2, 1).reshape(DEPTH, P + DEC, KV_HEADS, HD)[None]
        kv += [t[:, :, :P], t[:, :, P:]]
    st = [r[f"out_{n}"].reshape(DEPTH, RET_HEADS, 32, 2, HD).transpose(0, 1, 3, 2, 4)
          .reshape(1, DEPTH, RET_HEADS, HD, HD) for n in ("rp", "rs")]
    return tuple(np.ascontiguousarray(t) for t in
                 (y[None, :SEQ], y[None, SEQ:], kv[0], kv[2], kv[1], kv[3], st[0], st[1], r["out_gv"][None]))
```

```python
from contextlib import ExitStack

import numpy as np
import concourse.bass as bass
from concourse import mybir
from concourse.alu_op_type import AluOpType as ALU

F32 = mybir.dt.float32
F32R = mybir.dt.float32r
BF16 = mybir.dt.bfloat16
ACT = mybir.ActivationFunctionType
AX = mybir.AxisListType
ds = bass.ds

P = 128
DEPTH = 2
D = 1024
SEQ = 512
DEC = 64
PAST = 256
T = SEQ + DEC
HD = 64
KT = D // P
D_FF = ((8 * D + 3 * 256 - 1) // (3 * 256)) * 256
FT = D_FF // P
EPS = 1e-6
SCALE = HD ** -0.5
SWA_HEADS, KV_HEADS = 8, 2
RET_HEADS = 4
CHUNK = 64

GROUPS = ((0, 256), (256, T))
GW = max(b - a for a, b in GROUPS)
TB = [(0, 128), (128, 128), (256, 128), (384, 128), (512, 64)]
NB = len(TB)
GROUP_BLOCKS = ((0, 1), (2, 3, 4))

IN_QA, IN_QB, IN_KA, IN_KB, IN_V0, IN_V1, IN_G0, IN_G1, IN_VB0, IN_VB1, IN_UB0, IN_UB1, IN_K, IN_V, IN_Q0 = range(15)
IN_T = 18
OUT_T = KT
S_IN, S_OUT, S_GU, S_DN = 0, IN_T, IN_T + OUT_T, IN_T + OUT_T + 2 * FT
SLOTS = S_DN + KT * FT // 8
RING, RAW = 4, 2
assert SLOTS % RING == 0 and SLOTS % RAW == 0 and (KT * FT) % 8 == 0

TILES = IN_T + OUT_T + 2 * FT + KT
V_IN, V_GU, V_TOOK = 0, 2 * IN_T, 2 * IN_T + 4 * FT
A_OUT, A_DN, A_TOOK = 0, 2 * OUT_T, 2 * OUT_T + 2 * KT
HEAD = 4
HEAD_BANKS = ((0, 2, 6, 7), (1, 3, 5, 6))
K_OUT = (4, 5, 6, 7, 0, 1, 2, 3)


def order(tile, g):
    return HEAD * g + tile if tile < HEAD else 2 * tile + g


def square_order(head, late):
    post = sorted(((order(m, g) if head else 2 * m + g, "post", g, m) for m in range(KT) for g in (0, 1)))
    post = [s[1:] for s in post]
    pre = [("pre", g, k) for g in (0, 1) for k in range(KT)]
    return post[:-1] + pre[:late] + post[-1:] + pre[late:]


LATE = dict(mix=0, ffn=4)
SQUARES = dict(mix=square_order(True, LATE["mix"]), ffn=square_order(False, LATE["ffn"]))
SQ = dict(start=0, mix=2 * KT, ffn=6 * KT)
SQS = 8 * KT
ST = dict(pre_mix=0, b=2, a=4, post_mix=6, pre_ffn=8, post_ffn=10)
STS = 12
HR = dict(pre_mix=0, merged=16, pre_ffn=32, next_mix=48)
HRS = 48


def square_at(part, kind, g, k):
    return SQ[part] + SQUARES[part].index((kind, g, k))


SP = dict(pre_mix=0, next_mix=8, post_mix=16, pre_ffn=24, post_ffn=32, na=40, nb=44, rg=46, sink=48)
SP_N = 56
TAB = {}
_n = 0
for _name, _w in (("cos", T), ("sin", T), ("cosk", T), ("sink", T), ("xi", P), ("decay", 4 * P),
                  ("zeta", 2 * P), ("zetas", 2 * P), ("blk", P), ("cdec", 2), ("head", RET_HEADS)):
    TAB[_name] = _n
    _n += _w
TAB_N = _n
LP = {}
_n = 0
for _name, _w in (("lng", 256), ("lnb", 256), ("gb", 256), ("gw", 512)):
    LP[_name] = _n
    _n += _w
LP_N = _n

KC = SEQ + 128 + DEC
WINDOW = [(0, 128), (0, 256), (128, 256), (256, 256), (512, 192)]
VTILES = [(0,), (0, 1), (1, 2), (2, 3), (4, 5)]
NOUT = 13
DN_FREE = sum((8 * i + 7) % FT != FT - 1 for i in range(SLOTS - S_DN))
DVE_LINKS = 128
POOL_LINKS = 14
B_AT, A_AT = 1, 15
MERGED = ([(g, k) for g in (0, 1) for k in (4, 5, 6, 7)] + [(g, k) for g in (0, 1) for k in (0, 1, 2, 3)])
MERGED_AT = {2: (0, 1), 3: (2, 3), 4: (4, 5), 5: (6, 7), A_AT + 1: (8, 9), A_AT + 2: (10, 11)}
S_LAST = S_DN + (KT - 1) * FT // 8
SPLITS_AT = {0: (S_LAST,), 2: (S_LAST + 1,)}
assert SLOTS - S_LAST == 3
UNITS = NB * 4


def program(nc, xT, wts, small, tabs, lpar, kcache, vcache, ret0, ident_d, mask_d,
            o_x, o_k, o_v, o_rp, o_rs, o_gv):
    with ExitStack() as ctx:
        sem = lambda name: ctx.enter_context(nc.semaphore(name))

        base = (nc.sbuf_base + 63) // 64 * 64
        at = [base]

        def place(name, shape, dt=F32, offset=None):
            size = int(np.prod(shape[1:])) * (2 if dt == BF16 else 4)
            size = (size + 31) // 32 * 32
            o = at[0] if offset is None else offset
            t = nc.alloc_sbuf_tensor_at(name, shape, dt, offset=o)
            if offset is None:
                at[0] += size
            assert o + size <= nc.sbuf_usable_end, (name, o + size, nc.sbuf_usable_end)
            return t

        x = place("x", [P, KT, T])
        h_hi = place("h_hi", [P, KT, T], F32R)
        h_lo_at = at[0]
        h_lo = place("h_lo", [P, KT, T], F32R)
        raw = place("raw", [P, RAW, 1024])
        w_hi = place("w_hi", [P, RING, 1024], F32R)
        w_lo = place("w_lo", [P, RING, 1024], F32R)
        sp = place("sp", [P, SP_N])
        ident = place("ident", [P, P])
        ones = place("ones", [P, P])
        mask = place("mask", [P, P + 256], BF16)
        epsc = place("epsc", [P, 1])
        acc = place("acc", [P, T])
        rstd = place("rstd", [P, T])
        sq = place("sq", [P, 2, GW])
        tp = place("tp", [P, 2, GW])
        st_p = place("st_p", [P, 2, 256])
        bst = place("bst", [P, NB, 6])
        bmv = place("bmv", [P, NB, 2])
        brs = place("brs", [P, NB])
        nsink = place("nsink", [P, 8])
        mx = place("mx", [P, 2, 2])
        nm = place("nm", [P, 2, 2])
        sm = place("sm", [P, 2, 2])
        es = place("es", [P, 2, 2])
        den = place("den", [P, 2, 2])
        rd = place("rd", [P, 2, 2])
        region = at[0]
        hid_hi = place("hid_hi", [P, FT, T], F32R)
        hid_lo_at = at[0]
        hid_lo = place("hid_lo", [P, FT, T], F32R)
        region_end = at[0]
        at[0] = region
        ret = place("ret", [P, 6, T])
        rtmp = place("rtmp", [P, 2, T])
        qxi = place("qxi", [P, 2, T])
        vtok = place("vtok", [P, NB, 256])
        kz = place("kz", [P, 2, 256])
        inner = place("inner", [P, 2, 4, P])
        zone2 = at[0]
        at[0] = region
        prob = place("prob", [P, 4, 2, 256])
        probT = place("probT", [P, 4, 2, 2, P])
        sqa = place("sqa", [P, 4, P])
        assert at[0] <= zone2
        y_mix = place("y_mix", [P, KT, T], offset=region)
        h_whole = place("h_whole", [P, KT, T], offset=h_lo_at)
        gate_whole = place("gate_whole", [P, FT, T], offset=region)
        hid_whole = place("hid_whole", [P, FT, T], offset=hid_lo_at)
        y_ffn = place("y_ffn", [P, KT, T], offset=h_lo_at)
        at[0] = zone2
        sg = place("sg", [P, 2, T])
        gv = place("gv", [P, 2, T])
        ub = place("ub", [P, 2, T])
        rT = place("rT", [P, 2, T])
        rsq = place("rsq", [P, 2, T])
        gvt_at = at[0]
        gvt = place("gvt", [P, NB, 256])
        ptmp = place("ptmp", [P, 2, T], offset=gvt_at)
        kk = place("kk", [P, KC])
        vv = place("vv", [P, T])
        vk = place("vk", [P, 6, P])
        qm = place("qm", [P, 2, 2, RET_HEADS, P], offset=at[0])
        qq = place("qq", [P, 4, T])
        st_s = place("st_s", [P, 2, 256])
        tab_at = at[0]
        tab = place("tab", [P, TAB_N])
        lp = place("lp", [P, LP_N])
        aT = place("aT", [P, 4, T], offset=tab_at)
        assert max(at[0], region_end) <= nc.sbuf_usable_end

        psum = ctx.enter_context(nc.psum_tensor("psum", [P, 8, 512], F32))
        banks = [psum[:, i, :] for i in range(8)]

        def out_bank(parity, g):
            a, b = GROUPS[g]
            return banks[2 * parity + g][:, 0:b - a]

        def head_bank(t, g):
            a, b = GROUPS[g]
            return banks[HEAD_BANKS[g][t]][:, 0:b - a]

        def tile_bank(t, g):
            return head_bank(t, g) if t < HEAD else out_bank(t % 2, g)

        x_landed = [sem(f"x_landed{i}") for i in range(4)]
        const_landed = sem("const_landed")
        ones_set = sem("ones_set")
        small_landed = sem("small_landed")
        tab_landed = sem("tab_landed")
        cache_landed = sem("cache_landed")
        raw_landed = [sem(f"raw_landed{i}") for i in range(RAW)]
        hi_made = sem("hi_made")
        lo_made = sem("lo_made")
        dn_free = sem("dn_free")
        tile_done = sem("tile_done")
        act_took = sem("act_took")
        dve_took = sem("dve_took")
        sq_ready = sem("sq_ready")
        sq_added = sem("sq_added")
        stat_done = sem("stat_done")
        std_ready = sem("std_ready")
        x_ready = sem("x_ready")
        prod_ready = sem("prod_ready")
        hhi_ready = sem("hhi_ready")
        h_ready = sem("h_ready")
        curved = sem("curved")
        silu_ready = sem("silu_ready")
        hid_prod = sem("hid_prod")
        hid_hi_ready = sem("hid_hi_ready")
        hid_ready = sem("hid_ready")
        rotq_ready = sem("rotq_ready")
        rotk_ready = sem("rotk_ready")
        qm_ready = sem("qm_ready")
        rk_done = sem("rk_done")
        rv_done = sem("rv_done")
        vtok_ready = sem("vtok_ready")
        kz_ready = sem("kz_ready")
        rs_done = sem("rs_done")
        inner_ready = sem("inner_ready")
        ro_done = sem("ro_done")
        ro_taken = sem("ro_taken")
        state_ready = sem("state_ready")
        gn_mean = sem("gn_mean")
        gn_cent = sem("gn_cent")
        gn_sq = sem("gn_sq")
        gn_var = sem("gn_var")
        gn_std = sem("gn_std")
        c_ready = sem("c_ready")
        gt_done = sem("gt_done")
        gt_taken = sem("gt_taken")
        bn_ready = sem("bn_ready")
        ln_std = sem("ln_std")
        gvt_ready = sem("gvt_ready")
        mixed_done = sem("mixed_done")
        b_ready = sem("b_ready")
        b_ssq = sem("b_ssq")
        nsink_ready = sem("nsink_ready")
        vk_done = sem("vk_done")
        vk_ready = sem("vk_ready")
        s_done = sem("s_done")
        nm_ready = sem("nm_ready")
        p_ready = sem("p_ready")
        pn_ready = sem("pn_ready")
        pt_done = sem("pt_done")
        pt_ready = sem("pt_ready")
        o_done = sem("o_done")
        a_taken = sem("a_taken")
        a_ssq = sem("a_ssq")

        dve_chain = sem("dve_chain")
        pool_chain = sem("pool_chain")
        out_landed = sem("out_landed")
        y_landed = sem("y_landed")
        pe_passed, dve_passed, pool_passed = sem("pe_passed"), sem("dve_passed"), sem("pool_passed")

        block = ctx.enter_context(nc.Block())

        def cols(g):
            return slice(*GROUPS[g])

        def width(g):
            return GROUPS[g][1] - GROUPS[g][0]

        def slot_used(l, s):
            for first, count in ((S_IN, IN_T), (S_OUT, OUT_T), (S_GU, 2 * FT)):
                if first <= s < first + count:
                    return tile_done, l * (2 * TILES) + (2 + 2 * first + order(s - first, 1))
            last = 8 * (s - S_DN) + 7
            if last % FT == FT - 1:
                return tile_done, l * (2 * TILES) + (1 + 2 * (TILES - KT) + 2 * (last // FT + 1))
            before = sum((8 * i + 7) % FT != FT - 1 for i in range(s - S_DN + 1))
            return dn_free, l * DN_FREE + before

        def seg(g):
            if g == 0:
                return [(slice(0, 256), slice(0, 256))]
            return [(slice(0, 256), slice(256, 512)), (slice(256, GW), slice(KC - DEC, KC))]

        def score_bank(u, hh):
            return banks[2 * (u % 2) + hh]

        def grid(b, bank, w):
            return bank.rearrange("p (i n) -> p i n", n=P)[:, 0:w, 0:TB[b][1]]

        @block.sync
        def _(spe):
            for g in (0, 1):
                spe.dma_start(raw[:, g, :], wts[g]).then_inc(raw_landed[g], 16)
                for i in (0, 1):
                    ks = slice(i * KT // 2, (i + 1) * KT // 2)
                    spe.dma_start(x[:, ks, cols(g)], xT[:, ks, cols(g)]).then_inc(x_landed[2 * g + i], 16)
            with spe.Fori(1, DEPTH * SLOTS // RAW) as i:
                for r in range(RAW):
                    spe.wait_ge(lo_made, i * RAW + (r - RAW + 1))
                    spe.dma_start(raw[:, r, :], wts[ds(i * RAW + r, 1)].rearrange("o p n -> (o p) n"))\
                       .then_inc(raw_landed[r], 16)
            for r in range(RAW):
                spe.wait_ge(raw_landed[r], DEPTH * SLOTS // RAW * 16)
                spe.sem_inc(raw_landed[r], RING // RAW * 16)
            for g in (0, 1):
                for i in (0, 1):
                    ks = slice(i * KT // 2, (i + 1) * KT // 2)
                    spe.wait_ge(x_ready, (DEPTH - 1) * 32 + 1 + 16 + KT * g + KT // 2 * (i + 1))
                    spe.dma_start(o_x[:, ks, cols(g)], x[:, ks, cols(g)]).then_inc(y_landed, 16)
            spe.wait_ge(y_landed, 4 * 16)
            spe.wait_ge(out_landed, DEPTH * 16 * NOUT)

        @block.tensor
        def _(pe):
            pe.sem_inc(act_took, 1)
            pe.sem_inc(dve_took, 1)
            pe.sem_inc(tile_done, 1)
            pe.sem_inc(stat_done, 1)
            pe.wait_ge(const_landed, 32)
            pe.wait_ge(ones_set, 1)
            with pe.Fori(0, DEPTH) as l:

                def L(n, per):
                    return l * per + n

                def alone(s, v):
                    pe.wait_ge(s, v)
                    pe.sem_inc(pe_passed, 1)

                def three(out, ring, j, rhs_k, g, first, last, hi=h_hi, lo=h_lo):
                    wh, wl = w_hi[:, ring, j * P:(j + 1) * P], w_lo[:, ring, j * P:(j + 1) * P]
                    pe.matmul(out, wh, hi[:, rhs_k, cols(g)], start=first, stop=False)
                    pe.matmul(out, wh, lo[:, rhs_k, cols(g)], start=False, stop=False)
                    return pe.matmul(out, wl, hi[:, rhs_k, cols(g)], start=False, stop=last)

                def stat(n, g, src, bank, waits):
                    for s, v in waits:
                        pe.wait_ge(s, v)
                    pe.matmul(banks[bank][:, 0:width(g)], ones[:, :], src[:, cols(g)],
                              start=True, stop=True).then_inc(stat_done, 1)

                def head(name, first, base, took, per, wait0, operand, group1, ks=range(KT), between=None):
                    slot = lambda t: L(first + t, SLOTS)

                    def free(t, g):
                        if g == 0:
                            return wait0 if t == 0 else None
                        return (took, 1 + L(base + order(2, 0) + 1, per)) if t == 3 else None

                    def ring_run(tiles, g, op, kk_):
                        for t in tiles:
                            if g == 0:
                                pe.wait_ge(lo_made, slot(t) + 1)
                            if free(t, g) is not None:
                                pe.wait_ge(*free(t, g))
                        for n, k in enumerate(ks):
                            if op is not None and n >= kk_:
                                pe.wait_ge(h_ready, op + (n - kk_ + 1))
                            for t in tiles:
                                mm = three(head_bank(t, g), (first + t) % RING, k, k, g, n == 0, n == KT - 1)
                                if n == KT - 1:
                                    mm.then_inc(tile_done, 1)

                    late = 4 if ks is K_OUT else 0
                    ring_run((0, 1), 0, operand, late)
                    between(0)
                    ring_run((2, 3), 0, None, 0)
                    between(1)
                    ring_run((0, 1), 1, group1, late)
                    between(2)
                    ring_run((2,), 1, None, 0)
                    ring_run((3,), 1, None, 0)

                def tile(first, base, t, took, per, ks=range(KT), middle=None):
                    pe.wait_ge(lo_made, L(first + t + 1, SLOTS))
                    for g in (0, 1):
                        pe.wait_ge(took, 1 + L(base + order(t - 2, g) + 1, per) if t >= HEAD + 2 else
                                   1 + L(base + order(t - HEAD, g) + 1, per))
                        for n, k in enumerate(ks):
                            mm = three(out_bank(t % 2, g), (first + t) % RING, k, k, g, n == 0, n == KT - 1)
                            if g == 1 and n == 4 and middle is not None:
                                middle()
                        mm.then_inc(tile_done, 1)

                def post_stat(name, part, g):
                    stat(ST[name] + g, g, acc, 4 + g, [(sq_added, 1 + L(square_at(part, "post", g, KT - 1) + 1, SQS))])

                def pre_stat(name, count, g):
                    stat(ST[name] + g, g, acc, 4, [(sq_added, 1 + count),
                                                   (std_ready, 1 + L(ST[name] + g, STS))])

                def ret_in(b):
                    t0, n = TB[b]
                    if b == 0:
                        pe.wait_ge(dve_took, 1 + L(2 * (IN_V1 + 1), V_TOOK))
                        alone(rotk_ready, L(1, 1))
                    else:
                        pe.wait_ge(vtok_ready, L(b, NB))
                        alone(kz_ready, L(b, NB))
                    for bank, row, done in ((5, 2, rk_done), (4, 4, rv_done)):
                        for i in (0, 1):
                            mm = pe.transpose(banks[bank][0:n, i * P:(i + 1) * P], ret[:, row + i, t0:t0 + n],
                                              ident[:, :])
                        mm.then_inc(done, 1)
                    if b:
                        pe.wait_ge(inner_ready, L(b, NB))
                    alone(qm_ready, L(b + 1, NB))
                    for half in (0, 1):
                        mm = pe.matmul(banks[6][0:n, 0:RET_HEADS * P].rearrange("p (h n) -> p h n", n=P)[:, :, 0:n],
                                       ret[:, 2 + half, t0:t0 + n], qm[:, b % 2, half, :, 0:n],
                                       start=half == 0, stop=half == 1)
                    mm.then_inc(rs_done, 1)

                def ret_out(b):
                    t0, n = TB[b]
                    pe.wait_ge(vtok_ready, L(b + 1, NB))
                    pe.wait_ge(kz_ready, L(b + 1, NB))
                    if b > 0:
                        pe.wait_ge(ro_taken, L(b, NB))
                        pe.wait_ge(state_ready, L(b, NB))
                    if b == NB - 1:
                        pe.wait_ge(cache_landed, L(1, 1) * 96)
                    alone(inner_ready, L(b + 1, NB))
                    state = None if b == 0 else st_s if b == NB - 1 else st_p
                    for hh in range(RET_HEADS):
                        c = P * (hh // 2)
                        out = banks[7][64 * (hh % 2):64 * (hh % 2) + 64, c:c + n]
                        e = slice(hh * HD, (hh + 1) * HD)
                        pe.matmul(out, vtok[0:n, b, e], inner[0:n, b % 2, hh, 0:n], start=True, stop=state is None)
                        if state is not None:
                            for half in (0, 1):
                                pe.matmul(out, state[:, half, e], qxi[:, half, t0:t0 + n], start=False, stop=half == 1)
                    for hh in range(RET_HEADS):
                        for half in (0, 1):
                            c = 2 * P + half * HD
                            mm = pe.matmul(banks[7][32 * hh:32 * hh + 32, c:c + HD],
                                           kz[0:n, b % 2, half * P + 32 * hh:half * P + 32 * hh + 32],
                                           vtok[0:n, b, hh * HD:(hh + 1) * HD], start=True, stop=True,
                                           tile_position=(0, 32 * hh))
                    mm.then_inc(ro_done, 1)

                def gn(i, var):
                    c, g = i // 2, i % 2
                    a, b_ = GROUPS[g]
                    bank = banks[4 + i][:, 0:b_ - a]
                    if not var:
                        pe.wait_ge(state_ready, L(NB, NB))
                    else:
                        pe.wait_ge(gn_sq, L(i + 1, 4))
                    pe.matmul(bank, tab[:, TAB["blk"]:TAB["blk"] + P], (rsq if var else rT)[:, c, a:b_],
                              start=True, stop=True).then_inc(gn_var if var else gn_mean, 1)

                def gm_in(b):
                    t0, n = TB[b]
                    if b == 0:
                        alone(curved, L(8, 12))
                    if b < 4:
                        alone(gn_std, L(b + 1, 4))
                    else:
                        alone(gt_taken, L(b - 3, NB))
                    for i in (0, 1):
                        mm = pe.transpose(banks[4 + b % 4][0:n, i * P:(i + 1) * P], gv[:, i, t0:t0 + n], ident[:, :])
                    mm.then_inc(gt_done, 1)

                def gm_mix(b):
                    t0, n = TB[b]
                    if b == 4:
                        pe.wait_ge(b_ready, L(1, NB))
                    alone(gvt_ready, L(b + 1, NB))
                    for g4 in range(4):
                        mm = pe.matmul(banks[4 + b % 4][64 * (g4 % 2):64 * (g4 % 2) + 64,
                                                        (g4 // 2) * P:(g4 // 2) * P + n],
                                       gvt[0:n, b, g4 * HD:(g4 + 1) * HD],
                                       lp[0:n, LP["gw"] + g4 * P:LP["gw"] + g4 * P + n], start=True, stop=True)
                    mm.then_inc(mixed_done, 1)

                def v_tokens():
                    alone(b_ready, L(NB, NB))
                    for b in range(4):
                        mm = pe.transpose(banks[4][:, b * P:(b + 1) * P], vv[:, b * P:(b + 1) * P], ident[:, :])
                    mm.then_inc(vk_done, 1)
                    pe.transpose(banks[5][0:DEC, 0:P], vv[:, SEQ:T], ident[:, :]).then_inc(vk_done, 1)

                fill = {i: [] for i in range(IN_T)}
                for b in range(NB):
                    fill[6 + b].append(lambda b=b: ret_in(b))
                    fill[7 + b].insert(0, lambda b=b: ret_out(b))
                    fill[14].append(lambda b=b: gm_in(b))
                    fill[15].append(lambda b=b: gm_mix(b))
                fill[12].append(lambda: [gn(i, False) for i in range(4)])
                fill[13].append(lambda: [gn(i, True) for i in range(4)])
                fill[17].append(v_tokens)

                def between(n):
                    if n in (1, 2):
                        g = n - 1
                        pre_stat("pre_mix", L(SQ["start"] + 8 * (g + 1), SQS), g)

                head("in", S_IN, V_IN, dve_took, V_TOOK, (act_took, 1 + L(0, A_TOOK)), 1 + L(HR["pre_mix"], HRS),
                     1 + L(HR["pre_mix"] + 8, HRS), between=between)
                for i in range(HEAD, IN_T):
                    tile(S_IN, V_IN, i, dve_took, V_TOOK)
                    for f in fill[i]:
                        f()

                def scores(u):
                    b, j = divmod(u, 4)
                    t0, n = TB[b]
                    k0, kn = WINDOW[b]
                    if u == 0:
                        alone(dve_took, 1 + L(2 * IN_T, V_TOOK))
                    elif u >= 2:
                        alone(p_ready, L(u - 1, UNITS))
                    if b == NB - 1 and j == 0:
                        alone(cache_landed, L(1, 1) * 96)
                    for hh in (0, 1):
                        out = score_bank(u, hh)[0:n, 0:kn]
                        r = slice(64 * hh, 64 * hh + 64)
                        masked = b < NB - 1
                        if masked:
                            pe.matmul(out, mask[r, 0:P], mask[r, P + 256 - kn:P + 256], start=True, stop=False)
                        mm = pe.matmul(out, qq[r, j, t0:t0 + n], kk[r, k0:k0 + kn], start=not masked, stop=True)
                    mm.then_inc(s_done, 1)

                def turn(u):
                    b, j = divmod(u, 4)
                    t0, n = TB[b]
                    kn = WINDOW[b][1]
                    if u >= 2:
                        pe.wait_ge(pt_ready, L(u - 1, UNITS))
                    elif u == 0:
                        pe.wait_ge(vk_ready, L(2, 2))
                    alone(pn_ready, L(u + 1, UNITS))
                    for hh in (0, 1):
                        for kt in range((kn + P - 1) // P):
                            w = min(P, kn - kt * P)
                            mm = pe.transpose(banks[4 + u % 2][0:w, (hh * 2 + kt) * P:(hh * 2 + kt) * P + n],
                                              prob[0:n, u % 4, hh, kt * P:kt * P + w], ident[0:n, 0:n])
                    mm.then_inc(pt_done, 1)

                def values(u):
                    b, j = divmod(u, 4)
                    t0, n = TB[b]
                    kn = WINDOW[b][1]
                    if j == 0:
                        if b >= 2:
                            pe.wait_ge(a_taken, L(b - 1, NB))
                        if b == 0:
                            pe.wait_ge(ro_taken, L(NB, NB))
                            pe.wait_ge(state_ready, L(NB, NB))
                            pe.wait_ge(b_ready, L(NB, NB))
                            pe.wait_ge(std_ready, 1 + L(ST["b"] + 2, STS))
                        if b == 3:
                            pe.wait_ge(std_ready, 1 + L(ST["a"] + 1, STS))
                    alone(pt_ready, L(u + 1, UNITS))
                    for hh in (0, 1):
                        for kt in range((kn + P - 1) // P):
                            w = min(P, kn - kt * P)
                            mm = pe.matmul(banks[6 + b % 2][64 * hh:64 * hh + 64, j * P:j * P + n],
                                           vk[0:w, VTILES[b][kt], 64 * hh:64 * hh + 64],
                                           probT[0:w, u % 4, hh, kt, 0:n], start=kt == 0,
                                           stop=kt == (kn + P - 1) // P - 1, tile_position=(0, 64 * hh))
                    mm.then_inc(o_done, 1)

                for u in range(UNITS + 5):
                    if u < UNITS:
                        scores(u)
                    if 3 <= u < UNITS + 3:
                        turn(u - 3)
                    if u >= 5:
                        values(u - 5)
                    if u == B_AT:
                        for g in (0, 1):
                            stat(ST["b"] + g, g, rsq[:, 0, :], 6 + g, [(b_ssq, L(1, 1))])
                    if u == A_AT:
                        stat(ST["a"], 0, acc, 7, [(a_ssq, L(2, NB))])

                def between(n):
                    if n == 0:
                        stat(ST["a"] + 1, 1, acc, 4, [(a_ssq, L(NB, NB)), (pt_ready, L(UNITS, UNITS))])

                pe.wait_ge(p_ready, L(UNITS, UNITS))
                pe.wait_ge(nm_ready, L(UNITS, UNITS))
                pe.wait_ge(a_taken, L(NB, NB))
                head("out", S_OUT, A_OUT, act_took, A_TOOK, (h_ready, 1 + L(HR["merged"] + 12, HRS)), None,
                     1 + L(HR["merged"] + 12, HRS), ks=K_OUT, between=between)
                for m in range(HEAD, OUT_T):
                    tile(S_OUT, A_OUT, m, act_took, A_TOOK, ks=K_OUT,
                         middle=(lambda: post_stat("post_mix", "mix", 0)) if m == OUT_T - 1 else None)
                post_stat("post_mix", "mix", 1)

                def between(n):
                    if n in (1, 2):
                        pre_stat("pre_ffn", L(square_at("mix", "pre", n - 1, KT - 1) + 1, SQS), n - 1)

                head("gate", S_GU, V_GU, dve_took, V_TOOK, (act_took, 1 + L(A_DN, A_TOOK)),
                     1 + L(HR["pre_ffn"], HRS), 1 + L(HR["pre_ffn"] + 8, HRS), between=between)
                for t in (4, 5, 6, 7):
                    tile(S_GU, V_GU, t, dve_took, V_TOOK)
                with pe.Fori(0, FT // 2 - 2) as it:
                    for t in (8, 9, 10, 11):
                        pe.wait_ge(lo_made, L(S_GU + t + 1, SLOTS) + it * 4)
                        for g in (0, 1):
                            pe.wait_ge(dve_took, 1 + L(V_GU + order(t - 2, g) + 1, V_TOOK) + it * 8)
                            for k in range(KT):
                                mm = three(out_bank(t % 2, g), (S_GU + t) % RING, k, k, g, k == 0, k == KT - 1)
                            mm.then_inc(tile_done, 1)

                pe.wait_ge(hid_ready, L(2 * FT, 2 * FT))
                pe.wait_ge(dve_took, 1 + L(V_TOOK, V_TOOK))

                def down(m, k, g):
                    f = m * FT + k
                    s = S_DN + f // 8
                    if f % 8 == 0 and (g == 0 or m == KT - 1):
                        pe.wait_ge(lo_made, L(s + 1, SLOTS))
                    if k == 0 and m >= 2:
                        pe.wait_ge(act_took, 1 + L(A_DN + 2 * (m - 2) + g + 1, A_TOOK))
                    mm = three(out_bank(m % 2, g), s % RING, f % 8, k, g, k == 0, k == FT - 1, hid_hi, hid_lo)
                    if k == FT - 1:
                        mm.then_inc(tile_done, 1)
                    elif f % 8 == 7 and g == 1:
                        mm.then_inc(dn_free, 1)

                for m in range(KT - 1):
                    for k in range(FT):
                        for g in (0, 1):
                            down(m, k, g)
                for g in (0, 1):
                    for k in range(FT):
                        down(KT - 1, k, g)
                        if g == 1 and k == FT // 4:
                            post_stat("post_ffn", "ffn", 0)
                post_stat("post_ffn", "ffn", 1)

        @block.scalar
        def _(act):
            def fn(out, in_, f, **kw):
                return act.activation(out, in_, f, **kw)

            act.sem_inc(std_ready, 1)

            def split(s, off=0, l=0):
                r = s % RAW
                act.wait_ge(raw_landed[r], (l * (SLOTS // RAW) + (s // RAW + 1) + off // RAW) * 16)
                fn(w_hi[:, s % RING, :], raw[:, r, :], ACT.Copy).then_inc(hi_made, 1)

            def root(n, g, out, bank, count):
                act.wait_ge(stat_done, 2 + n)
                fn(out[:, cols(g)], banks[bank][:, 0:width(g)], ACT.Sqrt, bias=epsc[:, 0:1],
                   scale=1.0 / count).then_inc(std_ready, 1)

            def hi_of_x(g, k, name):
                c = SP[name] + k
                fn(h_hi[:, k, cols(g)], x[:, k, cols(g)], ACT.Copy, scale=sp[:, c:c + 1]).then_inc(hhi_ready, 1)

            act.wait_ge(ones_set, 1)
            act.wait_ge(small_landed, 16)
            for g in (0, 1):
                split(g)
                for k in range(KT):
                    if k % 4 == 0:
                        act.wait_ge(x_landed[2 * g + k // 4], 16)
                    i = 8 * g + k
                    act.wait_ge(sq_added, 1 + max(i - 1, 0))
                    fn(sq[:, i % 2, 0:width(g)], x[:, k, cols(g)], ACT.Square).then_inc(sq_ready, 1)
                    hi_of_x(g, k, "pre_mix")
            for s in range(2, RING):
                split(s)
            with act.Fori(0, DEPTH) as l:

                def L(n, per):
                    return l * per + n

                def square_of(part, kind, g, k, src):
                    i = square_at(part, kind, g, k)
                    act.wait_ge(sq_added, 1 + L(i - 1, SQS))
                    fn(sq[:, i % 2, 0:width(g)], src, ACT.Square).then_inc(sq_ready, 1)

                def take_y(part, m, g, count, bank, y, name):
                    act.wait_ge(tile_done, 1 + L(count, 2 * TILES))
                    square_of(part, "post", g, m, bank)
                    c = SP[name] + m
                    fn(y[:, m, cols(g)], bank, ACT.Copy, scale=sp[:, c:c + 1]).then_inc(act_took, 1)

                def next_norm(part, post, pre, base, take_last, at):
                    late = LATE[part]
                    for g in (0, 1):
                        for k in range(KT):
                            i = 8 * g + k
                            for s in at.get(i, ()):
                                act.wait_ge(*slot_used(l, s))
                                split(s + RING, l=l)
                            if i == late:
                                take_last()
                            if i == late + 2:
                                root(L(ST[post] + 1, STS), 1, rstd, 5, D)
                            act.wait_ge(x_ready, 1 + L(base + i + 1, 32))
                            square_of(part, "pre", g, k, x[:, k, cols(g)])
                            hi_of_x(g, k, pre)

                root(L(ST["pre_mix"], STS), 0, rstd, 4, D)
                root(L(ST["pre_mix"] + 1, STS), 1, rstd, 4, D)

                def vtok_copy(b):
                    n = TB[b][1]
                    act.wait_ge(rv_done, L(b + 1, NB))
                    fn(vtok[0:n, b, :], banks[4][0:n, 0:256], ACT.Copy).then_inc(vtok_ready, 1)

                def gt_copy(b):
                    n = TB[b][1]
                    act.wait_ge(gt_done, L(b + 1, NB))
                    fn(gvt[0:n, b, :], banks[4 + b % 4][0:n, 0:256], ACT.Copy)\
                        .then_inc(gt_taken, 1)

                def gn_square(i):
                    c, g = i // 2, i % 2
                    act.wait_ge(gn_cent, L(i + 1, 4))
                    fn(rsq[:, c, cols(g)], rT[:, c, cols(g)], ACT.Square).then_inc(gn_sq, 1)

                def gn_root(i):
                    c, g = i // 2, i % 2
                    act.wait_ge(gn_var, L(i + 1, 4))
                    fn(rsq[:, c, cols(g)], banks[4 + i][:, 0:width(g)], ACT.Sqrt, bias=epsc[:, 0:1])\
                        .then_inc(gn_std, 1)

                def ln_root():
                    act.wait_ge(bn_ready, L(NB, NB))
                    n = TB[-1][1]
                    fn(brs[:, 0:NB - 1], bmv[:, 0:NB - 1, 1], ACT.Sqrt, bias=epsc[:, 0:1])
                    fn(brs[0:n, NB - 1:NB], bmv[0:n, NB - 1:NB, 1], ACT.Sqrt, bias=epsc[0:n, 0:1])\
                        .then_inc(ln_std, 1)

                def vk_copy():
                    act.wait_ge(vk_done, L(1, 2))
                    fn(vk[:, 0:4, :], banks[4][:, :].rearrange("p (i n) -> p i n", n=P), ACT.Copy)\
                        .then_inc(vk_ready, 1)
                    act.wait_ge(vk_done, L(2, 2))
                    fn(vk[0:DEC, 5, :], banks[5][0:DEC, 0:P], ACT.Copy).then_inc(vk_ready, 1)

                more = {i: [] for i in range(IN_T)}
                for b in range(NB):
                    more[6 + b].append(lambda b=b: vtok_copy(b))
                    more[14].append(lambda b=b: gt_copy(b))
                for i in range(4):
                    more[12].append(lambda i=i: gn_square(i))
                    more[13].append(lambda i=i: gn_root(i))
                more[14].append(ln_root)
                more[17].append(vk_copy)

                for i in range(IN_T):
                    act.wait_ge(*slot_used(l, S_IN + i))
                    split(S_IN + i + RING, l=l)
                    if IN_G0 <= i <= IN_UB1:
                        t, f = ((sg, ACT.Silu) if i <= IN_G1 else (gv, ACT.Gelu_apprx_tanh) if i <= IN_VB1 else
                                (ub, ACT.Gelu_apprx_tanh))
                        for g in (0, 1):
                            act.wait_ge(dve_took, 1 + L(2 * i + g + 1, V_TOOK))
                            fn(t[:, i % 2, cols(g)], t[:, i % 2, cols(g)], f).then_inc(curved, 1)
                    for f in more[i]:
                        f()

                def exps(u):
                    b, j = divmod(u, 4)
                    n, kn = TB[b][1], WINDOW[b][1]
                    act.wait_ge(nm_ready, L(u + 1, UNITS))
                    for hh in (0, 1):
                        fn(prob[0:n, u % 4, hh, 0:kn], score_bank(u, hh)[0:n, 0:kn], ACT.Exp,
                           bias=nm[0:n, u % 2, hh:hh + 1], scale=SCALE, accum_out=den[0:n, u % 2, hh:hh + 1])
                    fn(es[0:n, u % 2, :], sm[0:n, u % 2, :], ACT.Exp).then_inc(p_ready, 1)

                def turned(u):
                    b = u // 4
                    n, kn = TB[b][1], WINDOW[b][1]
                    act.wait_ge(pt_done, L(u + 1, UNITS))
                    bank = banks[4 + u % 2][:, :].rearrange("p (h k n) -> p h k n", h=2, k=2)
                    for kt in range((kn + P - 1) // P):
                        w = min(P, kn - kt * P)
                        last = fn(probT[0:w, u % 4, :, kt, 0:n], bank[0:w, :, kt, 0:n], ACT.Copy)
                    last.then_inc(pt_ready, 1)

                def outs(b):
                    t0, n = TB[b]
                    act.wait_ge(o_done, L(4 * b + 4, UNITS))
                    fn(aT[:, :, t0:t0 + n], grid(b, banks[6 + b % 2][:, :], 4), ACT.Copy)
                    if b:
                        act.wait_ge(a_ssq, L(b, NB))
                    fn(sqa[:, :, 0:n], grid(b, banks[6 + b % 2][:, :], 4), ACT.Square).then_inc(a_taken, 1)

                def hi_of_merged(n):
                    g, k = MERGED[n]
                    act.wait_ge(prod_ready, L(n + 1, 2 * KT))
                    fn(h_hi[:, k, cols(g)], h_whole[:, k, cols(g)], ACT.Copy).then_inc(hhi_ready, 1)

                for u in range(UNITS + 5):
                    if u < UNITS:
                        exps(u)
                    if 3 <= u < UNITS + 3:
                        turned(u - 3)
                    if u >= 5 and (u - 5) % 4 == 3:
                        outs((u - 5) // 4)
                    if u == B_AT:
                        for g in (0, 1):
                            root(L(ST["b"] + g, STS), g, rsq[:, 0, :], 6 + g, 256)
                    if u == A_AT:
                        root(L(ST["a"], STS), 0, acc, 7, SWA_HEADS * HD)
                    for n in MERGED_AT.get(u, ()):
                        hi_of_merged(n)
                root(L(ST["a"] + 1, STS), 1, acc, 4, SWA_HEADS * HD)
                for n in range(12, 2 * KT):
                    hi_of_merged(n)

                def out_tile(m, g):
                    take_y("mix", m, g, 2 * S_OUT + order(m, g) + 1, tile_bank(m, g), y_mix, "post_mix")

                for g in (0, 1):
                    for m in range(HEAD):
                        out_tile(m, g)
                        if g == 1:
                            split(S_OUT + m + RING, l=l)
                for m in range(HEAD, OUT_T - 1):
                    for g in (0, 1):
                        out_tile(m, g)
                    split(S_OUT + m + RING, l=l)
                out_tile(OUT_T - 1, 0)
                root(L(ST["post_mix"], STS), 0, rstd, 4, D)

                def last_out():
                    out_tile(OUT_T - 1, 1)
                    split(S_OUT + OUT_T - 1 + RING, l=l)

                next_norm("mix", "post_mix", "pre_ffn", 0, last_out, {})
                for g in (0, 1):
                    root(L(ST["pre_ffn"] + g, STS), g, rstd, 4, D)

                def silu(gate, g):
                    act.wait_ge(dve_took, 1 + L(V_GU + order(2 * gate, g) + 1, V_TOOK))
                    t = gate_whole[:, gate, cols(g)]
                    fn(t, t, ACT.Silu).then_inc(silu_ready, 1)

                def hid_split(gate, g, n):
                    act.wait_ge(hid_prod, L(n + 1, 2 * FT))
                    fn(hid_hi[:, gate, cols(g)], hid_whole[:, gate, cols(g)], ACT.Copy)\
                        .then_inc(hid_hi_ready, 1)

                for g in (0, 1):
                    if g == 1:
                        for t in (0, 1):
                            act.wait_ge(*slot_used(l, S_GU + t))
                            split(S_GU + t + RING, l=l)
                    for gate in (0, 1):
                        silu(gate, g)
                    for gate in (0, 1):
                        hid_split(gate, g, 2 * g + gate)
                for t in (2, 3):
                    act.wait_ge(*slot_used(l, S_GU + t))
                    split(S_GU + t + RING, l=l)
                with act.Fori(0, FT // 2 - 1) as it:
                    for i in (0, 1):
                        t = HEAD + 2 * i
                        gate = ds(it * 2 + (2 + i), 1)
                        for g in (0, 1):
                            act.wait_ge(dve_took, 1 + L(V_GU + 2 * t + g + 1, V_TOOK) + it * 8)
                            h = gate_whole[:, gate, cols(g)]
                            fn(h, h, ACT.Silu).then_inc(silu_ready, 1)
                        for d in (0, 1):
                            act.wait_ge(tile_done, 1 + L(2 * (S_GU + t + d + 1), 2 * TILES) + it * 8)
                            split(S_GU + t + d + RING, off=it * 4, l=l)
                        for g in (0, 1):
                            act.wait_ge(hid_prod, L(t + g + 1, 2 * FT) + it * 4)
                            fn(hid_hi[:, gate, cols(g)], hid_whole[:, gate, cols(g)], ACT.Copy)\
                                .then_inc(hid_hi_ready, 1)

                def down_tile(m, g):
                    take_y("ffn", m, g, 2 * (TILES - KT + m) + g + 1, out_bank(m % 2, g), y_ffn, "post_ffn")

                for s in range(S_DN, S_LAST):
                    a, b = 8 * (s - S_DN), 8 * (s - S_DN) + 8
                    act.wait_ge(*slot_used(l, s))
                    split(s + RING, l=l)
                    for m in range(KT - 1):
                        if a <= m * FT + FT - 1 < b:
                            for g in (0, 1):
                                down_tile(m, g)
                for m in range(8 * (S_LAST - S_DN) // FT, KT - 1):
                    for g in (0, 1):
                        down_tile(m, g)
                down_tile(KT - 1, 0)
                root(L(ST["post_ffn"], STS), 0, rstd, 4, D)

                def last_down():
                    down_tile(KT - 1, 1)
                    act.wait_ge(*slot_used(l, SLOTS - 1))
                    split(SLOTS - 1 + RING, l=l)

                next_norm("ffn", "post_ffn", "next_mix", 16, last_down, SPLITS_AT)

        @block.vector
        def _(dve):
            def split(s, off=0, l=0):
                dve.wait_ge(hi_made, l * SLOTS + (s + 1) + off)
                dve.tensor_tensor(w_lo[:, s % RING, :], raw[:, s % RAW, :],
                                  w_hi[:, s % RING, :].bitcast(F32), ALU.subtract).then_inc(lo_made, 1)

            def lo_of_x(g, k, name, count):
                dve.wait_ge(hhi_ready, count)
                c = SP[name] + k
                dve.scalar_tensor_tensor(out=h_lo[:, k, cols(g)], in0=x[:, k, cols(g)], scalar=sp[:, c:c + 1],
                                         in1=h_hi[:, k, cols(g)].bitcast(F32),
                                         op0=ALU.mult, op1=ALU.subtract).then_inc(h_ready, 1)

            dve.sem_inc(x_ready, 1)
            dve.sem_inc(h_ready, 1)
            dve.memset(ones[:, :], 1.0).then_inc(dve_chain, 1)
            dve.memset(st_p[:, :, :], 0.0)
            dve.memset(epsc[:, :], EPS).then_inc(ones_set, 1)
            for g in (0, 1):
                split(g)
                for k in range(KT):
                    lo_of_x(g, k, "pre_mix", 8 * g + k + 1)
            for s in range(2, RING):
                split(s)
            with dve.Fori(0, DEPTH) as l:
                links = [0]

                def L(n, per):
                    return l * per + n

                def link(last):
                    links[0] += 1
                    last.then_inc(dve_chain, 1)
                    dve.wait_ge(dve_chain, l * DVE_LINKS + (links[0] + 1))

                def recip(n, g, t):
                    dve.wait_ge(std_ready, 2 + L(n, STS))
                    link(dve.reciprocal(t[:, cols(g)], t[:, cols(g)]))

                def take(count, out, bank, g):
                    dve.wait_ge(tile_done, 1 + count)
                    return dve.tensor_tensor(out, bank, rstd[:, cols(g)], ALU.mult)

                def residual(part, post, pre, base, y, at):
                    for g in (0, 1):
                        recip(ST[post] + g, g, rstd)
                        if g == 0:
                            dve.wait_ge(x_ready, 1 + L(base, 32))
                        for k in range(0, KT + 2, 2):
                            if k < KT:
                                i = 8 * g + k
                                for s in at.get(i, ()):
                                    split(s + RING, l=l)
                                if i:
                                    dve.wait_ge(x_ready, 1 + L(base + i, 32))
                                for d in (0, 1):
                                    last = dve.tensor_tensor(tp[:, d, 0:width(g)], y[:, k + d, cols(g)],
                                                             rstd[:, cols(g)], ALU.mult)
                                link(last)
                                for d in (0, 1):
                                    dve.tensor_tensor(x[:, k + d, cols(g)], x[:, k + d, cols(g)],
                                                      tp[:, d, 0:width(g)], ALU.add).then_inc(x_ready, 1)
                            if k:
                                for d in (0, 1):
                                    lo_of_x(g, k - 2 + d, pre, L(HR[pre] + 8 * g + k - 2 + d + 1, HRS))

                dve.wait_ge(small_landed, L(2, 1) * 16)
                dve.tensor_scalar(nsink[:, :], sp[:, SP["sink"]:SP["sink"] + 8], -1.0, None, ALU.mult)\
                   .then_inc(nsink_ready, 1)

                def table(name, w, n=P):
                    return tab[0:n, TAB[name]:TAB[name] + w]

                def rotate_q():
                    dve.wait_ge(tab_landed, L(1, 1) * 32)
                    gw = lp[CHUNK:P, LP["gw"]:LP["gw"] + 4 * P].rearrange("p (g i) -> p g i", i=P)
                    dve.memset(gw[:, :, 0:CHUNK], 0.0)
                    dve.wait_ge(dve_took, 1 + L(2 * HEAD, V_TOOK))
                    A, B = ret[:, 0, :], ret[:, 1, :]
                    dve.tensor_tensor(rtmp[:, 0, :], A, table("sin", T), ALU.mult)
                    link(dve.tensor_tensor(rtmp[:, 1, :], B, table("sin", T), ALU.mult))
                    dve.tensor_tensor(A, A, table("cos", T), ALU.mult)
                    link(dve.tensor_tensor(B, B, table("cos", T), ALU.mult))
                    dve.tensor_tensor(A, A, rtmp[:, 1, :], ALU.subtract)
                    link(dve.tensor_tensor(B, B, rtmp[:, 0, :], ALU.add))
                    xi = table("xi", P)
                    for half in (0, 1):
                        dve.tensor_tensor(qxi[:, half, 0:SEQ].rearrange("p (b n) -> p b n", n=P),
                                          ret[:, half, 0:SEQ].rearrange("p (b n) -> p b n", n=P),
                                          xi.unsqueeze(1).to_broadcast([P, 4, P]), ALU.mult)
                        last = dve.tensor_tensor(qxi[:, half, SEQ:T], ret[:, half, SEQ:T], xi[:, 0:DEC], ALU.mult)
                    last.then_inc(rotq_ready, 1)

                def decay(b):
                    n = TB[b][1]
                    if b >= 2:
                        dve.wait_ge(ro_done, L(b - 1, NB))
                    dve.wait_ge(rk_done, L(b + 1, NB))
                    dve.tensor_tensor(kz[0:n, b % 2, :], banks[5][0:n, 0:256],
                                      table("zeta" if b < NB - 1 else "zetas", 256, n), ALU.mult).then_inc(kz_ready, 1)
                    dve.wait_ge(rs_done, L(b + 1, NB))
                    dve.tensor_tensor(inner[0:n, b % 2, :, 0:n], grid(b, banks[6][0:n, :], 4),
                                      grid(b, table("decay", 512, n), 4), ALU.mult).then_inc(inner_ready, 1)

                def state(b):
                    t0, n = TB[b]
                    dve.wait_ge(ro_done, L(b + 1, NB))
                    dve.tensor_copy(rT[:, :, t0:t0 + n], grid(b, banks[7][:, 0:2 * P], 2)).then_inc(ro_taken, 1)
                    if b:
                        dve.wait_ge(state_ready, L(b, NB))
                    st = st_s if b == NB - 1 else st_p
                    c = TAB["cdec"] + (b == NB - 1)
                    for hh in range(RET_HEADS):
                        r = slice(32 * hh, 32 * hh + 32)
                        new = banks[7][r, 2 * P:3 * P].rearrange("p (h d) -> p h d", h=2)
                        old = st[r, :, hh * HD:(hh + 1) * HD]
                        if b == 0:
                            last = dve.tensor_copy(old, new)
                        else:
                            last = dve.scalar_tensor_tensor(out=old, in0=old, scalar=tab[r, c:c + 1], in1=new,
                                                            op0=ALU.mult, op1=ALU.add)
                    last.then_inc(state_ready, 1)

                def bn(b):
                    n = TB[b][1]
                    dve.wait_ge(gt_taken, L(b + 1, NB))
                    link(dve.bn_stats(bst[0:n, b, :], gvt[0:n, b, :]))
                    dve.sem_inc(dve_passed, 1)
                    dve.bn_aggr(bmv[0:n, b, :], bst[0:n, b, :]).then_inc(bn_ready, 1)

                def centre(i):
                    c, g = i // 2, i % 2
                    dve.wait_ge(gn_mean, L(i + 1, 4))
                    dve.tensor_tensor(rT[:, c, cols(g)], rT[:, c, cols(g)], banks[4 + i][:, 0:width(g)],
                                      ALU.subtract).then_inc(gn_cent, 1)

                def scale_r(i):
                    c, g = i // 2, i % 2
                    dve.wait_ge(gn_std, L(i + 1, 4))
                    link(dve.reciprocal(rsq[:, c, cols(g)], rsq[:, c, cols(g)]))
                    dve.tensor_tensor(rT[:, c, cols(g)], rT[:, c, cols(g)], rsq[:, c, cols(g)], ALU.mult)\
                       .then_inc(c_ready, 1)

                def v_rows():
                    dve.wait_ge(ln_std, L(1, 1))
                    dve.wait_ge(gt_taken, L(NB, NB))
                    n = TB[-1][1]
                    dve.reciprocal(brs[:, 0:NB - 1], brs[:, 0:NB - 1])
                    link(dve.reciprocal(brs[0:n, NB - 1:NB], brs[0:n, NB - 1:NB]))
                    for b in range(NB):
                        n = TB[b][1]
                        last = dve.tensor_scalar(gvt[0:n, b, :], gvt[0:n, b, :], bmv[0:n, b, 0:1],
                                                 brs[0:n, b:b + 1], ALU.subtract, ALU.mult)
                    link(last)
                    for b in range(NB):
                        n = TB[b][1]
                        last = dve.tensor_tensor(gvt[0:n, b, :], gvt[0:n, b, :], lp[0:n, LP["lng"]:LP["lng"] + 256],
                                                 ALU.mult)
                    link(last)
                    for b in range(NB):
                        n = TB[b][1]
                        dve.tensor_tensor(gvt[0:n, b, :], gvt[0:n, b, :], lp[0:n, LP["lnb"]:LP["lnb"] + 256],
                                          ALU.add).then_inc(gvt_ready, 1)

                def gate_b(b):
                    t0, n = TB[b]
                    dve.wait_ge(mixed_done, L(b + 1, NB))
                    bank = banks[4 + b % 4][:, 0:2 * P]
                    if b == 0:
                        dve.wait_ge(c_ready, L(4, 4))
                        dve.wait_ge(curved, L(12, 12))
                    link(dve.tensor_tensor(rsq[:, :, t0:t0 + n], grid(b, bank, 2),
                                           grid(b, lp[:, LP["gb"]:LP["gb"] + 256], 2), ALU.add))
                    dve.tensor_tensor(ub[:, :, t0:t0 + n], ub[:, :, t0:t0 + n], rsq[:, :, t0:t0 + n],
                                      ALU.mult).then_inc(b_ready, 1)

                more = {i: [] for i in range(IN_T)}
                for b in range(NB):
                    more[7 + b].append(lambda b=b: state(b))
                    more[6 + b].append(lambda b=b: decay(b))
                    more[14].append(lambda b=b: bn(b))
                    more[15].append(lambda b=b: gate_b(b))
                for i in range(4):
                    more[12].append(lambda i=i: centre(i))
                    more[13].append(lambda i=i: scale_r(i))
                more[14].append(v_rows)

                def in_tile(i, g):
                    count, bank = L(order(i, g) + 1, 2 * TILES), tile_bank(i, g)
                    if i == IN_K:
                        dve.wait_ge(tile_done, 1 + count)
                        for a, b in seg(g):
                            r = slice(GROUPS[g][0] + a.start, GROUPS[g][0] + a.stop)
                            last = dve.tensor_tensor(kk[:, b], bank[:, a], rstd[:, r], ALU.mult)
                    else:
                        if i <= IN_V1:
                            out = ret[:, i, cols(g)]
                        elif i <= IN_UB1:
                            out = (sg if i <= IN_G1 else gv if i <= IN_VB1 else ub)[:, i % 2, cols(g)]
                        elif i == IN_V:
                            out = vv[:, cols(g)]
                        else:
                            out = qq[:, i - IN_Q0, cols(g)]
                        last = take(count, out, bank, g)
                    last.then_inc(dve_took, 1)

                for g in (0, 1):
                    recip(ST["pre_mix"] + g, g, rstd)
                    for i in range(HEAD):
                        in_tile(i, g)
                        if g == 1:
                            split(S_IN + i + RING, l=l)
                rotate_q()
                for i in range(HEAD, IN_T):
                    for g in (0, 1):
                        in_tile(i, g)
                    split(S_IN + i + RING, l=l)
                    for f in more[i]:
                        f()

                dve.wait_ge(nsink_ready, L(1, 1))

                def maxima(u):
                    b, j = divmod(u, 4)
                    n, kn = TB[b][1], WINDOW[b][1]
                    dve.wait_ge(s_done, L(u + 1, UNITS))
                    i = 2 * (u % 2)
                    bank = psum[0:n, i:i + 2, 0:kn]
                    ns = nsink[0:n, 2 * j:2 * j + 2]
                    if u >= 2:
                        dve.wait_ge(nm_ready, L(u - 1, UNITS))
                    link(dve.tensor_reduce(mx[0:n, u % 2, :], bank, AX.X, ALU.max))
                    link(dve.scalar_tensor_tensor(out=nm[0:n, u % 2, :], in0=mx[0:n, u % 2, :], scalar=-SCALE,
                                                  in1=ns, op0=ALU.mult, op1=ALU.min))
                    dve.tensor_tensor(sm[0:n, u % 2, :], nm[0:n, u % 2, :], ns, ALU.subtract).then_inc(nm_ready, 1)

                def normalise(u):
                    b = u // 4
                    n, kn = TB[b][1], WINDOW[b][1]
                    dve.wait_ge(p_ready, L(u + 1, UNITS))
                    if u >= 2:
                        dve.wait_ge(pn_ready, L(u - 1, UNITS))
                    link(dve.tensor_tensor(rd[0:n, u % 2, :], den[0:n, u % 2, :], es[0:n, u % 2, :], ALU.add))
                    link(dve.reciprocal(rd[0:n, u % 2, :], rd[0:n, u % 2, :]))
                    for hh in (0, 1):
                        last = dve.tensor_scalar(prob[0:n, u % 4, hh, 0:kn], prob[0:n, u % 4, hh, 0:kn],
                                                 rd[0:n, u % 2, hh:hh + 1], None, ALU.mult)
                    last.then_inc(pn_ready, 1)

                def merged(n):
                    g, k = MERGED[n]
                    if k < 4:
                        src, c, scale = aT[:, k, cols(g)], SP["na"] + k, acc[:, cols(g)]
                    elif k < 6:
                        src, c, scale = ub[:, k - 4, cols(g)], SP["nb"] + k - 4, rsq[:, 0, cols(g)]
                    else:
                        src, c, scale = rT[:, k - 6, cols(g)], SP["rg"] + k - 6, sg[:, k - 6, cols(g)]
                    dve.scalar_tensor_tensor(out=h_whole[:, k, cols(g)], in0=src, scalar=sp[:, c:c + 1],
                                             in1=scale, op0=ALU.mult, op1=ALU.mult).then_inc(prod_ready, 1)

                def lo_of_merged(n):
                    g, k = MERGED[n]
                    dve.wait_ge(hhi_ready, L(HR["merged"] + n + 1, HRS))
                    dve.tensor_tensor(h_lo[:, k, cols(g)], h_whole[:, k, cols(g)],
                                      h_hi[:, k, cols(g)].bitcast(F32), ALU.subtract).then_inc(h_ready, 1)

                for u in range(UNITS + 1):
                    if u < UNITS:
                        maxima(u)
                    if u:
                        normalise(u - 1)
                    if u - 1 in MERGED_AT:
                        for n in MERGED_AT[u - 1]:
                            lo_of_merged(n)
                    if u in MERGED_AT:
                        if u == min(MERGED_AT):
                            for g in (0, 1):
                                recip(ST["b"] + g, g, rsq[:, 0, :])
                        if u == A_AT + 1:
                            recip(ST["a"], 0, acc)
                        for n in MERGED_AT[u]:
                            merged(n)
                recip(ST["a"] + 1, 1, acc)
                for n in range(12, 2 * KT):
                    merged(n)
                for n in range(12, 2 * KT):
                    lo_of_merged(n)

                for m in range(OUT_T):
                    split(S_OUT + m + RING, l=l)
                residual("mix", "post_mix", "pre_ffn", 0, y_mix, {})

                def gate_up(t, g):
                    out = (gate_whole, hid_whole)[t % 2][:, t // 2, cols(g)]
                    take(L(2 * S_GU + order(t, g) + 1, 2 * TILES), out, head_bank(t, g), g).then_inc(dve_took, 1)

                dve.wait_ge(out_landed, L(NOUT, NOUT) * 16)
                for g in (0, 1):
                    recip(ST["pre_ffn"] + g, g, rstd)
                    if g == 1:
                        for t in (0, 1):
                            split(S_GU + t + RING, l=l)
                    for t in range(HEAD):
                        gate_up(t, g)
                    for gate in (0, 1):
                        n = 2 * g + gate
                        dve.wait_ge(silu_ready, L(n + 1, 2 * FT))
                        dve.wait_ge(dve_took, 1 + L(V_GU + order(2 * gate + 1, g) + 1, V_TOOK))
                        t = hid_whole[:, gate, cols(g)]
                        dve.tensor_tensor(t, t, gate_whole[:, gate, cols(g)], ALU.mult).then_inc(hid_prod, 1)
                    for gate in (0, 1):
                        dve.wait_ge(hid_hi_ready, L(2 * g + gate + 1, 2 * FT))
                        dve.tensor_tensor(hid_lo[:, gate, cols(g)], hid_whole[:, gate, cols(g)], hid_hi[:, gate, cols(g)].bitcast(F32), ALU.subtract)\
                           .then_inc(hid_ready, 1)
                for t in (2, 3):
                    split(S_GU + t + RING, l=l)
                with dve.Fori(0, FT // 2 - 1) as it:
                    for i in (0, 1):
                        t = HEAD + 2 * i
                        gate = ds(it * 2 + (2 + i), 1)

                        def part(buf, g):
                            return buf[:, gate, cols(g)]

                        for d, buf in ((0, gate_whole), (1, hid_whole)):
                            for g in (0, 1):
                                dve.wait_ge(tile_done, 1 + L(2 * (S_GU + t + d) + g + 1, 2 * TILES) + it * 8)
                                dve.tensor_tensor(part(buf, g), out_bank(d, g).unsqueeze(1), rstd[:, cols(g)].unsqueeze(1),
                                                  ALU.mult).then_inc(dve_took, 1)
                            if d == 0:
                                split(S_GU + t + RING, off=it * 4, l=l)
                        for g in (0, 1):
                            dve.wait_ge(silu_ready, L(t + g + 1, 2 * FT) + it * 4)
                            dve.wait_ge(dve_took, 1 + L(V_GU + 2 * (t + 1) + g + 1, V_TOOK) + it * 8)
                            dve.tensor_tensor(part(hid_whole, g), part(hid_whole, g), part(gate_whole, g), ALU.mult)\
                               .then_inc(hid_prod, 1)
                        split(S_GU + t + 1 + RING, off=it * 4, l=l)
                        for g in (0, 1):
                            dve.wait_ge(hid_hi_ready, L(t + g + 1, 2 * FT) + it * 4)
                            dve.tensor_tensor(part(hid_lo, g), part(hid_whole, g), part(hid_hi, g).bitcast(F32),
                                              ALU.subtract)\
                               .then_inc(hid_ready, 1)

                for s in range(S_DN, S_LAST):
                    split(s + RING, l=l)
                residual("ffn", "post_ffn", "next_mix", 16, y_ffn, SPLITS_AT)
                split(SLOTS - 1 + RING, l=l)
                assert links[0] == DVE_LINKS, links[0]

        @block.gpsimd
        def _(pool):
            pool.sem_inc(sq_added, 1)
            pool.dma_start(sp[:, :], small[0]).then_inc(small_landed, 16)
            pool.dma_start(ident[:, :], ident_d).then_inc(const_landed, 16)
            pool.dma_start(mask[:, :], mask_d).then_inc(const_landed, 16)

            def add_square(n, count, g, first, stats):
                pool.wait_ge(sq_ready, count + 1)
                buf = sq[:, n % 2, 0:width(g)]
                if first:
                    if stats is not None:
                        pool.wait_ge(stat_done, 1 + stats)
                        pool.sem_inc(pool_passed, 1)
                    pool.tensor_copy(acc[:, cols(g)], buf).then_inc(sq_added, 1)
                else:
                    pool.wait_ge(sq_added, 1 + count)
                    pool.tensor_tensor(acc[:, cols(g)], acc[:, cols(g)], buf, ALU.add).then_inc(sq_added, 1)

            for n in range(2 * KT):
                add_square(n, n, n // KT, n % KT == 0, None)
            with pool.Fori(0, DEPTH) as l:
                links = [0]

                def L(n, per):
                    return l * per + n

                def link(last):
                    links[0] += 1
                    last.then_inc(pool_chain, 1)
                    pool.wait_ge(pool_chain, l * POOL_LINKS + links[0])

                def alone(s, v):
                    pool.wait_ge(s, v)
                    pool.sem_inc(pool_passed, 1)

                def states(dram):
                    return dram[ds(l, 1)].rearrange("o p h d -> (o p) h d")

                def layer(dram):
                    return dram[ds(l, 1)].rearrange("o p n -> (o p) n")

                pool.wait_ge(ones_set, 1)
                alone(h_ready, 1 + L(HR["pre_mix"] + 16, HRS))
                pool.dma_start(sp[:, :], layer(small)).then_inc(small_landed, 16)
                alone(tile_done, 1 + L(0, 2 * TILES))
                link(pool.memset(st_s[:, :, :], 0.0))
                pool.sem_inc(pool_passed, 1)
                pool.dma_start(tab[:, :], tabs).then_inc(tab_landed, 16)
                pool.dma_start(lp[:, :], layer(lpar)).then_inc(tab_landed, 16)
                pool.dma_start(kk[:, SEQ:SEQ + P], layer(kcache)).then_inc(cache_landed, 16)
                pool.dma_start(vk[:, 4, :], layer(vcache)).then_inc(cache_landed, 16)
                for hh in range(RET_HEADS):
                    r = slice(32 * hh, 32 * hh + 32)
                    pool.dma_start(st_s[r, :, hh * HD:(hh + 1) * HD], states(ret0)[r]).then_inc(cache_landed, 16)

                def add_squares(part):
                    post = ST["post_mix"] if part == "mix" else ST["post_ffn"]
                    for n, (kind, g, k) in enumerate(SQUARES[part]):
                        n += SQ[part]
                        stats = post if kind == "post" else post + g + 1
                        add_square(n, L(n, SQS), g, k == 0, L(stats, STS))

                pool.wait_ge(tab_landed, L(1, 1) * 32)
                pool.wait_ge(dve_took, 1 + L(2 * HEAD, V_TOOK))
                A, B = ret[:, 2, :], ret[:, 3, :]
                cosk, sink = (tab[:, TAB[x_]:TAB[x_] + T] for x_ in ("cosk", "sink"))
                pool.tensor_tensor(ptmp[:, 0, :], A, sink, ALU.mult)
                link(pool.tensor_tensor(ptmp[:, 1, :], B, sink, ALU.mult))
                pool.tensor_tensor(A, A, cosk, ALU.mult)
                link(pool.tensor_tensor(B, B, cosk, ALU.mult))
                pool.tensor_tensor(A, A, ptmp[:, 1, :], ALU.subtract)
                pool.tensor_tensor(B, B, ptmp[:, 0, :], ALU.add).then_inc(rotk_ready, 1)

                head = tab[:, TAB["head"]:TAB["head"] + RET_HEADS].unsqueeze(2)
                pool.wait_ge(rotq_ready, L(1, 1))
                for b in range(NB):
                    t0, n = TB[b]
                    if b >= 2:
                        pool.wait_ge(rs_done, L(b - 1, NB))
                    for half in (0, 1):
                        last = pool.tensor_tensor(qm[:, b % 2, half, :, 0:n],
                                                  ret[:, half, t0:t0 + n].unsqueeze(1).to_broadcast([P, RET_HEADS, n]),
                                                  head.to_broadcast([P, RET_HEADS, n]), ALU.mult)
                    last.then_inc(qm_ready, 1)

                alone(state_ready, L(NB, NB))
                for hh in range(RET_HEADS):
                    r = slice(32 * hh, 32 * hh + 32)
                    for dram, st in ((o_rp, st_p), (o_rs, st_s)):
                        pool.dma_start(states(dram)[r], st[r, :, hh * HD:(hh + 1) * HD]).then_inc(out_landed, 16)
                alone(gvt_ready, L(NB, NB))
                pool.dma_start(layer(o_gv), gvt[0:DEC, NB - 1, :]).then_inc(out_landed, 16)
                alone(dve_took, 1 + L(2 * (IN_V + 1), V_TOOK))
                W = P + DEC
                for dram, t, end in ((o_k, kk, KC), (o_v, vv, T)):
                    pool.dma_start(layer(dram)[:, 0:P], t[:, SEQ - P:SEQ]).then_inc(out_landed, 16)
                    pool.dma_start(layer(dram)[:, P:W], t[:, end - DEC:end]).then_inc(out_landed, 16)

                pool.wait_ge(b_ready, L(NB, NB))
                link(pool.tensor_tensor(gv[:, :, :], ub[:, :, :], ub[:, :, :], ALU.mult))
                pool.tensor_tensor(rsq[:, 0, :], gv[:, 0, :], gv[:, 1, :], ALU.add).then_inc(b_ssq, 1)
                for b in range(NB):
                    t0, n = TB[b]
                    pool.wait_ge(a_taken, L(b + 1, NB))
                    link(pool.tensor_tensor(acc[:, t0:t0 + n], sqa[:, 0, 0:n], sqa[:, 1, 0:n], ALU.add))
                    link(pool.tensor_tensor(acc[:, t0:t0 + n], acc[:, t0:t0 + n], sqa[:, 2, 0:n], ALU.add))
                    pool.tensor_tensor(acc[:, t0:t0 + n], acc[:, t0:t0 + n], sqa[:, 3, 0:n], ALU.add)\
                        .then_inc(a_ssq, 1)

                add_squares("mix")
                add_squares("ffn")
                assert links[0] == POOL_LINKS, links[0]


IN_SPLITS = (512, 128, 128, 256, 256, 256, 256, 256, 256)


def in_columns():
    qa, ka, va, ub, vb, qc, kc, vc, gc = (int(v) for v in np.cumsum((0,) + IN_SPLITS[:-1]))
    half = lambda o, h: np.concatenate([o + HD * r + 32 * h + np.arange(32) for r in range(RET_HEADS)])
    run = lambda o, n: np.arange(o, o + n)
    pairs = [np.concatenate([qa + HD * j + np.arange(HD), qa + HD * (j + 4) + np.arange(HD)]) for j in range(4)]
    return np.concatenate([half(qc, 0), half(qc, 1), half(kc, 0), half(kc, 1), run(vc, 256), run(gc, 256),
                           run(vb, 256), run(ub, 256), run(ka, 128), run(va, 128)] + pairs)


def pair_rows():
    return np.concatenate([np.concatenate([HD * j + np.arange(HD), HD * (j + 4) + np.arange(HD)]) for j in range(4)])


def slots_of(w):
    k, n = w.shape
    return w.reshape(k // P, P, n // P, P).transpose(2, 1, 0, 3)


def constants():
    f = np.float32
    half = HD // 2
    inv = (f(10000.0) ** (-np.arange(half, dtype=f) / f(half))).astype(f)
    pos = np.concatenate([np.arange(SEQ), PAST + np.arange(DEC)]).astype(f)
    ang = (pos[:, None] * inv[None, :]).astype(f).astype(np.float64)
    cos, sin = (np.tile(t(ang).astype(f).T, (RET_HEADS, 1)) for t in (np.cos, np.sin))
    logg = np.log(1.0 - 2.0 ** (-5.0 - np.arange(RET_HEADS)))
    i = np.arange(P)
    of_row = np.repeat(np.arange(RET_HEADS), 32)
    xi = np.exp(logg[of_row][:, None] * (i + 1.0)[None, :])
    rel = i[None, :] - i[:, None]
    decay = np.where(rel[:, None, :] >= 0, np.exp(logg[None, :, None] * np.maximum(rel, 0)[:, None, :]), 0.0)
    zeta = lambda block: np.tile(np.exp(logg[of_row][None, :] * (block - 1.0 - i)[:, None]), (1, 2))
    blk = np.kron(np.eye(2), np.ones((HD, HD))) / HD
    cdec = np.exp(logg[of_row][:, None] * np.array([P, DEC], float)[None, :])
    parts = [cos, sin, cos * f(SCALE), sin * f(SCALE), xi, decay.reshape(P, -1), zeta(P),
             np.where(i[:, None] < DEC, zeta(DEC), 0.0), blk, cdec,
             of_row[:, None] == np.arange(RET_HEADS)[None, :]]
    return np.ascontiguousarray(np.concatenate([p.astype(f) for p in parts], axis=1))


def kernel(**inputs):
    import concourse.bacc as bacc
    from concourse.bass_utils import run_bass_kernel_spmd
    import ml_dtypes

    a = {k: np.asarray(v) for k, v in inputs.items()}
    f = np.float32
    to_tiles = lambda t: np.ascontiguousarray(t.reshape(t.shape[0], -1, P).transpose(2, 1, 0))
    xT = to_tiles(np.concatenate([a["x_prompt"][0], a["x_sample"][0]], axis=0))
    cols_in, rows_a = in_columns(), pair_rows()
    rows_out = np.concatenate([rows_a, np.arange(512, 1024)])
    wts = []
    for l in range(DEPTH):
        wts.append(slots_of(a["w_in"][l][:, cols_in]))
        wts.append(slots_of(a["w_out"][l][rows_out]))
        gu = np.stack([slots_of(a["w_gate"][l]), slots_of(a["w_up"][l])], axis=1)
        wts.append(gu.reshape((2 * FT,) + gu.shape[2:]))
        dn = slots_of(a["w_down"][l]).transpose(0, 2, 1, 3).reshape(-1, 8, P, P)
        wts.append(dn.transpose(0, 2, 1, 3))
    wts = np.ascontiguousarray(np.concatenate(wts, axis=0).reshape(DEPTH * SLOTS, P, 1024))

    col = lambda v: v.reshape(-1, P).T
    small = np.stack([np.concatenate([
        col(a["ln_pre_mix"][l]), col(a["ln_pre_mix"][(l + 1) % DEPTH]), col(a["ln_post_mix"][l]), col(a["ln_pre_ffn"][l]), col(a["ln_post_ffn"][l]),
        col(a["norm_a_g"][l][rows_a]), col(a["norm_b_g"][l]), col(a["ret_norm_g"][l]),
        np.broadcast_to(a["swa_sinks"][l].reshape(2, 4).T.reshape(1, 8), (P, 8))], axis=1) for l in range(DEPTH)])
    rows = lambda v: np.broadcast_to(v[None, :], (P, v.size))
    lpar = []
    for l in range(DEPTH):
        gb = np.repeat(a["gmlp_b"][l].reshape(2, 2, 1, P), HD, axis=2).transpose(1, 2, 0, 3).reshape(P, 2 * P)
        gw = np.ascontiguousarray(a["gmlp_w"][l].transpose(2, 0, 1))
        lpar.append(np.concatenate([rows(a["gmlp_ln_g"][l]), rows(a["gmlp_ln_b"][l]), gb, gw.reshape(P, 4 * P)], axis=1))
    lpar = np.stack(lpar)
    ck, cv = a["cache_swa_k"][0], a["cache_swa_v"][0]
    kcache = np.ascontiguousarray(ck.reshape(DEPTH, P, P).transpose(0, 2, 1))
    vcache = np.ascontiguousarray(cv.reshape(DEPTH, P, P))
    ret0 = np.ascontiguousarray(a["state_ret"][0].reshape(DEPTH, RET_HEADS, 2, 32, HD).transpose(0, 1, 3, 2, 4)
                                .reshape(DEPTH, P, 2, HD))
    q = np.arange(P) < CHUNK
    keys = np.arange(256)
    two = np.concatenate([np.stack([q, ~q]).astype(f), np.stack([keys >= 192, keys < 64]) * f(-1e30)], axis=1)
    mask = np.zeros((2, HD, P + 256), ml_dtypes.bfloat16)
    mask[:, 0:2] = two
    mask = mask.reshape(P, -1)

    arrays = dict(xT=xT, wts=wts, small=small, tabs=constants(), lpar=lpar, kcache=kcache, vcache=vcache, ret0=ret0,
                  ident=np.eye(P, dtype=f), mask=mask)
    outs = dict(x=(P, KT, T), k=(DEPTH, P, P + DEC), v=(DEPTH, P, P + DEC), rp=(DEPTH, P, 2, HD),
                rs=(DEPTH, P, 2, HD), gv=(DEPTH, DEC, 256))
    nc = bacc.Bacc("TRN2", target_bir_lowering=False, num_devices=1)
    arrays = {f"in_{n}": np.ascontiguousarray(v) for n, v in arrays.items()}
    args = [nc.dram_tensor(n, v.shape, mybir.dt.from_np(v.dtype), kind="ExternalInput").ap() for n, v in arrays.items()]
    args += [nc.dram_tensor(f"out_{n}", s, F32, kind="ExternalOutput").ap() for n, s in outs.items()]
    program(nc, *args)
    r = run_bass_kernel_spmd(nc, [arrays], core_ids=[0]).results[0]

    y = r["out_x"].transpose(2, 1, 0).reshape(T, D)
    kv = []
    for n in ("k", "v"):
        t = r[f"out_{n}"].transpose(0, 2, 1).reshape(DEPTH, P + DEC, KV_HEADS, HD)[None]
        kv += [t[:, :, :P], t[:, :, P:]]
    st = [r[f"out_{n}"].reshape(DEPTH, RET_HEADS, 32, 2, HD).transpose(0, 1, 3, 2, 4)
          .reshape(1, DEPTH, RET_HEADS, HD, HD) for n in ("rp", "rs")]
    return tuple(np.ascontiguousarray(t) for t in
                 (y[None, :SEQ], y[None, SEQ:], kv[0], kv[2], kv[1], kv[3], st[0], st[1], r["out_gv"][None]))
```

```python
from contextlib import ExitStack

import numpy as np
import concourse.bass as bass
from concourse import mybir
from concourse.alu_op_type import AluOpType as ALU

F32 = mybir.dt.float32
F32R = mybir.dt.float32r
BF16 = mybir.dt.bfloat16
ACT = mybir.ActivationFunctionType
AX = mybir.AxisListType
ds = bass.ds

P = 128
DEPTH = 2
D = 1024
SEQ = 512
DEC = 64
PAST = 256
T = SEQ + DEC
HD = 64
KT = D // P
D_FF = ((8 * D + 3 * 256 - 1) // (3 * 256)) * 256
FT = D_FF // P
EPS = 1e-6
SCALE = HD ** -0.5
SWA_HEADS, KV_HEADS = 8, 2
RET_HEADS = 4
CHUNK = 64

GROUPS = ((0, 256), (256, T))
GW = max(b - a for a, b in GROUPS)
TB = [(0, 128), (128, 128), (256, 128), (384, 128), (512, 64)]
NB = len(TB)

IN_QA, IN_QB, IN_KA, IN_KB, IN_V0, IN_V1, IN_G0, IN_G1, IN_VB0, IN_VB1, IN_UB0, IN_UB1, IN_K, IN_V, IN_Q0 = range(15)
IN_T = 18
OUT_T = KT
S_IN, S_OUT, S_GU, S_DN = 0, IN_T, IN_T + OUT_T, IN_T + OUT_T + 2 * FT
SLOTS = S_DN + KT * FT // 8
RING, RAW = 4, 2
assert SLOTS % RING == 0 and SLOTS % RAW == 0 and (KT * FT) % 8 == 0

TILES = IN_T + OUT_T + 2 * FT + KT
V_IN, V_GU, V_TOOK = 0, 2 * IN_T, 2 * IN_T + 4 * FT
A_OUT, A_DN, A_TOOK = 0, 2 * OUT_T, 2 * OUT_T + 2 * KT
HEAD = 4
HEAD_BANKS = ((0, 2, 6, 7), (1, 3, 5, 6))
K_OUT = (4, 5, 6, 7, 0, 1, 2, 3)


def order(tile, g):
    return HEAD * g + tile if tile < HEAD else 2 * tile + g


def out_order(m, g):
    return 2 * (OUT_T - 2) + 2 * g + m - (OUT_T - 2) if m >= OUT_T - 2 else order(m, g)


def square_order(head, late):
    post = sorted(((out_order(m, g) if head else 2 * m + g, "post", g, m) for m in range(KT) for g in (0, 1)))
    post = [s[1:] for s in post]
    pre = [("pre", g, k) for g in (0, 1) for k in range(KT)]
    return post[:-1] + pre[:late] + post[-1:] + pre[late:]


LATE = dict(mix=2, ffn=2)
SQUARES = dict(mix=square_order(True, LATE["mix"]), ffn=square_order(False, LATE["ffn"]))
SQ = dict(start=0, mix=2 * KT, ffn=6 * KT)
SQS = 8 * KT
ST = dict(pre_mix=0, b=2, a=4, post_mix=6, pre_ffn=8, post_ffn=10)
STS = 12
HR = dict(pre_mix=0, merged=16, pre_ffn=32, next_mix=48)
HRS = 48


def square_at(part, kind, g, k):
    return SQ[part] + SQUARES[part].index((kind, g, k))


SP = dict(pre_mix=0, next_mix=8, post_mix=16, pre_ffn=24, post_ffn=32, na=40, nb=44, rg=46, sink=48)
SP_N = 56
TAB = {}
_n = 0
for _name, _w in (("cos", T), ("sin", T), ("xi", P), ("head", RET_HEADS),
                  ("decay", 4 * P), ("zeta", 2 * P), ("zetas", 2 * P), ("blk", P), ("cdec", 2)):
    TAB[_name] = _n
    _n += _w
TAB_N = _n
TAB_FIRST = TAB["decay"]
LP = {}
_n = 0
for _name, _w in (("lng", 256), ("lnb", 256), ("gb", 256), ("gw", 512)):
    LP[_name] = _n
    _n += _w
LP_N = _n

KC = SEQ + 128 + DEC
WINDOW = [(0, 128), (0, 256), (128, 256), (256, 256), (512, 192)]
VTILES = [(0,), (0, 1), (1, 2), (2, 3), (4, 5)]
CACHES = 3 + RET_HEADS
NOUT = 17
DN_FREE = sum((8 * i + 7) % FT != FT - 1 for i in range(SLOTS - S_DN))
DVE_LINKS = 127
POOL_LINKS = 16
UNITS = NB * 4
START_OUT = {UNITS + 1: (0, 1), UNITS + 2: (2, 3), UNITS + 3: (4, 5), UNITS + 4: (6, 7)}
SPLIT_AT = 8
A_AT = 15
MERGED = ([(g, k) for g in (0, 1) for k in (4, 5, 6, 7)] + [(g, k) for g in (0, 1) for k in (0, 1, 2, 3)])
MERGED_AT = {5: (0, 1), 7: (2, 3), 9: (4, 5), 11: (6, 7), A_AT + 1: (8, 9), A_AT + 2: (10, 11)}
S_LAST = S_DN + (KT - 1) * FT // 8
SPLITS_AT = {0: (S_LAST, S_LAST + 1)}
LO_AT = {0: (S_LAST,), 2: (S_LAST + 1,), KT: (S_LAST + 2,)}
assert SLOTS - S_LAST == 3


def program(nc, xT, wts, small, tabs, lpar, kcache, vcache, ret0, ident_d, mask_d,
            o_x, o_k, o_v, o_rp, o_rs, o_gv):
    with ExitStack() as ctx:
        sem = lambda name: ctx.enter_context(nc.semaphore(name))

        base = (nc.sbuf_base + 63) // 64 * 64
        at = [base]

        def place(name, shape, dt=F32, offset=None):
            size = int(np.prod(shape[1:])) * (2 if dt == BF16 else 4)
            size = (size + 31) // 32 * 32
            o = at[0] if offset is None else offset
            t = nc.alloc_sbuf_tensor_at(name, shape, dt, offset=o)
            if offset is None:
                at[0] += size
            assert o + size <= nc.sbuf_usable_end, (name, o + size, nc.sbuf_usable_end)
            return t

        x = place("x", [P, KT, T])
        h_hi = place("h_hi", [P, KT, T], F32R)
        h_lo_at = at[0]
        h_lo = place("h_lo", [P, KT, T], F32R)
        raw = place("raw", [P, RAW, 1024])
        w_hi = place("w_hi", [P, RING, 1024], F32R)
        w_lo = place("w_lo", [P, RING, 1024], F32R)
        sp = place("sp", [P, SP_N])
        ident = place("ident", [P, P])
        ones = place("ones", [P, P])
        mask = place("mask", [P, P + 256], BF16)
        epsc = place("epsc", [P, 1])
        scratch = place("scratch", [P, 3])
        acc = place("acc", [P, T])
        rstd = place("rstd", [P, T])
        sq = place("sq", [P, 2, GW])
        tp = place("tp", [P, 2, GW])
        st_p = place("st_p", [P, 2, 256])
        bst = place("bst", [P, NB, 6])
        bmv = place("bmv", [P, NB, 2])
        brs = place("brs", [P, NB])
        nsink = place("nsink", [P, 8])
        mx = place("mx", [P, 2, 2])
        nm = place("nm", [P, 2, 2])
        sm = place("sm", [P, 2, 2])
        es = place("es", [P, 2, 2])
        den = place("den", [P, 2, 2])
        rd = place("rd", [P, 2, 2])
        region = at[0]
        hid_hi = place("hid_hi", [P, FT, T], F32R)
        hid_lo_at = at[0]
        hid_lo = place("hid_lo", [P, FT, T], F32R)
        region_end = at[0]
        at[0] = region
        ret = place("ret", [P, 6, T])
        qxi = place("qxi", [P, 2, T])
        vtok = place("vtok", [P, NB, 256])
        rtmp_at = at[0]
        kz = place("kz", [P, 2, 256])
        inner = place("inner", [P, 2, 4, P])
        rtmp = place("rtmp", [P, 2, T], offset=rtmp_at)
        assert rtmp_at + 2 * T * 4 <= at[0]
        zone2 = at[0]
        at[0] = region
        prob = place("prob", [P, 4, 2, 256])
        probT = place("probT", [P, 4, 2, 2, P])
        sqa = place("sqa", [P, 4, P])
        assert at[0] <= zone2
        y_mix = place("y_mix", [P, KT, T], offset=region)
        h_whole = place("h_whole", [P, KT, T], offset=h_lo_at)
        gate_whole = place("gate_whole", [P, FT, T], offset=region)
        hid_whole = place("hid_whole", [P, FT, T], offset=hid_lo_at)
        y_ffn = place("y_ffn", [P, KT, T], offset=h_lo_at)
        at[0] = zone2
        sg = place("sg", [P, 2, T])
        gv = place("gv", [P, 2, T])
        ub = place("ub", [P, 2, T])
        rT = place("rT", [P, 2, T])
        rsq = place("rsq", [P, 2, T])
        gvt_at = at[0]
        gvt = place("gvt", [P, NB, 256])
        ptmp = place("ptmp", [P, 2, T], offset=gvt_at)
        kk = place("kk", [P, 2, KC])
        vv = place("vv", [P, T])
        vk = place("vk", [P, 6, P])
        qm = place("qm", [P, 2, 2, RET_HEADS, P], offset=at[0])
        qq = place("qq", [P, 4, T])
        st_s = place("st_s", [P, 2, 256])
        tab_at = at[0]
        tab = place("tab", [P, TAB_N])
        lp = place("lp", [P, LP_N])
        aT = place("aT", [P, 4, T], offset=tab_at)
        assert max(at[0], region_end) <= nc.sbuf_usable_end

        psum = ctx.enter_context(nc.psum_tensor("psum", [P, 8, 512], F32))
        banks = [psum[:, i, :] for i in range(8)]

        def out_bank(parity, g):
            a, b = GROUPS[g]
            return banks[2 * parity + g][:, 0:b - a]

        def head_bank(t, g):
            a, b = GROUPS[g]
            return banks[HEAD_BANKS[g][t]][:, 0:b - a]

        def tile_bank(t, g):
            return head_bank(t, g) if t < HEAD else out_bank(t % 2, g)

        x_landed = [sem(f"x_landed{i}") for i in range(4)]
        const_landed = sem("const_landed")
        ones_set = sem("ones_set")
        small_landed = sem("small_landed")
        tab_landed = sem("tab_landed")
        rest_landed = sem("rest_landed")
        cache_landed = sem("cache_landed")
        raw_landed = [sem(f"raw_landed{i}") for i in range(RAW)]
        hi_made = sem("hi_made")
        lo_made = sem("lo_made")
        dn_free = sem("dn_free")
        tile_done = sem("tile_done")
        act_took = sem("act_took")
        dve_took = sem("dve_took")
        sq_ready = sem("sq_ready")
        sq_added = sem("sq_added")
        stat_done = sem("stat_done")
        std_ready = sem("std_ready")
        x_ready = sem("x_ready")
        prod_ready = sem("prod_ready")
        hhi_ready = sem("hhi_ready")
        h_ready = sem("h_ready")
        curved = sem("curved")
        silu_ready = sem("silu_ready")
        hid_prod = sem("hid_prod")
        hid_hi_ready = sem("hid_hi_ready")
        hid_ready = sem("hid_ready")
        rotq_ready = sem("rotq_ready")
        rotk_ready = sem("rotk_ready")
        qm_ready = sem("qm_ready")
        rk_done = sem("rk_done")
        rv_done = sem("rv_done")
        vtok_ready = sem("vtok_ready")
        kz_ready = sem("kz_ready")
        rs_done = sem("rs_done")
        inner_ready = sem("inner_ready")
        ro_done = sem("ro_done")
        ro_taken = sem("ro_taken")
        state_ready = sem("state_ready")
        gn_mean = sem("gn_mean")
        gn_cent = sem("gn_cent")
        gn_sq = sem("gn_sq")
        gn_var = sem("gn_var")
        gn_std = sem("gn_std")
        c_ready = sem("c_ready")
        gt_done = sem("gt_done")
        gt_taken = sem("gt_taken")
        bn_ready = sem("bn_ready")
        ln_std = sem("ln_std")
        gvt_ready = sem("gvt_ready")
        mixed_done = sem("mixed_done")
        b_ready = sem("b_ready")
        b_ssq = sem("b_ssq")
        nsink_ready = sem("nsink_ready")
        vk_done = sem("vk_done")
        vk_ready = sem("vk_ready")
        s_done = sem("s_done")
        nm_ready = sem("nm_ready")
        p_ready = sem("p_ready")
        pn_ready = sem("pn_ready")
        pt_done = sem("pt_done")
        pt_ready = sem("pt_ready")
        o_done = sem("o_done")
        a_taken = sem("a_taken")
        a_ssq = sem("a_ssq")

        dve_chain = sem("dve_chain")
        pool_chain = sem("pool_chain")
        out_landed = sem("out_landed")
        y_landed = sem("y_landed")
        pe_passed, dve_passed, pool_passed = sem("pe_passed"), sem("dve_passed"), sem("pool_passed")

        block = ctx.enter_context(nc.Block())

        def cols(g):
            return slice(*GROUPS[g])

        def width(g):
            return GROUPS[g][1] - GROUPS[g][0]

        def slot_used(l, s):
            for first, count in ((S_IN, IN_T), (S_OUT, OUT_T), (S_GU, 2 * FT)):
                if first <= s < first + count:
                    nth = (out_order if first == S_OUT else order)(s - first, 1)
                    return tile_done, l * (2 * TILES) + (2 + 2 * first + nth)
            last = 8 * (s - S_DN) + 7
            if last % FT == FT - 1:
                return tile_done, l * (2 * TILES) + (1 + 2 * (TILES - KT) + 2 * (last // FT + 1))
            before = sum((8 * i + 7) % FT != FT - 1 for i in range(s - S_DN + 1))
            return dn_free, l * DN_FREE + before

        def seg(g):
            if g == 0:
                return [(slice(0, 256), slice(0, 256))]
            return [(slice(0, 256), slice(256, 512)), (slice(256, GW), slice(KC - DEC, KC))]

        def score_bank(u, hh):
            return banks[2 * (u % 2) + hh]

        def grid(b, bank, w):
            return bank.rearrange("p (i n) -> p i n", n=P)[:, 0:w, 0:TB[b][1]]

        @block.sync
        def _(spe):
            def load_x(g, i):
                ks = slice(i * KT // 2, (i + 1) * KT // 2)
                spe.dma_start(x[:, ks, cols(g)], xT[:, ks, cols(g)]).then_inc(x_landed[2 * g + i], 16)

            def load_slot(n, r):
                spe.dma_start(raw[:, r, :], wts[ds(n, 1)].rearrange("o p n -> (o p) n")).then_inc(raw_landed[r], 16)

            for r in range(RAW):
                load_slot(r, r)
                load_x(0, r)
            for r in range(RAW):
                spe.wait_ge(lo_made, r + 1)
                load_slot(RAW + r, r)
            for i in (0, 1):
                load_x(1, i)
            with spe.Fori(2, DEPTH * SLOTS // RAW) as i:
                for r in range(RAW):
                    spe.wait_ge(lo_made, i * RAW + (r - RAW + 1))
                    load_slot(i * RAW + r, r)
            for r in range(RAW):
                spe.wait_ge(raw_landed[r], DEPTH * SLOTS // RAW * 16)
                spe.sem_inc(raw_landed[r], RING // RAW * 16)
            for g in (0, 1):
                for k in range(0, KT, 2):
                    spe.wait_ge(x_ready, (DEPTH - 1) * 32 + 1 + 16 + KT * g + k + 2)
                    spe.dma_start(o_x[:, k:k + 2, cols(g)], x[:, k:k + 2, cols(g)]).then_inc(y_landed, 16)
            spe.wait_ge(y_landed, KT * 16)
            spe.wait_ge(out_landed, DEPTH * 16 * NOUT)

        @block.tensor
        def _(pe):
            pe.sem_inc(act_took, 1)
            pe.sem_inc(dve_took, 1)
            pe.sem_inc(tile_done, 1)
            pe.sem_inc(stat_done, 1)
            pe.wait_ge(const_landed, 32)
            pe.wait_ge(ones_set, 1)
            with pe.Fori(0, DEPTH) as l:

                def L(n, per):
                    return l * per + n

                def alone(s, v):
                    pe.wait_ge(s, v)
                    pe.sem_inc(pe_passed, 1)

                def three(out, ring, j, rhs_k, g, first, last, hi=h_hi, lo=h_lo):
                    wh, wl = w_hi[:, ring, j * P:(j + 1) * P], w_lo[:, ring, j * P:(j + 1) * P]
                    pe.matmul(out, wh, hi[:, rhs_k, cols(g)], start=first, stop=False)
                    pe.matmul(out, wh, lo[:, rhs_k, cols(g)], start=False, stop=False)
                    return pe.matmul(out, wl, hi[:, rhs_k, cols(g)], start=False, stop=last)

                def stat(n, g, src, bank, waits):
                    for s, v in waits:
                        pe.wait_ge(s, v)
                    pe.matmul(banks[bank][:, 0:width(g)], ones[:, :], src[:, cols(g)],
                              start=True, stop=True).then_inc(stat_done, 1)

                def head(first, base, took, per, free, operand, group1, between, ks=range(KT), late=0,
                         pairs=((0, 1), (2, 3)), early=None, started=False):
                    def part(tiles, g, ready=None):
                        if g == 0:
                            for t in tiles:
                                pe.wait_ge(lo_made, L(first + t + 1, SLOTS))
                            if 0 in tiles:
                                pe.wait_ge(*free)
                        elif 3 in tiles:
                            pe.wait_ge(took, 1 + L(base + order(2, 0) + 1, per))
                        for n, k in enumerate(ks):
                            if ready is not None and n >= late:
                                pe.wait_ge(h_ready, ready + (n - late + 1))
                            for t in tiles:
                                mm = three(head_bank(t, g), (first + t) % RING, k, k, g, n == 0, n == KT - 1)
                                if n == KT - 1:
                                    mm.then_inc(tile_done, 1)
                            if n == 3 and g == 0 and 0 in tiles and early is not None:
                                early()

                    if not started:
                        for p in pairs[:-1]:
                            part(p, 0, operand if 0 in p else None)
                    between(0)
                    part(pairs[-1], 0)
                    between(1)
                    part((0, 1), 1, group1)
                    between(2)
                    part((2,), 1)
                    part((3,), 1)

                def tile(first, base, t, took, per, ks=range(KT), middle=None, groups=(0, 1)):
                    pe.wait_ge(lo_made, L(first + t + 1, SLOTS))
                    for g in groups:
                        before = t - 2 if t >= HEAD + 2 else t - HEAD
                        pe.wait_ge(took, 1 + L(base + order(before, g) + 1, per))
                        for n, k in enumerate(ks):
                            mm = three(out_bank(t % 2, g), (first + t) % RING, k, k, g, n == 0, n == KT - 1)
                            if g == 1 and n == 3 and middle is not None:
                                middle()
                        mm.then_inc(tile_done, 1)

                def post_stat(name, part, g):
                    stat(ST[name] + g, g, acc, 4 + g, [(sq_added, 1 + L(square_at(part, "post", g, KT - 1) + 1, SQS))])

                def pre_stat(name, count, g):
                    stat(ST[name] + g, g, acc, 4, [(sq_added, 1 + count),
                                                   (std_ready, 1 + L(ST[name] + g, STS))])

                def ret_in(b):
                    t0, n = TB[b]
                    if b == 0:
                        pe.wait_ge(dve_took, 1 + L(2 * (IN_V1 + 1), V_TOOK))
                        alone(rotk_ready, L(1, 1))
                    else:
                        pe.wait_ge(vtok_ready, L(b, NB))
                        alone(kz_ready, L(b, NB))
                    for bank, row, done in ((5, 2, rk_done), (4, 4, rv_done)):
                        for i in (0, 1):
                            mm = pe.transpose(banks[bank][0:n, i * P:(i + 1) * P], ret[:, row + i, t0:t0 + n],
                                              ident[:, :])
                        mm.then_inc(done, 1)
                    if b:
                        pe.wait_ge(inner_ready, L(b, NB))
                    alone(qm_ready, L(b + 1, NB))
                    for half in (0, 1):
                        mm = pe.matmul(banks[6][0:n, 0:RET_HEADS * P].rearrange("p (h n) -> p h n", n=P)[:, :, 0:n],
                                       ret[:, 2 + half, t0:t0 + n], qm[:, b % 2, half, :, 0:n],
                                       start=half == 0, stop=half == 1)
                    mm.then_inc(rs_done, 1)

                def ret_out(b):
                    t0, n = TB[b]
                    pe.wait_ge(vtok_ready, L(b + 1, NB))
                    pe.wait_ge(kz_ready, L(b + 1, NB))
                    if b > 0:
                        pe.wait_ge(ro_taken, L(b, NB))
                        pe.wait_ge(state_ready, L(b, NB))
                    if b == NB - 1:
                        pe.wait_ge(cache_landed, L(1, 1) * CACHES * 16)
                    alone(inner_ready, L(b + 1, NB))
                    state = None if b == 0 else st_s if b == NB - 1 else st_p
                    for hh in range(RET_HEADS):
                        c = P * (hh // 2)
                        out = banks[7][64 * (hh % 2):64 * (hh % 2) + 64, c:c + n]
                        e = slice(hh * HD, (hh + 1) * HD)
                        pe.matmul(out, vtok[0:n, b, e], inner[0:n, b % 2, hh, 0:n], start=True, stop=state is None)
                        if state is not None:
                            for half in (0, 1):
                                pe.matmul(out, state[:, half, e], qxi[:, half, t0:t0 + n], start=False, stop=half == 1)
                    for hh in range(RET_HEADS):
                        for half in (0, 1):
                            c = 2 * P + half * HD
                            mm = pe.matmul(banks[7][32 * hh:32 * hh + 32, c:c + HD],
                                           kz[0:n, b % 2, half * P + 32 * hh:half * P + 32 * hh + 32],
                                           vtok[0:n, b, hh * HD:(hh + 1) * HD], start=True, stop=True,
                                           tile_position=(0, 32 * hh))
                    mm.then_inc(ro_done, 1)

                def gn(i, var):
                    c, g = i // 2, i % 2
                    a, b_ = GROUPS[g]
                    bank = banks[4 + i][:, 0:b_ - a]
                    if not var:
                        pe.wait_ge(gt_taken, L(NB, NB))
                    else:
                        pe.wait_ge(gn_sq, L(i + 1, 4))
                    pe.matmul(bank, tab[:, TAB["blk"]:TAB["blk"] + P], (rsq if var else rT)[:, c, a:b_],
                              start=True, stop=True).then_inc(gn_var if var else gn_mean, 1)

                def gm_in(b):
                    t0, n = TB[b]
                    if b == 0:
                        pe.wait_ge(state_ready, L(NB, NB))
                        alone(curved, L(8, 12))
                    elif b == 4:
                        alone(gt_taken, L(b - 3, NB))
                    for i in (0, 1):
                        mm = pe.transpose(banks[4 + b % 4][0:n, i * P:(i + 1) * P], gv[:, i, t0:t0 + n], ident[:, :])
                    mm.then_inc(gt_done, 1)

                def gm_mix(b):
                    t0, n = TB[b]
                    if b == 0:
                        pe.wait_ge(gn_std, L(4, 4))
                    elif b == 4:
                        pe.wait_ge(b_ready, L(1, NB))
                    alone(gvt_ready, L(b + 1, NB))
                    for g4 in range(4):
                        mm = pe.matmul(banks[4 + b % 4][64 * (g4 % 2):64 * (g4 % 2) + 64,
                                                        (g4 // 2) * P:(g4 // 2) * P + n],
                                       gvt[0:n, b, g4 * HD:(g4 + 1) * HD],
                                       lp[0:n, LP["gw"] + g4 * P:LP["gw"] + g4 * P + n], start=True, stop=True)
                    mm.then_inc(mixed_done, 1)

                def v_tokens():
                    alone(b_ready, L(NB, NB))
                    for b in range(4):
                        mm = pe.transpose(banks[4][:, b * P:(b + 1) * P], vv[:, b * P:(b + 1) * P], ident[:, :])
                    mm.then_inc(vk_done, 1)
                    pe.transpose(banks[5][0:DEC, 0:P], vv[:, SEQ:T], ident[:, :]).then_inc(vk_done, 1)

                fill = {i: [] for i in range(IN_T)}
                for b in range(NB):
                    fill[6 + b].append(lambda b=b: ret_in(b))
                    fill[7 + b].insert(0, lambda b=b: ret_out(b))
                    fill[12].append(lambda b=b: gm_in(b))
                    fill[15].append(lambda b=b: gm_mix(b))
                fill[13].append(lambda: [gn(i, False) for i in range(4)])
                fill[14].append(lambda: [gn(i, True) for i in range(4)])
                fill[16].append(lambda: [stat(ST["b"] + g, g, gv[:, 0, :], 6 + g, [(b_ssq, L(1, 1))]) for g in (0, 1)])

                def between(n):
                    if n in (1, 2):
                        g = n - 1
                        pre_stat("pre_mix", L(SQ["start"] + 8 * (g + 1), SQS), g)

                head(S_IN, V_IN, dve_took, V_TOOK, (act_took, 1 + L(0, A_TOOK)), 1 + L(HR["pre_mix"], HRS),
                     1 + L(HR["pre_mix"] + 8, HRS), between, pairs=((0,), (1,), (2,), (3,)))
                for i in range(HEAD, IN_T):
                    tile(S_IN, V_IN, i, dve_took, V_TOOK)
                    for f in fill[i]:
                        f()

                def scores(u):
                    b, j = divmod(u, 4)
                    t0, n = TB[b]
                    k0, kn = WINDOW[b]
                    if u == 0:
                        alone(dve_took, 1 + L(2 * IN_T, V_TOOK))
                    elif u >= 2:
                        alone(p_ready, L(u - 1, UNITS))
                    if u == 0:
                        alone(cache_landed, L(1, 1) * CACHES * 16)
                    masked = b < NB - 1
                    for hh in (0, 1):
                        out = score_bank(u, hh)[0:n, 0:kn]
                        if masked:
                            pe.matmul(out, mask[:, 0:P], mask[:, P + 256 - kn:P + 256], start=True, stop=False)
                        mm = pe.matmul(out, qq[:, j, t0:t0 + n], kk[:, hh, k0:k0 + kn], start=not masked, stop=True)
                    mm.then_inc(s_done, 1)

                def turn(u):
                    b, j = divmod(u, 4)
                    t0, n = TB[b]
                    kn = WINDOW[b][1]
                    if u >= 2:
                        pe.wait_ge(pt_ready, L(u - 1, UNITS))
                    elif u == 0:
                        pe.wait_ge(vk_ready, L(2, 2))
                    alone(pn_ready, L(u + 1, UNITS))
                    for hh in (0, 1):
                        for kt in range((kn + P - 1) // P):
                            w = min(P, kn - kt * P)
                            mm = pe.transpose(banks[4 + u % 2][0:w, (hh * 2 + kt) * P:(hh * 2 + kt) * P + n],
                                              prob[0:n, u % 4, hh, kt * P:kt * P + w], ident[0:n, 0:n])
                    mm.then_inc(pt_done, 1)

                def values(u):
                    b, j = divmod(u, 4)
                    t0, n = TB[b]
                    kn = WINDOW[b][1]
                    if j == 0:
                        if b >= 2:
                            pe.wait_ge(a_taken, L(b - 1, NB))
                        if b == 0:
                            pe.wait_ge(ro_taken, L(NB, NB))
                            pe.wait_ge(state_ready, L(NB, NB))
                            pe.wait_ge(b_ready, L(NB, NB))
                            pe.wait_ge(std_ready, 1 + L(ST["b"] + 2, STS))
                        if b == 3:
                            pe.wait_ge(std_ready, 1 + L(ST["a"] + 1, STS))
                    alone(pt_ready, L(u + 1, UNITS))
                    for hh in (0, 1):
                        for kt in range((kn + P - 1) // P):
                            w = min(P, kn - kt * P)
                            mm = pe.matmul(banks[6 + b % 2][64 * hh:64 * hh + 64, j * P:j * P + n],
                                           vk[0:w, VTILES[b][kt], 64 * hh:64 * hh + 64],
                                           probT[0:w, u % 4, hh, kt, 0:n], start=kt == 0,
                                           stop=kt == (kn + P - 1) // P - 1, tile_position=(0, 64 * hh))
                    mm.then_inc(o_done, 1)

                def start_out(ns):
                    if 0 in ns:
                        pe.wait_ge(p_ready, L(UNITS, UNITS))
                        pe.wait_ge(nm_ready, L(UNITS, UNITS))
                        pe.wait_ge(lo_made, L(S_OUT + 2, SLOTS))
                        pe.wait_ge(h_ready, 1 + L(HR["merged"] + 12, HRS))
                    for n in ns:
                        for t in (0, 1):
                            mm = three(head_bank(t, 0), (S_OUT + t) % RING, K_OUT[n], K_OUT[n], 0, n == 0, n == KT - 1)
                            if n == KT - 1:
                                mm.then_inc(tile_done, 1)

                for u in range(UNITS + 5):
                    if u < UNITS:
                        scores(u)
                    if u == 1:
                        v_tokens()
                    if 3 <= u < UNITS + 3:
                        turn(u - 3)
                    if u >= 5:
                        values(u - 5)
                    if u in START_OUT:
                        start_out(START_OUT[u])
                    if u == A_AT:
                        stat(ST["a"], 0, acc, 7, [(a_ssq, L(2, NB))])

                def between(n):
                    if n == 0:
                        stat(ST["a"] + 1, 1, acc, 4, [(a_ssq, L(NB, NB)), (pt_ready, L(UNITS, UNITS))])

                head(S_OUT, A_OUT, act_took, A_TOOK, None, None, 1 + L(HR["merged"] + 12, HRS), between,
                     ks=K_OUT, late=4, started=True)
                for m in range(HEAD, OUT_T - 2):
                    tile(S_OUT, A_OUT, m, act_took, A_TOOK, ks=K_OUT)
                for g in (0, 1):
                    for m in (OUT_T - 2, OUT_T - 1):
                        tile(S_OUT, A_OUT, m, act_took, A_TOOK, ks=K_OUT, groups=(g,),
                             middle=(lambda: post_stat("post_mix", "mix", 0)) if m == OUT_T - 2 else None)

                def between(n):
                    if n in (1, 2):
                        pre_stat("pre_ffn", L(square_at("mix", "pre", n - 1, KT - 1) + 1, SQS), n - 1)

                head(S_GU, V_GU, dve_took, V_TOOK, (act_took, 1 + L(A_DN, A_TOOK)), 1 + L(HR["pre_ffn"], HRS),
                     1 + L(HR["pre_ffn"] + 8, HRS), between, early=lambda: post_stat("post_mix", "mix", 1))
                for t in (4, 5, 6, 7):
                    tile(S_GU, V_GU, t, dve_took, V_TOOK)
                with pe.Fori(0, FT // 2 - 2) as it:
                    for t in (8, 9, 10, 11):
                        pe.wait_ge(lo_made, L(S_GU + t + 1, SLOTS) + it * 4)
                        for g in (0, 1):
                            pe.wait_ge(dve_took, 1 + L(V_GU + order(t - 2, g) + 1, V_TOOK) + it * 8)
                            for k in range(KT):
                                mm = three(out_bank(t % 2, g), (S_GU + t) % RING, k, k, g, k == 0, k == KT - 1)
                            mm.then_inc(tile_done, 1)

                pe.wait_ge(hid_ready, L(2 * FT - 4, 2 * FT))
                pe.wait_ge(dve_took, 1 + L(V_TOOK - 2, V_TOOK))

                def down(m, k, g):
                    f = m * FT + k
                    s = S_DN + f // 8
                    if f % 8 == 0 and (g == 0 or m == KT - 1):
                        pe.wait_ge(lo_made, L(s + 1, SLOTS))
                    if m == 0 and k == FT - 2 and g == 0:
                        pe.wait_ge(hid_ready, L(2 * FT, 2 * FT))
                    if m == 1 and k == 0 and g == 0:
                        pe.wait_ge(dve_took, 1 + L(V_TOOK, V_TOOK))
                    if k == 0 and m >= 2:
                        pe.wait_ge(act_took, 1 + L(A_DN + 2 * (m - 2) + g + 1, A_TOOK))
                    mm = three(out_bank(m % 2, g), s % RING, f % 8, k, g, k == 0, k == FT - 1, hid_hi, hid_lo)
                    if k == FT - 1:
                        mm.then_inc(tile_done, 1)
                    elif f % 8 == 7 and g == 1:
                        mm.then_inc(dn_free, 1)

                for m in range(KT - 1):
                    for k in range(FT):
                        for g in (0, 1):
                            down(m, k, g)
                for g in (0, 1):
                    for k in range(FT):
                        down(KT - 1, k, g)
                        if g == 1 and k == 3:
                            post_stat("post_ffn", "ffn", 0)
                post_stat("post_ffn", "ffn", 1)

        @block.scalar
        def _(act):
            def fn(out, in_, f, **kw):
                return act.activation(out, in_, f, **kw)

            act.sem_inc(std_ready, 1)

            def split(s, off=0, l=0):
                r = s % RAW
                act.wait_ge(raw_landed[r], (l * (SLOTS // RAW) + (s // RAW + 1) + off // RAW) * 16)
                fn(w_hi[:, s % RING, :], raw[:, r, :], ACT.Copy).then_inc(hi_made, 1)

            def root(n, g, out, bank, count):
                act.wait_ge(stat_done, 2 + n)
                fn(out[:, cols(g)], banks[bank][:, 0:width(g)], ACT.Sqrt, bias=epsc[:, 0:1],
                   scale=1.0 / count).then_inc(std_ready, 1)

            def preload(f):
                i = [ACT.Sqrt, ACT.Exp, ACT.Silu].index(f)
                fn(scratch[:, i:i + 1], epsc[:, 0:1], f)

            def hi_of_x(g, k, name):
                c = SP[name] + k
                fn(h_hi[:, k, cols(g)], x[:, k, cols(g)], ACT.Copy, scale=sp[:, c:c + 1]).then_inc(hhi_ready, 1)

            act.wait_ge(ones_set, 1)
            act.wait_ge(small_landed, 16)
            for g in (0, 1):
                for k in range(KT):
                    if k % 4 == 0:
                        split(2 * g + k // 4)
                        act.wait_ge(x_landed[2 * g + k // 4], 16)
                    i = 8 * g + k
                    act.wait_ge(sq_added, 1 + max(i - 1, 0))
                    fn(sq[:, i % 2, 0:width(g)], x[:, k, cols(g)], ACT.Square).then_inc(sq_ready, 1)
                    hi_of_x(g, k, "pre_mix")
            with act.Fori(0, DEPTH) as l:

                def L(n, per):
                    return l * per + n

                def square_of(part, kind, g, k, src):
                    i = square_at(part, kind, g, k)
                    act.wait_ge(sq_added, 1 + L(i - 1, SQS))
                    fn(sq[:, i % 2, 0:width(g)], src, ACT.Square).then_inc(sq_ready, 1)

                def take_y(part, m, g, count, bank, y, name):
                    act.wait_ge(tile_done, 1 + L(count, 2 * TILES))
                    square_of(part, "post", g, m, bank)
                    c = SP[name] + m
                    fn(y[:, m, cols(g)], bank, ACT.Copy, scale=sp[:, c:c + 1]).then_inc(act_took, 1)

                def next_norm(part, post, pre, base, take_last, at):
                    late = LATE[part]
                    for g in (0, 1):
                        for k in range(KT):
                            i = 8 * g + k
                            for s in at.get(i, ()):
                                act.wait_ge(*slot_used(l, s))
                                split(s + RING, l=l)
                            if i == late:
                                take_last()
                            if i == late + 4:
                                root(L(ST[post] + 1, STS), 1, rstd, 5, D)
                            act.wait_ge(x_ready, 1 + L(base + i + 1, 32))
                            hi_of_x(g, k, pre)
                            square_of(part, "pre", g, k, x[:, k, cols(g)])

                root(L(ST["pre_mix"], STS), 0, rstd, 4, D)
                root(L(ST["pre_mix"] + 1, STS), 1, rstd, 4, D)

                def vtok_copy(b):
                    n = TB[b][1]
                    act.wait_ge(rv_done, L(b + 1, NB))
                    fn(vtok[0:n, b, :], banks[4][0:n, 0:256], ACT.Copy).then_inc(vtok_ready, 1)

                def gt_copy(b):
                    n = TB[b][1]
                    act.wait_ge(gt_done, L(b + 1, NB))
                    fn(gvt[0:n, b, :], banks[4 + b % 4][0:n, 0:256], ACT.Copy)\
                        .then_inc(gt_taken, 1)

                def gn_square(i):
                    c, g = i // 2, i % 2
                    act.wait_ge(gn_cent, L(i + 1, 4))
                    fn(rsq[:, c, cols(g)], rT[:, c, cols(g)], ACT.Square).then_inc(gn_sq, 1)

                def gn_root(i):
                    c, g = i // 2, i % 2
                    act.wait_ge(gn_var, L(i + 1, 4))
                    fn(rsq[:, c, cols(g)], banks[4 + i][:, 0:width(g)], ACT.Sqrt, bias=epsc[:, 0:1])\
                        .then_inc(gn_std, 1)

                def ln_root():
                    act.wait_ge(bn_ready, L(NB, NB))
                    n = TB[-1][1]
                    fn(brs[:, 0:NB - 1], bmv[:, 0:NB - 1, 1], ACT.Sqrt, bias=epsc[:, 0:1])
                    fn(brs[0:n, NB - 1:NB], bmv[0:n, NB - 1:NB, 1], ACT.Sqrt, bias=epsc[0:n, 0:1])\
                        .then_inc(ln_std, 1)

                def vk_copy():
                    act.wait_ge(vk_done, L(1, 2))
                    fn(vk[:, 0:4, :], banks[4][:, :].rearrange("p (i n) -> p i n", n=P), ACT.Copy)\
                        .then_inc(vk_ready, 1)
                    act.wait_ge(vk_done, L(2, 2))
                    fn(vk[0:DEC, 5, :], banks[5][0:DEC, 0:P], ACT.Copy).then_inc(vk_ready, 1)

                more = {i: [] for i in range(IN_T)}
                for b in range(NB):
                    more[6 + b].append(lambda b=b: vtok_copy(b))
                    more[12].append(lambda b=b: gt_copy(b))
                for i in range(4):
                    more[13].append(lambda i=i: gn_square(i))
                    more[14].append(lambda i=i: gn_root(i))
                more[12].append(ln_root)
                more[16].append(lambda: [root(L(ST["b"] + g, STS), g, gv[:, 0, :], 6 + g, 256) for g in (0, 1)])
                more[16].append(lambda: preload(ACT.Exp))

                for i in range(IN_T):
                    if i < HEAD:
                        act.wait_ge(*slot_used(l, S_IN + i))
                        split(S_IN + i + RING, l=l)
                    if IN_G0 <= i <= IN_UB1:
                        t, f = ((sg, ACT.Silu) if i <= IN_G1 else (gv, ACT.Gelu_apprx_tanh) if i <= IN_VB1 else
                                (ub, ACT.Gelu_apprx_tanh))
                        for g in (0, 1):
                            act.wait_ge(dve_took, 1 + L(2 * i + g + 1, V_TOOK))
                            fn(t[:, i % 2, cols(g)], t[:, i % 2, cols(g)], f).then_inc(curved, 1)
                    for f in more[i]:
                        f()
                    if HEAD <= i < IN_T - 1:
                        act.wait_ge(*slot_used(l, S_IN + i))
                        split(S_IN + i + RING, l=l)

                def exps(u):
                    b, j = divmod(u, 4)
                    n, kn = TB[b][1], WINDOW[b][1]
                    act.wait_ge(nm_ready, L(u + 1, UNITS))
                    for hh in (0, 1):
                        fn(prob[0:n, u % 4, hh, 0:kn], score_bank(u, hh)[0:n, 0:kn], ACT.Exp,
                           bias=nm[0:n, u % 2, hh:hh + 1], scale=SCALE, accum_out=den[0:n, u % 2, hh:hh + 1])
                    fn(es[0:n, u % 2, :], sm[0:n, u % 2, :], ACT.Exp).then_inc(p_ready, 1)

                def turned(u):
                    b = u // 4
                    n, kn = TB[b][1], WINDOW[b][1]
                    act.wait_ge(pt_done, L(u + 1, UNITS))
                    bank = banks[4 + u % 2][:, :].rearrange("p (h k n) -> p h k n", h=2, k=2)
                    for kt in range((kn + P - 1) // P):
                        w = min(P, kn - kt * P)
                        last = fn(probT[0:w, u % 4, :, kt, 0:n], bank[0:w, :, kt, 0:n], ACT.Copy)
                    last.then_inc(pt_ready, 1)

                def outs(b):
                    t0, n = TB[b]
                    act.wait_ge(o_done, L(4 * b + 4, UNITS))
                    fn(aT[:, :, t0:t0 + n], grid(b, banks[6 + b % 2][:, :], 4), ACT.Copy)
                    if b:
                        act.wait_ge(a_ssq, L(b, NB))
                    fn(sqa[:, :, 0:n], grid(b, banks[6 + b % 2][:, :], 4), ACT.Square).then_inc(a_taken, 1)

                def hi_of_merged(n):
                    g, k = MERGED[n]
                    act.wait_ge(prod_ready, L(n + 1, 2 * KT))
                    fn(h_hi[:, k, cols(g)], h_whole[:, k, cols(g)], ACT.Copy).then_inc(hhi_ready, 1)

                for u in range(UNITS + 5):
                    if u < UNITS:
                        exps(u)
                    if u == 1:
                        vk_copy()
                    if u == SPLIT_AT:
                        split(S_IN + IN_T - 1 + RING, l=l)
                    if 3 <= u < UNITS + 3:
                        turned(u - 3)
                    if u >= 5 and (u - 5) % 4 == 3:
                        outs((u - 5) // 4)
                    if u == A_AT:
                        root(L(ST["a"], STS), 0, acc, 7, SWA_HEADS * HD)
                    if u == UNITS:
                        preload(ACT.Sqrt)
                    for n in MERGED_AT.get(u, ()):
                        hi_of_merged(n)
                root(L(ST["a"] + 1, STS), 1, acc, 4, SWA_HEADS * HD)
                for n in range(12, 2 * KT):
                    hi_of_merged(n)

                def out_tile(m, g):
                    take_y("mix", m, g, 2 * S_OUT + out_order(m, g) + 1, tile_bank(m, g), y_mix, "post_mix")

                for g in (0, 1):
                    for m in range(HEAD):
                        out_tile(m, g)
                        if g == 1:
                            split(S_OUT + m + RING, l=l)
                for m in range(HEAD, OUT_T - 2):
                    for g in (0, 1):
                        out_tile(m, g)
                    split(S_OUT + m + RING, l=l)
                out_tile(OUT_T - 2, 0)
                out_tile(OUT_T - 1, 0)
                root(L(ST["post_mix"], STS), 0, rstd, 4, D)
                out_tile(OUT_T - 2, 1)
                split(S_OUT + OUT_T - 2 + RING, l=l)

                def last_out():
                    out_tile(OUT_T - 1, 1)
                    split(S_OUT + OUT_T - 1 + RING, l=l)

                next_norm("mix", "post_mix", "pre_ffn", 0, last_out, {})
                for g in (0, 1):
                    root(L(ST["pre_ffn"] + g, STS), g, rstd, 4, D)
                preload(ACT.Silu)

                def silu(gate, g):
                    act.wait_ge(dve_took, 1 + L(V_GU + order(2 * gate, g) + 1, V_TOOK))
                    t = gate_whole[:, gate, cols(g)]
                    fn(t, t, ACT.Silu).then_inc(silu_ready, 1)

                def hid_split(gate, g, n):
                    act.wait_ge(hid_prod, L(n + 1, 2 * FT))
                    fn(hid_hi[:, gate, cols(g)], hid_whole[:, gate, cols(g)], ACT.Copy)\
                        .then_inc(hid_hi_ready, 1)

                for g in (0, 1):
                    if g == 1:
                        for t in (0, 1):
                            act.wait_ge(*slot_used(l, S_GU + t))
                            split(S_GU + t + RING, l=l)
                    for gate in (0, 1):
                        silu(gate, g)
                    for gate in (0, 1):
                        hid_split(gate, g, 2 * g + gate)
                for t in (2, 3):
                    act.wait_ge(*slot_used(l, S_GU + t))
                    split(S_GU + t + RING, l=l)
                with act.Fori(0, FT // 2 - 1) as it:
                    for i in (0, 1):
                        t = HEAD + 2 * i
                        gate = ds(it * 2 + (2 + i), 1)
                        for g in (0, 1):
                            act.wait_ge(dve_took, 1 + L(V_GU + 2 * t + g + 1, V_TOOK) + it * 8)
                            h = gate_whole[:, gate, cols(g)]
                            fn(h, h, ACT.Silu).then_inc(silu_ready, 1)
                        for d in (0, 1):
                            act.wait_ge(tile_done, 1 + L(2 * (S_GU + t + d + 1), 2 * TILES) + it * 8)
                            split(S_GU + t + d + RING, off=it * 4, l=l)
                        for g in (0, 1):
                            act.wait_ge(hid_prod, L(t + g + 1, 2 * FT) + it * 4)
                            fn(hid_hi[:, gate, cols(g)], hid_whole[:, gate, cols(g)], ACT.Copy)\
                                .then_inc(hid_hi_ready, 1)

                def down_tile(m, g):
                    take_y("ffn", m, g, 2 * (TILES - KT + m) + g + 1, out_bank(m % 2, g), y_ffn, "post_ffn")

                preload(ACT.Sqrt)
                for s in range(S_DN, S_LAST):
                    a, b = 8 * (s - S_DN), 8 * (s - S_DN) + 8
                    act.wait_ge(*slot_used(l, s))
                    split(s + RING, l=l)
                    for m in range(KT - 1):
                        if a <= m * FT + FT - 1 < b:
                            for g in (0, 1):
                                down_tile(m, g)
                for m in range(8 * (S_LAST - S_DN) // FT, KT - 1):
                    for g in (0, 1):
                        down_tile(m, g)
                down_tile(KT - 1, 0)
                root(L(ST["post_ffn"], STS), 0, rstd, 4, D)

                def last_down():
                    down_tile(KT - 1, 1)
                    act.wait_ge(*slot_used(l, SLOTS - 1))
                    split(SLOTS - 1 + RING, l=l)

                next_norm("ffn", "post_ffn", "next_mix", 16, last_down, SPLITS_AT)

        @block.vector
        def _(dve):
            def split(s, off=0, l=0):
                dve.wait_ge(hi_made, l * SLOTS + (s + 1) + off)
                dve.tensor_tensor(w_lo[:, s % RING, :], raw[:, s % RAW, :],
                                  w_hi[:, s % RING, :].bitcast(F32), ALU.subtract).then_inc(lo_made, 1)

            def lo_of_x(g, k, name, count):
                dve.wait_ge(hhi_ready, count)
                c = SP[name] + k
                dve.scalar_tensor_tensor(out=h_lo[:, k, cols(g)], in0=x[:, k, cols(g)], scalar=sp[:, c:c + 1],
                                         in1=h_hi[:, k, cols(g)].bitcast(F32),
                                         op0=ALU.mult, op1=ALU.subtract).then_inc(h_ready, 1)

            dve.sem_inc(x_ready, 1)
            dve.sem_inc(h_ready, 1)
            dve.memset(ones[:, :], 1.0).then_inc(dve_chain, 1)
            dve.memset(st_p[:, :, :], 0.0)
            dve.memset(epsc[:, :], EPS).then_inc(ones_set, 1)
            for g in (0, 1):
                for k in range(KT):
                    if k % 4 == 0:
                        split(2 * g + k // 4)
                    lo_of_x(g, k, "pre_mix", 8 * g + k + 1)
            with dve.Fori(0, DEPTH) as l:
                links = [0]

                def L(n, per):
                    return l * per + n

                def link(last):
                    links[0] += 1
                    last.then_inc(dve_chain, 1)
                    dve.wait_ge(dve_chain, l * DVE_LINKS + (links[0] + 1))

                def recip(n, g, t):
                    dve.wait_ge(std_ready, 2 + L(n, STS))
                    link(dve.reciprocal(t[:, cols(g)], t[:, cols(g)]))

                def take(count, out, bank, g):
                    dve.wait_ge(tile_done, 1 + count)
                    return dve.tensor_tensor(out, bank, rstd[:, cols(g)], ALU.mult)

                def residual(part, post, pre, base, y, at):
                    for g in (0, 1):
                        if g == 1:
                            for s in at.get(KT, ()):
                                split(s + RING, l=l)
                        recip(ST[post] + g, g, rstd)
                        if g == 0:
                            dve.wait_ge(x_ready, 1 + L(base, 32))
                        lag = 4 if g == 1 and part == "ffn" else 2
                        for k in range(0, KT + lag, 2):
                            i = 8 * g + k
                            if k < KT:
                                if i:
                                    dve.wait_ge(x_ready, 1 + L(base + i, 32))
                                two = slice(k, k + 2)
                                link(dve.tensor_tensor(tp[:, :, 0:width(g)], y[:, two, cols(g)],
                                                       rstd[:, cols(g)].unsqueeze(1).to_broadcast([P, 2, width(g)]),
                                                       ALU.mult))
                                dve.tensor_tensor(x[:, two, cols(g)], x[:, two, cols(g)], tp[:, :, 0:width(g)],
                                                  ALU.add).then_inc(x_ready, 2)
                                for s in at.get(i, ()) if i < KT else ():
                                    split(s + RING, l=l)
                            if i == 0:
                                behind = (0, 1)
                            elif k - lag >= (2 if g == 0 else 0):
                                behind = (k - lag, k - lag + 1)
                            else:
                                behind = ()
                            for d in behind:
                                lo_of_x(g, d, pre, L(HR[pre] + 8 * g + d + 1, HRS))

                dve.wait_ge(small_landed, L(2, 1) * 16)
                dve.tensor_scalar(nsink[:, :], sp[:, SP["sink"]:SP["sink"] + 8], -1.0, None, ALU.mult)\
                   .then_inc(nsink_ready, 1)

                def table(name, w, n=P):
                    return tab[0:n, TAB[name]:TAB[name] + w]

                def rotate_q():
                    dve.wait_ge(tab_landed, L(1, 1) * 16)
                    dve.wait_ge(dve_took, 1 + L(2 * HEAD, V_TOOK))
                    A, B = ret[:, 0, :], ret[:, 1, :]
                    dve.tensor_tensor(rtmp[:, 0, :], A, table("sin", T), ALU.mult)
                    link(dve.tensor_tensor(rtmp[:, 1, :], B, table("sin", T), ALU.mult))
                    dve.tensor_tensor(A, A, table("cos", T), ALU.mult)
                    link(dve.tensor_tensor(B, B, table("cos", T), ALU.mult))
                    dve.tensor_tensor(A, A, rtmp[:, 1, :], ALU.subtract)
                    link(dve.tensor_tensor(B, B, rtmp[:, 0, :], ALU.add))
                    xi = table("xi", P)
                    for half in (0, 1):
                        dve.tensor_tensor(qxi[:, half, 0:SEQ].rearrange("p (b n) -> p b n", n=P),
                                          ret[:, half, 0:SEQ].rearrange("p (b n) -> p b n", n=P),
                                          xi.unsqueeze(1).to_broadcast([P, 4, P]), ALU.mult)
                        last = dve.tensor_tensor(qxi[:, half, SEQ:T], ret[:, half, SEQ:T], xi[:, 0:DEC], ALU.mult)
                    last.then_inc(rotq_ready, 1)

                def decay(b):
                    n = TB[b][1]
                    if b >= 2:
                        dve.wait_ge(ro_done, L(b - 1, NB))
                    if b == 0:
                        dve.wait_ge(rest_landed, L(1, 1) * 32)
                        gw = lp[CHUNK:P, LP["gw"]:LP["gw"] + 4 * P].rearrange("p (g i) -> p g i", i=P)
                        dve.memset(gw[:, :, 0:CHUNK], 0.0)
                    dve.wait_ge(rk_done, L(b + 1, NB))
                    dve.tensor_tensor(kz[0:n, b % 2, :], banks[5][0:n, 0:256],
                                      table("zeta" if b < NB - 1 else "zetas", 256, n), ALU.mult).then_inc(kz_ready, 1)
                    dve.wait_ge(rs_done, L(b + 1, NB))
                    dve.tensor_tensor(inner[0:n, b % 2, :, 0:n], grid(b, banks[6][0:n, :], 4),
                                      grid(b, table("decay", 512, n), 4), ALU.mult).then_inc(inner_ready, 1)

                def state(b):
                    t0, n = TB[b]
                    dve.wait_ge(ro_done, L(b + 1, NB))
                    dve.tensor_copy(rT[:, :, t0:t0 + n], grid(b, banks[7][:, 0:2 * P], 2)).then_inc(ro_taken, 1)
                    if b:
                        dve.wait_ge(state_ready, L(b, NB))
                    st = st_s if b == NB - 1 else st_p
                    c = TAB["cdec"] + (b == NB - 1)
                    for hh in range(RET_HEADS):
                        r = slice(32 * hh, 32 * hh + 32)
                        new = banks[7][r, 2 * P:3 * P].rearrange("p (h d) -> p h d", h=2)
                        old = st[r, :, hh * HD:(hh + 1) * HD]
                        if b == 0:
                            last = dve.tensor_copy(old, new)
                        else:
                            last = dve.scalar_tensor_tensor(out=old, in0=old, scalar=tab[r, c:c + 1], in1=new,
                                                            op0=ALU.mult, op1=ALU.add)
                    last.then_inc(state_ready, 1)

                def bn(b):
                    n = TB[b][1]
                    dve.wait_ge(gt_taken, L(b + 1, NB))
                    link(dve.bn_stats(bst[0:n, b, :], gvt[0:n, b, :]))
                    dve.sem_inc(dve_passed, 1)
                    dve.bn_aggr(bmv[0:n, b, :], bst[0:n, b, :]).then_inc(bn_ready, 1)

                def centre(i):
                    c, g = i // 2, i % 2
                    dve.wait_ge(gn_mean, L(i + 1, 4))
                    dve.tensor_tensor(rT[:, c, cols(g)], rT[:, c, cols(g)], banks[4 + i][:, 0:width(g)],
                                      ALU.subtract).then_inc(gn_cent, 1)

                def scale_r(i):
                    c, g = i // 2, i % 2
                    dve.wait_ge(gn_std, L(i + 1, 4))
                    link(dve.reciprocal(rsq[:, c, cols(g)], rsq[:, c, cols(g)]))
                    dve.tensor_tensor(rT[:, c, cols(g)], rT[:, c, cols(g)], rsq[:, c, cols(g)], ALU.mult)\
                       .then_inc(c_ready, 1)

                def v_rows():
                    dve.wait_ge(ln_std, L(1, 1))
                    dve.wait_ge(gt_taken, L(NB, NB))
                    n = TB[-1][1]
                    dve.reciprocal(brs[:, 0:NB - 1], brs[:, 0:NB - 1])
                    link(dve.reciprocal(brs[0:n, NB - 1:NB], brs[0:n, NB - 1:NB]))
                    for b in range(NB):
                        n = TB[b][1]
                        last = dve.scalar_tensor_tensor(out=gvt[0:n, b, :], in0=gvt[0:n, b, :], scalar=bmv[0:n, b, 0:1],
                                                        in1=lp[0:n, LP["lng"]:LP["lng"] + 256],
                                                        op0=ALU.subtract, op1=ALU.mult)
                    link(last)
                    for b in range(NB):
                        n = TB[b][1]
                        dve.scalar_tensor_tensor(out=gvt[0:n, b, :], in0=gvt[0:n, b, :], scalar=brs[0:n, b:b + 1],
                                                 in1=lp[0:n, LP["lnb"]:LP["lnb"] + 256],
                                                 op0=ALU.mult, op1=ALU.add).then_inc(gvt_ready, 1)

                def gate_b(b):
                    t0, n = TB[b]
                    dve.wait_ge(mixed_done, L(b + 1, NB))
                    bank = banks[4 + b % 4][:, 0:2 * P]
                    if b == 0:
                        dve.wait_ge(curved, L(12, 12))
                    link(dve.tensor_tensor(gv[:, :, t0:t0 + n], grid(b, bank, 2),
                                           grid(b, lp[:, LP["gb"]:LP["gb"] + 256], 2), ALU.add))
                    dve.tensor_tensor(ub[:, :, t0:t0 + n], ub[:, :, t0:t0 + n], gv[:, :, t0:t0 + n],
                                      ALU.mult).then_inc(b_ready, 1)

                more = {i: [] for i in range(IN_T)}
                for b in range(NB):
                    more[7 + b].append(lambda b=b: state(b))
                    more[6 + b].append(lambda b=b: decay(b))
                    more[12].append(lambda b=b: bn(b))
                    more[15].append(lambda b=b: gate_b(b))
                for i in range(4):
                    more[13].append(lambda i=i: centre(i))
                for i in range(3):
                    more[14].append(lambda i=i: scale_r(i))
                more[13].append(v_rows)
                more[15].append(lambda: scale_r(3))
                more[16].append(lambda: [recip(ST["b"] + g, g, gv[:, 0, :]) for g in (0, 1)])

                def in_tile(i, g):
                    count, bank = L(order(i, g) + 1, 2 * TILES), tile_bank(i, g)
                    if i == IN_K:
                        dve.wait_ge(tile_done, 1 + count)
                        for a, b in seg(g):
                            r = slice(GROUPS[g][0] + a.start, GROUPS[g][0] + a.stop)
                            for hh in (0, 1):
                                rows = slice(64 * hh, 64 * hh + 64)
                                last = dve.tensor_tensor(kk[rows, hh, b], bank[rows, a], rstd[rows, r], ALU.mult)
                    else:
                        if i <= IN_V1:
                            out = ret[:, i, cols(g)]
                            if i in (IN_KA, IN_KB):
                                dve.wait_ge(tile_done, 1 + count)
                                dve.scalar_tensor_tensor(out=out, in0=bank, scalar=SCALE, in1=rstd[:, cols(g)],
                                                         op0=ALU.mult, op1=ALU.mult).then_inc(dve_took, 1)
                                return
                        elif i <= IN_UB1:
                            out = (sg if i <= IN_G1 else gv if i <= IN_VB1 else ub)[:, i % 2, cols(g)]
                        elif i == IN_V:
                            out = vv[:, cols(g)]
                        else:
                            out = qq[:, i - IN_Q0, cols(g)]
                        last = take(count, out, bank, g)
                    last.then_inc(dve_took, 1)

                for g in (0, 1):
                    recip(ST["pre_mix"] + g, g, rstd)
                    for i in range(HEAD):
                        in_tile(i, g)
                        if g == 1:
                            split(S_IN + i + RING, l=l)
                rotate_q()
                for i in range(HEAD, IN_T):
                    for g in (0, 1):
                        in_tile(i, g)
                    for f in more[i]:
                        f()
                    if i < IN_T - 1:
                        split(S_IN + i + RING, l=l)

                dve.wait_ge(nsink_ready, L(1, 1))

                def maxima(u):
                    b, j = divmod(u, 4)
                    n, kn = TB[b][1], WINDOW[b][1]
                    dve.wait_ge(s_done, L(u + 1, UNITS))
                    i = 2 * (u % 2)
                    bank = psum[0:n, i:i + 2, 0:kn]
                    ns = nsink[0:n, 2 * j:2 * j + 2]
                    if u >= 2:
                        dve.wait_ge(nm_ready, L(u - 1, UNITS))
                    link(dve.tensor_reduce(mx[0:n, u % 2, :], bank, AX.X, ALU.max))
                    link(dve.scalar_tensor_tensor(out=nm[0:n, u % 2, :], in0=mx[0:n, u % 2, :], scalar=-SCALE,
                                                  in1=ns, op0=ALU.mult, op1=ALU.min))
                    dve.tensor_tensor(sm[0:n, u % 2, :], nm[0:n, u % 2, :], ns, ALU.subtract).then_inc(nm_ready, 1)

                def normalise(u):
                    b = u // 4
                    n, kn = TB[b][1], WINDOW[b][1]
                    dve.wait_ge(p_ready, L(u + 1, UNITS))
                    if u >= 2:
                        dve.wait_ge(pn_ready, L(u - 1, UNITS))
                    link(dve.tensor_tensor(rd[0:n, u % 2, :], den[0:n, u % 2, :], es[0:n, u % 2, :], ALU.add))
                    link(dve.reciprocal(rd[0:n, u % 2, :], rd[0:n, u % 2, :]))
                    for hh in (0, 1):
                        last = dve.tensor_scalar(prob[0:n, u % 4, hh, 0:kn], prob[0:n, u % 4, hh, 0:kn],
                                                 rd[0:n, u % 2, hh:hh + 1], None, ALU.mult)
                    last.then_inc(pn_ready, 1)

                def merged(n):
                    g, k = MERGED[n]
                    if k < 4:
                        src, c, scale = aT[:, k, cols(g)], SP["na"] + k, acc[:, cols(g)]
                    elif k < 6:
                        src, c, scale = ub[:, k - 4, cols(g)], SP["nb"] + k - 4, gv[:, 0, cols(g)]
                    else:
                        src, c, scale = rT[:, k - 6, cols(g)], SP["rg"] + k - 6, sg[:, k - 6, cols(g)]
                    dve.scalar_tensor_tensor(out=h_whole[:, k, cols(g)], in0=src, scalar=sp[:, c:c + 1],
                                             in1=scale, op0=ALU.mult, op1=ALU.mult).then_inc(prod_ready, 1)

                def lo_of_merged(n):
                    g, k = MERGED[n]
                    dve.wait_ge(hhi_ready, L(HR["merged"] + n + 1, HRS))
                    dve.tensor_tensor(h_lo[:, k, cols(g)], h_whole[:, k, cols(g)],
                                      h_hi[:, k, cols(g)].bitcast(F32), ALU.subtract).then_inc(h_ready, 1)

                for u in range(UNITS + 1):
                    if u < UNITS:
                        maxima(u)
                    if u == SPLIT_AT:
                        split(S_IN + IN_T - 1 + RING, l=l)
                    if u:
                        normalise(u - 1)
                    if u - 1 in MERGED_AT:
                        for n in MERGED_AT[u - 1]:
                            lo_of_merged(n)
                    if u in MERGED_AT:
                        if u == min(MERGED_AT):
                            dve.wait_ge(c_ready, L(3, 4))
                        if u == max(v for v in MERGED_AT if v < A_AT):
                            dve.wait_ge(c_ready, L(4, 4))
                        if u == A_AT + 1:
                            recip(ST["a"], 0, acc)
                        for n in MERGED_AT[u]:
                            merged(n)
                recip(ST["a"] + 1, 1, acc)
                for n in range(12, 2 * KT):
                    merged(n)
                for n in range(12, 2 * KT):
                    lo_of_merged(n)

                for m in range(OUT_T - 2):
                    split(S_OUT + m + RING, l=l)
                residual("mix", "post_mix", "pre_ffn", 0, y_mix, {0: (S_OUT + OUT_T - 2,), KT: (S_OUT + OUT_T - 1,)})

                def gate_up(t, g):
                    out = (gate_whole, hid_whole)[t % 2][:, t // 2, cols(g)]
                    take(L(2 * S_GU + order(t, g) + 1, 2 * TILES), out, head_bank(t, g), g).then_inc(dve_took, 1)

                dve.wait_ge(out_landed, L(NOUT, NOUT) * 16)
                for g in (0, 1):
                    recip(ST["pre_ffn"] + g, g, rstd)
                    if g == 1:
                        for t in (0, 1):
                            split(S_GU + t + RING, l=l)
                    for t in range(HEAD):
                        gate_up(t, g)
                    for gate in (0, 1):
                        n = 2 * g + gate
                        dve.wait_ge(silu_ready, L(n + 1, 2 * FT))
                        dve.wait_ge(dve_took, 1 + L(V_GU + order(2 * gate + 1, g) + 1, V_TOOK))
                        t = hid_whole[:, gate, cols(g)]
                        dve.tensor_tensor(t, t, gate_whole[:, gate, cols(g)], ALU.mult).then_inc(hid_prod, 1)
                    for gate in (0, 1):
                        dve.wait_ge(hid_hi_ready, L(2 * g + gate + 1, 2 * FT))
                        dve.tensor_tensor(hid_lo[:, gate, cols(g)], hid_whole[:, gate, cols(g)],
                                          hid_hi[:, gate, cols(g)].bitcast(F32), ALU.subtract)\
                           .then_inc(hid_ready, 1)
                for t in (2, 3):
                    split(S_GU + t + RING, l=l)
                with dve.Fori(0, FT // 2 - 1) as it:
                    for i in (0, 1):
                        t = HEAD + 2 * i
                        gate = ds(it * 2 + (2 + i), 1)

                        def part(buf, g):
                            return buf[:, gate, cols(g)]

                        for d, buf in ((0, gate_whole), (1, hid_whole)):
                            for g in (0, 1):
                                dve.wait_ge(tile_done, 1 + L(2 * (S_GU + t + d) + g + 1, 2 * TILES) + it * 8)
                                dve.tensor_tensor(part(buf, g), out_bank(d, g).unsqueeze(1),
                                                  rstd[:, cols(g)].unsqueeze(1), ALU.mult).then_inc(dve_took, 1)
                            if d == 0:
                                split(S_GU + t + RING, off=it * 4, l=l)
                        for g in (0, 1):
                            dve.wait_ge(silu_ready, L(t + g + 1, 2 * FT) + it * 4)
                            dve.wait_ge(dve_took, 1 + L(V_GU + 2 * (t + 1) + g + 1, V_TOOK) + it * 8)
                            dve.tensor_tensor(part(hid_whole, g), part(hid_whole, g), part(gate_whole, g), ALU.mult)\
                               .then_inc(hid_prod, 1)
                        split(S_GU + t + 1 + RING, off=it * 4, l=l)
                        for g in (0, 1):
                            dve.wait_ge(hid_hi_ready, L(t + g + 1, 2 * FT) + it * 4)
                            dve.tensor_tensor(part(hid_lo, g), part(hid_whole, g), part(hid_hi, g).bitcast(F32),
                                              ALU.subtract)\
                               .then_inc(hid_ready, 1)

                for s in range(S_DN, S_LAST):
                    split(s + RING, l=l)
                residual("ffn", "post_ffn", "next_mix", 16, y_ffn, LO_AT)
                assert links[0] == DVE_LINKS, links[0]

        @block.gpsimd
        def _(pool):
            pool.sem_inc(sq_added, 1)
            pool.dma_start(sp[:, :], small[0]).then_inc(small_landed, 16)
            pool.dma_start(ident[:, :], ident_d).then_inc(const_landed, 16)
            pool.dma_start(mask[:, :], mask_d).then_inc(const_landed, 16)

            def add_square(n, count, g, first, stats):
                pool.wait_ge(sq_ready, count + 1)
                buf = sq[:, n % 2, 0:width(g)]
                if first:
                    if stats is not None:
                        pool.wait_ge(stat_done, 1 + stats)
                        pool.sem_inc(pool_passed, 1)
                    pool.tensor_copy(acc[:, cols(g)], buf).then_inc(sq_added, 1)
                else:
                    pool.wait_ge(sq_added, 1 + count)
                    pool.tensor_tensor(acc[:, cols(g)], acc[:, cols(g)], buf, ALU.add).then_inc(sq_added, 1)

            for n in range(2 * KT):
                add_square(n, n, n // KT, n % KT == 0, None)
            with pool.Fori(0, DEPTH) as l:
                links = [0]

                def L(n, per):
                    return l * per + n

                def link(last):
                    links[0] += 1
                    last.then_inc(pool_chain, 1)
                    pool.wait_ge(pool_chain, l * POOL_LINKS + links[0])

                def alone(s, v):
                    pool.wait_ge(s, v)
                    pool.sem_inc(pool_passed, 1)

                def states(dram):
                    return dram[ds(l, 1)].rearrange("o p h d -> (o p) h d")

                def layer(dram):
                    return dram[ds(l, 1)].rearrange("o p n -> (o p) n")

                pool.wait_ge(ones_set, 1)
                alone(h_ready, 1 + L(HR["pre_mix"] + 16, HRS))
                pool.dma_start(sp[:, :], layer(small)).then_inc(small_landed, 16)
                alone(tile_done, 1 + L(0, 2 * TILES))
                link(pool.memset(st_s[:, :, :], 0.0))
                for hh in (0, 1):
                    pool.sem_inc(pool_passed, 1)
                    link(pool.memset(kk[64 - 64 * hh:128 - 64 * hh, hh, :], 0.0))
                pool.sem_inc(pool_passed, 1)
                pool.dma_start(tab[:, 0:TAB_FIRST], tabs[:, 0:TAB_FIRST]).then_inc(tab_landed, 16)
                for hh in (0, 1):
                    r = slice(64 * hh, 64 * hh + 64)
                    pool.dma_start(kk[r, hh, SEQ:SEQ + P], layer(kcache)[r]).then_inc(cache_landed, 16)
                pool.dma_start(vk[:, 4, :], layer(vcache)).then_inc(cache_landed, 16)
                for hh in range(RET_HEADS):
                    r = slice(32 * hh, 32 * hh + 32)
                    pool.dma_start(st_s[r, :, hh * HD:(hh + 1) * HD], states(ret0)[r]).then_inc(cache_landed, 16)

                def add_squares(part):
                    post = ST["post_mix"] if part == "mix" else ST["post_ffn"]
                    for n, (kind, g, k) in enumerate(SQUARES[part]):
                        n += SQ[part]
                        stats = post if kind == "post" else post + g + 1
                        add_square(n, L(n, SQS), g, k == 0, L(stats, STS))

                pool.wait_ge(tab_landed, L(1, 1) * 16)
                alone(dve_took, 1 + L(2 * HEAD, V_TOOK))
                pool.dma_start(tab[:, TAB_FIRST:TAB_N], tabs[:, TAB_FIRST:TAB_N]).then_inc(rest_landed, 16)
                pool.dma_start(lp[:, :], layer(lpar)).then_inc(rest_landed, 16)
                A, B = ret[:, 2, :], ret[:, 3, :]
                cos, sin = (tab[:, TAB[name]:TAB[name] + T] for name in ("cos", "sin"))
                pool.tensor_tensor(ptmp[:, 0, :], A, sin, ALU.mult)
                link(pool.tensor_tensor(ptmp[:, 1, :], B, sin, ALU.mult))
                pool.tensor_tensor(A, A, cos, ALU.mult)
                link(pool.tensor_tensor(B, B, cos, ALU.mult))
                pool.tensor_tensor(A, A, ptmp[:, 1, :], ALU.subtract)
                pool.tensor_tensor(B, B, ptmp[:, 0, :], ALU.add).then_inc(rotk_ready, 1)

                head = tab[:, TAB["head"]:TAB["head"] + RET_HEADS].unsqueeze(2)
                pool.wait_ge(rotq_ready, L(1, 1))
                for b in range(NB):
                    t0, n = TB[b]
                    if b >= 2:
                        pool.wait_ge(rs_done, L(b - 1, NB))
                    for half in (0, 1):
                        last = pool.tensor_tensor(qm[:, b % 2, half, :, 0:n],
                                                  ret[:, half, t0:t0 + n].unsqueeze(1).to_broadcast([P, RET_HEADS, n]),
                                                  head.to_broadcast([P, RET_HEADS, n]), ALU.mult)
                    last.then_inc(qm_ready, 1)

                alone(state_ready, L(NB, NB))
                for hh in range(RET_HEADS):
                    r = slice(32 * hh, 32 * hh + 32)
                    for dram, st in ((o_rp, st_p), (o_rs, st_s)):
                        pool.dma_start(states(dram)[r], st[r, :, hh * HD:(hh + 1) * HD]).then_inc(out_landed, 16)
                alone(gvt_ready, L(NB, NB))
                pool.dma_start(layer(o_gv), gvt[0:DEC, NB - 1, :]).then_inc(out_landed, 16)
                alone(dve_took, 1 + L(2 * (IN_V + 1), V_TOOK))
                W = P + DEC
                for hh in (0, 1):
                    r = slice(64 * hh, 64 * hh + 64)
                    for dram, t, end in ((o_k, kk[r, hh, :], KC), (o_v, vv[r, :], T)):
                        pool.dma_start(layer(dram)[r, 0:P], t[:, SEQ - P:SEQ]).then_inc(out_landed, 16)
                        pool.dma_start(layer(dram)[r, P:W], t[:, end - DEC:end]).then_inc(out_landed, 16)

                pool.wait_ge(b_ready, L(NB, NB))
                link(pool.tensor_tensor(gv[:, :, :], ub[:, :, :], ub[:, :, :], ALU.mult))
                pool.tensor_tensor(gv[:, 0, :], gv[:, 0, :], gv[:, 1, :], ALU.add).then_inc(b_ssq, 1)
                for b in range(NB):
                    t0, n = TB[b]
                    pool.wait_ge(a_taken, L(b + 1, NB))
                    link(pool.tensor_tensor(acc[:, t0:t0 + n], sqa[:, 0, 0:n], sqa[:, 1, 0:n], ALU.add))
                    link(pool.tensor_tensor(acc[:, t0:t0 + n], acc[:, t0:t0 + n], sqa[:, 2, 0:n], ALU.add))
                    pool.tensor_tensor(acc[:, t0:t0 + n], acc[:, t0:t0 + n], sqa[:, 3, 0:n], ALU.add)\
                        .then_inc(a_ssq, 1)

                add_squares("mix")
                add_squares("ffn")
                assert links[0] == POOL_LINKS, links[0]


IN_SPLITS = (512, 128, 128, 256, 256, 256, 256, 256, 256)


def in_columns():
    qa, ka, va, ub, vb, qc, kc, vc, gc = (int(v) for v in np.cumsum((0,) + IN_SPLITS[:-1]))
    half = lambda o, h: np.concatenate([o + HD * r + 32 * h + np.arange(32) for r in range(RET_HEADS)])
    run = lambda o, n: np.arange(o, o + n)
    pairs = [np.concatenate([qa + HD * j + np.arange(HD), qa + HD * (j + 4) + np.arange(HD)]) for j in range(4)]
    return np.concatenate([half(qc, 0), half(qc, 1), half(kc, 0), half(kc, 1), run(vc, 256), run(gc, 256),
                           run(vb, 256), run(ub, 256), run(ka, 128), run(va, 128)] + pairs)


def pair_rows():
    return np.concatenate([np.concatenate([HD * j + np.arange(HD), HD * (j + 4) + np.arange(HD)]) for j in range(4)])


def slots_of(w):
    k, n = w.shape
    return w.reshape(k // P, P, n // P, P).transpose(2, 1, 0, 3)


def constants():
    f = np.float32
    half = HD // 2
    inv = (f(10000.0) ** (-np.arange(half, dtype=f) / f(half))).astype(f)
    pos = np.concatenate([np.arange(SEQ), PAST + np.arange(DEC)]).astype(f)
    ang = (pos[:, None] * inv[None, :]).astype(f).astype(np.float64)
    cos, sin = (np.tile(t(ang).astype(f).T, (RET_HEADS, 1)) for t in (np.cos, np.sin))
    logg = np.log(1.0 - 2.0 ** (-5.0 - np.arange(RET_HEADS)))
    i = np.arange(P)
    of_row = np.repeat(np.arange(RET_HEADS), 32)
    xi = np.exp(logg[of_row][:, None] * (i + 1.0)[None, :])
    rel = i[None, :] - i[:, None]
    decay = np.where(rel[:, None, :] >= 0, np.exp(logg[None, :, None] * np.maximum(rel, 0)[:, None, :]), 0.0)
    zeta = lambda block: np.tile(np.exp(logg[of_row][None, :] * (block - 1.0 - i)[:, None]), (1, 2))
    blk = np.kron(np.eye(2), np.ones((HD, HD))) / HD
    cdec = np.exp(logg[of_row][:, None] * np.array([P, DEC], float)[None, :])
    parts = [cos, sin, xi, of_row[:, None] == np.arange(RET_HEADS)[None, :], decay.reshape(P, -1), zeta(P),
             np.where(i[:, None] < DEC, zeta(DEC), 0.0), blk, cdec]
    return np.ascontiguousarray(np.concatenate([p.astype(f) for p in parts], axis=1))


def kernel(**inputs):
    import concourse.bacc as bacc
    from concourse.bass_utils import run_bass_kernel_spmd
    import ml_dtypes

    a = {k: np.asarray(v) for k, v in inputs.items()}
    f = np.float32
    to_tiles = lambda t: np.ascontiguousarray(t.reshape(t.shape[0], -1, P).transpose(2, 1, 0))
    xT = to_tiles(np.concatenate([a["x_prompt"][0], a["x_sample"][0]], axis=0))
    cols_in, rows_a = in_columns(), pair_rows()
    rows_out = np.concatenate([rows_a, np.arange(512, 1024)])
    wts = []
    for l in range(DEPTH):
        wts.append(slots_of(a["w_in"][l][:, cols_in]))
        wts.append(slots_of(a["w_out"][l][rows_out]))
        gu = np.stack([slots_of(a["w_gate"][l]), slots_of(a["w_up"][l])], axis=1)
        wts.append(gu.reshape((2 * FT,) + gu.shape[2:]))
        dn = slots_of(a["w_down"][l]).transpose(0, 2, 1, 3).reshape(-1, 8, P, P)
        wts.append(dn.transpose(0, 2, 1, 3))
    wts = np.ascontiguousarray(np.concatenate(wts, axis=0).reshape(DEPTH * SLOTS, P, 1024))

    col = lambda v: v.reshape(-1, P).T
    small = np.stack([np.concatenate([
        col(a["ln_pre_mix"][l]), col(a["ln_pre_mix"][(l + 1) % DEPTH]), col(a["ln_post_mix"][l]),
        col(a["ln_pre_ffn"][l]), col(a["ln_post_ffn"][l]),
        col(a["norm_a_g"][l][rows_a]), col(a["norm_b_g"][l]), col(a["ret_norm_g"][l]),
        np.broadcast_to(a["swa_sinks"][l].reshape(2, 4).T.reshape(1, 8), (P, 8))], axis=1) for l in range(DEPTH)])
    rows = lambda v: np.broadcast_to(v[None, :], (P, v.size))
    lpar = []
    for l in range(DEPTH):
        gb = np.repeat(a["gmlp_b"][l].reshape(2, 2, 1, P), HD, axis=2).transpose(1, 2, 0, 3).reshape(P, 2 * P)
        gw = np.ascontiguousarray(a["gmlp_w"][l].transpose(2, 0, 1))
        lpar.append(np.concatenate([rows(a["gmlp_ln_g"][l]), rows(a["gmlp_ln_b"][l]), gb, gw.reshape(P, 4 * P)],
                                   axis=1))
    lpar = np.stack(lpar)
    ck, cv = a["cache_swa_k"][0], a["cache_swa_v"][0]
    kcache = np.ascontiguousarray(ck.reshape(DEPTH, P, P).transpose(0, 2, 1))
    vcache = np.ascontiguousarray(cv.reshape(DEPTH, P, P))
    ret0 = np.ascontiguousarray(a["state_ret"][0].reshape(DEPTH, RET_HEADS, 2, 32, HD).transpose(0, 1, 3, 2, 4)
                                .reshape(DEPTH, P, 2, HD))
    q = np.arange(P) < CHUNK
    keys = np.arange(256)
    two = np.concatenate([np.stack([q, ~q]).astype(f), np.stack([keys >= 192, keys < 64]) * f(-1e30)], axis=1)
    mask = np.zeros((P, P + 256), ml_dtypes.bfloat16)
    mask[0:2] = two


    arrays = dict(xT=xT, wts=wts, small=small, tabs=constants(), lpar=lpar, kcache=kcache, vcache=vcache, ret0=ret0,
                  ident=np.eye(P, dtype=f), mask=mask)
    outs = dict(x=(P, KT, T), k=(DEPTH, P, P + DEC), v=(DEPTH, P, P + DEC), rp=(DEPTH, P, 2, HD),
                rs=(DEPTH, P, 2, HD), gv=(DEPTH, DEC, 256))
    nc = bacc.Bacc("TRN2", target_bir_lowering=False, num_devices=1)
    arrays = {f"in_{n}": np.ascontiguousarray(v) for n, v in arrays.items()}
    args = [nc.dram_tensor(n, v.shape, mybir.dt.from_np(v.dtype), kind="ExternalInput").ap() for n, v in arrays.items()]
    args += [nc.dram_tensor(f"out_{n}", s, F32, kind="ExternalOutput").ap() for n, s in outs.items()]
    program(nc, *args)
    r = run_bass_kernel_spmd(nc, [arrays], core_ids=[0]).results[0]

    y = r["out_x"].transpose(2, 1, 0).reshape(T, D)
    kv = []
    for n in ("k", "v"):
        t = r[f"out_{n}"].transpose(0, 2, 1).reshape(DEPTH, P + DEC, KV_HEADS, HD)[None]
        kv += [t[:, :, :P], t[:, :, P:]]
    st = [r[f"out_{n}"].reshape(DEPTH, RET_HEADS, 32, 2, HD).transpose(0, 1, 3, 2, 4)
          .reshape(1, DEPTH, RET_HEADS, HD, HD) for n in ("rp", "rs")]
    return tuple(np.ascontiguousarray(t) for t in
                 (y[None, :SEQ], y[None, SEQ:], kv[0], kv[2], kv[1], kv[3], st[0], st[1], r["out_gv"][None]))
```
